# Optimizing a Trainium2 kernel written in Bass

```python
import math
import jax, jax.numpy as jnp
from jax import lax
import numpy as np

D_MODEL = 1024
BATCH = 1
SEQ = 128
DEPTH = 2
DEC_BATCH = 1
DEC_SEQ = 256
PAST_LEN = 128

GRID_W = 64
EPS = 1e-6
ATT_HEADS = 8
ATT_KV_HEADS = 2
HEAD_DIM = 64
ATT_GROUP = ATT_HEADS // ATT_KV_HEADS
ATT_W = ATT_HEADS * HEAD_DIM
KV_W = ATT_KV_HEADS * HEAD_DIM
ATT_COLS = ATT_W + 2 * KV_W
WINDOW = 128
BLK = 128
ROPE_BASE = 10000.0
RW_HEADS = 4
RW_HD = 64
RW_W = RW_HEADS * RW_HD
RW_W_RANK = 32
RW_A_RANK = 32
RW_G_RANK = 64
RW_COLS = 3 * RW_W + RW_W_RANK + RW_A_RANK + RW_G_RANK
RW_DECAY_SCALE = 0.606531
RW_GN_EPS = 64e-5
SSD_HEADS = 4
SSD_HD = 64
SSD_W = SSD_HEADS * SSD_HD
SSD_GROUPS = 2
SSD_STATE = 64
SSD_CONV_K = 3
SSD_CONV_DIM = SSD_W + 2 * SSD_GROUPS * SSD_STATE
SSD_CHUNK = 128
SSD_COLS = SSD_W + SSD_CONV_DIM + SSD_HEADS
IN_COLS = ATT_COLS + RW_COLS + SSD_COLS
MIX_W = ATT_W + RW_W + SSD_W
N_EXPERTS = 16
N_GROUPS = 4
EXP_PER_GROUP = N_EXPERTS // N_GROUPS
TOP_K = 2
D_FF = 256
MOE_BLK = 128

kernel_name = 'hybrid_diffusion_prefix_trunk_step'

def split_cols(u, sizes):
    return jnp.split(u, [int(s) for s in np.cumsum(sizes)[:-1]], axis=-1)

def rmsnorm(x, w):
    xf = x.astype(jnp.float32)
    y = xf * lax.rsqrt(jnp.mean(xf * xf, -1, keepdims=True) + EPS)
    return (y * w.astype(jnp.float32)).astype(x.dtype)

def modulation(cond, w_mod, b_mod):
    m = (jax.nn.silu(cond) @ w_mod + b_mod)[..., None, :]
    return jnp.split(m, 6, axis=-1)

def rope_axis(x, cos, sin):
    x1, x2 = jnp.split(x, 2, -1)
    return jnp.concatenate([x1 * cos - x2 * sin, x2 * cos + x1 * sin], -1)

def apply_axial_rope(x):
    L = x.shape[1]
    t = jnp.arange(L)
    pos = jnp.stack([t // GRID_W, t % GRID_W], 0).astype(jnp.float32)
    n_freq = HEAD_DIM // 4
    inv = ROPE_BASE ** (-jnp.arange(n_freq, dtype=jnp.float32) / n_freq)
    ang = (pos[:, :, None] * inv).reshape((2, L) + (1,) * (x.ndim - 3) + (n_freq,))
    cos, sin = jnp.cos(ang).astype(x.dtype), jnp.sin(ang).astype(x.dtype)
    xr, xc = jnp.split(x, 2, -1)
    return jnp.concatenate([rope_axis(xr, cos[0], sin[0]), rope_axis(xc, cos[1], sin[1])], -1)

def attend(q, k, v, sink, mask):
    s = jnp.einsum('bqhgd,bjhd->bhgqj', q, k).astype(jnp.float32) * HEAD_DIM ** -0.5
    if mask is not None:
        s = jnp.where(mask, s, -1e30)
    sk = jnp.broadcast_to(sink.astype(jnp.float32)[None, :, :, None, None], s.shape[:-1] + (1,))
    p = jax.nn.softmax(jnp.concatenate([s, sk], -1), axis=-1)[..., :-1]
    return jnp.einsum('bhgqj,bjhd->bqhgd', p.astype(v.dtype), v)

def attn_context(q, k, v, sink):
    b, Lc = q.shape[:2]
    qb = jnp.moveaxis(q.reshape((b, Lc // BLK, BLK) + q.shape[2:]), 1, 0)
    out = lax.map(lambda qi: attend(qi, k, v, sink, None), qb)
    return jnp.moveaxis(out, 0, 1).reshape(q.shape)

def attn_latent(q, k, v, k_ctx, v_ctx, sink):
    b, L = q.shape[:2]
    nb = L // BLK
    pad = ((0, 0), (BLK, BLK), (0, 0), (0, 0))
    band = lambda t: jnp.concatenate([t[:, :-2], t[:, 1:-1], t[:, 2:]], axis=2)
    kb = jnp.moveaxis(band(jnp.pad(k, pad).reshape(b, nb + 2, BLK, ATT_KV_HEADS, HEAD_DIM)), 1, 0)
    vb = jnp.moveaxis(band(jnp.pad(v, pad).reshape(b, nb + 2, BLK, ATT_KV_HEADS, HEAD_DIM)), 1, 0)
    qb = jnp.moveaxis(q.reshape(b, nb, BLK, ATT_KV_HEADS, ATT_GROUP, HEAD_DIM), 1, 0)
    qpos = jnp.arange(nb)[:, None] * BLK + jnp.arange(BLK)[None]
    kpos = (jnp.arange(nb)[:, None] - 1) * BLK + jnp.arange(3 * BLK)[None]
    band_mask = ((jnp.abs(qpos[:, :, None] - kpos[:, None, :]) <= WINDOW)
                 & ((kpos >= 0) & (kpos < L))[:, None, :])
    mask = jnp.concatenate([band_mask, jnp.ones((nb, BLK, k_ctx.shape[1]), bool)], -1)

    def block(args):
        qi, ki, vi, mi = args
        return attend(qi, jnp.concatenate([ki, k_ctx], 1), jnp.concatenate([vi, v_ctx], 1), sink, mi)

    out = lax.map(block, (qb, kb, vb, mask))
    return jnp.moveaxis(out, 0, 1).reshape(q.shape)

def shift_mix(u, mu):
    prev = jnp.pad(u[:, :-1], ((0, 0), (1, 0), (0, 0)))
    nxt = jnp.pad(u[:, 1:], ((0, 0), (0, 1), (0, 0)))
    return u + mu[0] * (prev - u) + mu[1] * (nxt - u)

def rwkv_scan(r, w, k, v, kk, bb, s0, reverse):
    def step(S, xs):
        rt, wt, kt, vt, kkt, bt = xs
        sa = jnp.einsum('bhvk,bhk->bhv', S, kkt)
        S = S * wt[:, :, None, :] - sa[..., None] * bt[:, :, None, :] + vt[..., None] * kt[:, :, None, :]
        return S, jnp.einsum('bhvk,bhk->bhv', S, rt)
    xs = tuple(jnp.moveaxis(t, 1, 0) for t in (r, w, k, v, kk, bb))
    S, y = lax.scan(step, s0, xs, reverse=reverse)
    return jnp.moveaxis(y, 0, 1), S

def rwkv_mixer(u, s0, mu, w0, w_up, a0, a_up, g_up, k_k, k_a, r_k, ln_w, ln_b):
    b, L, _ = u.shape
    u = shift_mix(u, mu).astype(jnp.float32)
    r, k, v, wd, ad, gd = split_cols(u, [RW_W, RW_W, RW_W, RW_W_RANK, RW_A_RANK, RW_G_RANK])
    heads = lambda t: t.reshape(b, L, RW_HEADS, RW_HD)
    g = jax.nn.sigmoid(gd) @ g_up
    kk = heads(k * k_k)
    kk = kk * lax.rsqrt(jnp.sum(kk * kk, -1, keepdims=True) + 1e-12)
    s0 = s0.astype(jnp.float32)
    y = jnp.zeros((b, L, RW_HEADS, RW_HD), jnp.float32)
    states = []
    for d in range(2):
        w = jnp.exp(-RW_DECAY_SCALE * jax.nn.sigmoid(w0[d] + jnp.tanh(wd) @ w_up[d]))
        a = jax.nn.sigmoid(a0[d] + ad @ a_up[d])
        kd = k * (1 + (a - 1) * k_a)
        yd, sd = rwkv_scan(heads(r), heads(w), heads(kd), heads(v), kk, kk * heads(a), s0[:, d], d == 1)
        y = y + yd
        states.append(sd)
    mean = jnp.mean(y, -1, keepdims=True)
    var = jnp.mean(jnp.square(y - mean), -1, keepdims=True)
    y = ((y - mean) * lax.rsqrt(var + RW_GN_EPS)).reshape(b, L, RW_W) * ln_w + ln_b
    bonus = jnp.sum(heads(r) * heads(k) * r_k, -1, keepdims=True) * heads(v)
    y = (y + bonus.reshape(b, L, RW_W)) * g
    return y, jnp.stack(states, 1)

def centred_dwconv(x, w, bias):
    L = x.shape[1]
    p = SSD_CONV_K // 2
    xp = jnp.pad(x, ((0, 0), (p, p), (0, 0)))
    return sum(xp[:, i:i + L] * w[i] for i in range(SSD_CONV_K)) + bias

def ssd_chunked(x, dt, A, B, C, h0):
    b, L, H, P = x.shape
    nc = L // SSD_CHUNK
    ch = lambda t: t.reshape((b, nc, SSD_CHUNK) + t.shape[2:])
    xdt, Bc, Cc = ch(x * dt[..., None]), ch(B), ch(C)
    dA_cs = jnp.cumsum(ch(dt * A), axis=2)
    diff = dA_cs[:, :, :, None, :] - dA_cs[:, :, None, :, :]
    causal = jnp.tril(jnp.ones((SSD_CHUNK, SSD_CHUNK), bool))[None, None, :, :, None]
    Lmat = jnp.exp(jnp.where(causal, diff, -jnp.inf))
    y_diag = jnp.einsum('bcihn,bcjhn,bcijh,bcjhp->bcihp', Cc, Bc, Lmat, xdt)
    decay_in = jnp.exp(dA_cs[:, :, -1:] - dA_cs)
    chunk_states = jnp.einsum('bcjhn,bcjh,bcjhp->bchpn', Bc, decay_in, xdt)
    chunk_decay = jnp.exp(dA_cs[:, :, -1])

    def step(h, xs):
        st, dec = xs
        return h * dec[:, :, None, None] + st, h

    h_final, h_enter = lax.scan(step, h0, (jnp.moveaxis(chunk_states, 1, 0), jnp.moveaxis(chunk_decay, 1, 0)))
    h_enter = jnp.moveaxis(h_enter, 0, 1)
    y_off = jnp.einsum('bcihn,bchpn,bcih->bcihp', Cc, h_enter, jnp.exp(dA_cs))
    return (y_diag + y_off).reshape(b, L, H, P), h_final

def ssd_mixer(u, h0, conv_w, conv_b, dt_bias, a_log, d_skip, norm_w):
    b, L, _ = u.shape
    u = u.astype(jnp.float32)
    z, xbc, dt_raw = split_cols(u, [SSD_W, SSD_CONV_DIM, SSD_HEADS])
    xbc = jax.nn.silu(centred_dwconv(xbc, conv_w, conv_b))
    x, B, C = split_cols(xbc, [SSD_W, SSD_GROUPS * SSD_STATE, SSD_GROUPS * SSD_STATE])
    x = x.reshape(b, L, SSD_HEADS, SSD_HD)
    rep = SSD_HEADS // SSD_GROUPS
    B = jnp.repeat(B.reshape(b, L, SSD_GROUPS, SSD_STATE), rep, axis=2)
    C = jnp.repeat(C.reshape(b, L, SSD_GROUPS, SSD_STATE), rep, axis=2)
    h0 = h0.astype(jnp.float32)
    y = d_skip[:, None] * x
    states = []
    for d in range(2):
        flip = (lambda t: jnp.flip(t, 1)) if d == 1 else (lambda t: t)
        dt = jax.nn.softplus(dt_raw + dt_bias[d])
        A = -jnp.exp(a_log[d])
        yd, hd = ssd_chunked(flip(x), flip(dt), A, flip(B), flip(C), h0[:, d])
        y = y + flip(yd)
        states.append(hd)
    y = rmsnorm(y.reshape(b, L, SSD_W) * jax.nn.silu(z), norm_w)
    return y, jnp.stack(states, 1)

def moe(h, router_w, router_bias, w_gate, w_up, w_down):
    b, L, D = h.shape
    t = h.reshape(-1, MOE_BLK, D)

    def block(xb):
        scores = jax.nn.sigmoid((xb @ router_w).astype(jnp.float32))
        sel = scores + router_bias
        grp = lax.top_k(sel.reshape(-1, N_GROUPS, EXP_PER_GROUP), TOP_K)[0].sum(-1)
        g_idx = jnp.argmax(grp, -1)
        in_grp = (jnp.arange(N_EXPERTS) // EXP_PER_GROUP)[None] == g_idx[:, None]
        _, e_idx = lax.top_k(jnp.where(in_grp, sel, -jnp.inf), TOP_K)
        wts = jnp.take_along_axis(scores, e_idx, -1)
        wts = wts / jnp.sum(wts, -1, keepdims=True)
        combine = jnp.sum(jax.nn.one_hot(e_idx, N_EXPERTS, dtype=jnp.float32) * wts[..., None], 1)
        hid = jax.nn.silu(jnp.einsum('td,edf->tef', xb, w_gate)) * jnp.einsum('td,edf->tef', xb, w_up)
        return jnp.einsum('tef,te,efd->td', hid, combine.astype(hid.dtype), w_down)

    return lax.map(block, t).reshape(b, L, D)

def trunk(x, cond, is_ctx, cache_k, cache_v, state_rwkv, state_ssd, P):
    b, L, _ = x.shape
    new_k, new_v, new_rw, new_ssd = [], [], [], []
    for l in range(DEPTH):
        sh1, sc1, g1, sh2, sc2, g2 = modulation(cond, P['w_mod'][l], P['b_mod'][l])
        h = rmsnorm(x, P['norm1_w'][l]) * (1 + sc1) + sh1
        u_att, u_rw, u_ssd = split_cols(h @ P['w_in'][l], [ATT_COLS, RW_COLS, SSD_COLS])
        q, k, v = split_cols(u_att, [ATT_W, KV_W, KV_W])
        q = rmsnorm(q.reshape(b, L, ATT_KV_HEADS, ATT_GROUP, HEAD_DIM), P['q_norm_w'][l])
        k = rmsnorm(k.reshape(b, L, ATT_KV_HEADS, HEAD_DIM), P['k_norm_w'][l])
        v = v.reshape(b, L, ATT_KV_HEADS, HEAD_DIM)
        sink = P['attn_sink'][l].reshape(ATT_KV_HEADS, ATT_GROUP)
        if is_ctx:
            o_att = attn_context(q, k, v, sink)
            rw0 = jnp.zeros((b, 2, RW_HEADS, RW_HD, RW_HD), jnp.float32)
            ssd0 = jnp.zeros((b, 2, SSD_HEADS, SSD_HD, SSD_STATE), jnp.float32)
        else:
            q, k = apply_axial_rope(q), apply_axial_rope(k)
            o_att = attn_latent(q, k, v, cache_k[:, l], cache_v[:, l], sink)
            rw0, ssd0 = state_rwkv[:, l], state_ssd[:, l]
        o_rw, s_rw = rwkv_mixer(u_rw, rw0, P['rw_mu'][l], P['rw_w0'][l], P['rw_w_up'][l], P['rw_a0'][l],
                                P['rw_a_up'][l], P['rw_g_up'][l], P['rw_k_k'][l], P['rw_k_a'][l],
                                P['rw_r_k'][l], P['rw_ln_w'][l], P['rw_ln_b'][l])
        o_ssd, s_ssd = ssd_mixer(u_ssd, ssd0, P['ssd_conv_w'][l], P['ssd_conv_b'][l], P['ssd_dt_bias'][l],
                                 P['ssd_a_log'][l], P['ssd_d'][l], P['ssd_norm_w'][l])
        if is_ctx:
            new_k.append(k)
            new_v.append(v)
            new_rw.append(s_rw.astype(x.dtype))
            new_ssd.append(s_ssd.astype(x.dtype))
        o = jnp.concatenate([o_att.reshape(b, L, ATT_W), o_rw.astype(x.dtype), o_ssd.astype(x.dtype)], -1)
        x = x + g1 * (o @ P['w_out'][l])
        h = rmsnorm(x, P['norm2_w'][l]) * (1 + sc2) + sh2
        x = x + g2 * moe(h, P['router_w'], P['router_bias'], P['exp_gate'][l], P['exp_up'][l], P['exp_down'][l])
    if is_ctx:
        return x, (jnp.stack(new_k, 1), jnp.stack(new_v, 1), jnp.stack(new_rw, 1), jnp.stack(new_ssd, 1))
    return x, None

def setup_inputs(seed: int = 0) -> dict:
    key = jax.random.key(seed)
    keys = jax.random.split(key, 64)
    ks = (keys[i] for i in range(64))
    nrm = lambda shape, scale: jax.random.normal(next(ks), shape, jnp.float32) * scale
    uni = lambda shape, lo, hi: jax.random.uniform(next(ks), shape, jnp.float32, minval=lo, maxval=hi)
    L = DEPTH
    D = D_MODEL
    dt0 = jnp.exp(uni((L, 2, SSD_HEADS), math.log(1e-3), math.log(1e-1)))
    return {
        'x_prompt': nrm((BATCH, SEQ, D), 1.0),
        'x_sample': nrm((DEC_BATCH, DEC_SEQ, D), 1.0),
        'cache_k': nrm((DEC_BATCH, DEPTH, PAST_LEN, ATT_KV_HEADS, HEAD_DIM), 1.0),
        'cache_v': nrm((DEC_BATCH, DEPTH, PAST_LEN, ATT_KV_HEADS, HEAD_DIM), 1.0),
        'state_rwkv': nrm((DEC_BATCH, DEPTH, 2, RW_HEADS, RW_HD, RW_HD), 0.5),
        'state_ssd': nrm((DEC_BATCH, DEPTH, 2, SSD_HEADS, SSD_HD, SSD_STATE), 0.3),
        'c': nrm((DEC_BATCH, D), 1.0),
        'c_ctx': nrm((D,), 1.0),
        'w_mod': nrm((L, D, 6 * D), 0.5 * D ** -0.5),
        'b_mod': nrm((L, 6 * D), 0.02),
        'norm1_w': 1.0 + nrm((L, D), 0.05),
        'norm2_w': 1.0 + nrm((L, D), 0.05),
        'w_in': nrm((L, D, IN_COLS), D ** -0.5),
        'w_out': nrm((L, MIX_W, D), MIX_W ** -0.5),
        'q_norm_w': 1.0 + nrm((L, HEAD_DIM), 0.05),
        'k_norm_w': 1.0 + nrm((L, HEAD_DIM), 0.05),
        'attn_sink': nrm((L, ATT_HEADS), 0.5),
        'rw_mu': uni((L, 2, RW_COLS), 0.0, 0.5),
        'rw_w0': nrm((L, 2, RW_W), 0.5),
        'rw_w_up': nrm((L, 2, RW_W_RANK, RW_W), 0.1),
        'rw_a0': nrm((L, 2, RW_W), 0.1),
        'rw_a_up': nrm((L, 2, RW_A_RANK, RW_W), 0.1),
        'rw_g_up': nrm((L, RW_G_RANK, RW_W), RW_G_RANK ** -0.5),
        'rw_k_k': 0.85 + nrm((L, RW_W), 0.05),
        'rw_k_a': 1.0 + nrm((L, RW_W), 0.05),
        'rw_r_k': nrm((L, RW_HEADS, RW_HD), 0.1),
        'rw_ln_w': 1.0 + nrm((L, RW_W), 0.05),
        'rw_ln_b': nrm((L, RW_W), 0.02),
        'ssd_conv_w': nrm((L, SSD_CONV_K, SSD_CONV_DIM), SSD_CONV_K ** -0.5),
        'ssd_conv_b': nrm((L, SSD_CONV_DIM), 0.02),
        'ssd_dt_bias': dt0 + jnp.log(-jnp.expm1(-dt0)),
        'ssd_a_log': jnp.log(uni((L, 2, SSD_HEADS), 1.0, 16.0)),
        'ssd_d': 1.0 + nrm((L, SSD_HEADS), 0.1),
        'ssd_norm_w': 1.0 + nrm((L, SSD_W), 0.05),
        'router_w': nrm((D, N_EXPERTS), D ** -0.5),
        'router_bias': nrm((N_EXPERTS,), 0.01),
        'exp_gate': nrm((L, N_EXPERTS, D, D_FF), D ** -0.5),
        'exp_up': nrm((L, N_EXPERTS, D, D_FF), D ** -0.5),
        'exp_down': nrm((L, N_EXPERTS, D_FF, D), D_FF ** -0.5),
    }

def reference(x_prompt, x_sample, cache_k, cache_v, state_rwkv, state_ssd, c, c_ctx,
              w_mod, b_mod, norm1_w, norm2_w, w_in, w_out, q_norm_w, k_norm_w, attn_sink,
              rw_mu, rw_w0, rw_w_up, rw_a0, rw_a_up, rw_g_up, rw_k_k, rw_k_a, rw_r_k, rw_ln_w, rw_ln_b,
              ssd_conv_w, ssd_conv_b, ssd_dt_bias, ssd_a_log, ssd_d, ssd_norm_w,
              router_w, router_bias, exp_gate, exp_up, exp_down):
    P = {
        'w_mod': w_mod, 'b_mod': b_mod, 'norm1_w': norm1_w, 'norm2_w': norm2_w,
        'w_in': w_in, 'w_out': w_out, 'q_norm_w': q_norm_w, 'k_norm_w': k_norm_w, 'attn_sink': attn_sink,
        'rw_mu': rw_mu, 'rw_w0': rw_w0, 'rw_w_up': rw_w_up, 'rw_a0': rw_a0, 'rw_a_up': rw_a_up,
        'rw_g_up': rw_g_up, 'rw_k_k': rw_k_k, 'rw_k_a': rw_k_a, 'rw_r_k': rw_r_k,
        'rw_ln_w': rw_ln_w, 'rw_ln_b': rw_ln_b,
        'ssd_conv_w': ssd_conv_w, 'ssd_conv_b': ssd_conv_b, 'ssd_dt_bias': ssd_dt_bias,
        'ssd_a_log': ssd_a_log, 'ssd_d': ssd_d, 'ssd_norm_w': ssd_norm_w,
        'router_w': router_w, 'router_bias': router_bias,
        'exp_gate': exp_gate, 'exp_up': exp_up, 'exp_down': exp_down,
    }
    y_prompt, ctx_state = trunk(x_prompt, c_ctx, True, None, None, None, None, P)
    new_cache_k, new_cache_v, new_state_rwkv, new_state_ssd = ctx_state
    y_sample, _ = trunk(x_sample, c, False, cache_k, cache_v, state_rwkv, state_ssd, P)
    return (y_prompt, y_sample, new_cache_k, new_cache_v, new_state_rwkv, new_state_ssd)


_drawn_inputs = setup_inputs


def setup_inputs(seed=0):
    import zlib

    import numpy as np

    out = dict(_drawn_inputs(seed))
    spreads = {}
    factors = {'state_rwkv': 2.934,
     'q_norm_w': 8.0,
     'attn_sink': 64.0,
     'rw_ln_w': 3.334,
     'rw_ln_b': 3.954,
     'ssd_d': 2.725}
    for name, (base, spread) in spreads.items():
        noise = np.random.default_rng([zlib.crc32(name.encode()), seed]).standard_normal(out[name].shape)
        drawn = base * np.exp(spread * noise) if base else spread * noise
        out[name] = __import__('jax').numpy.asarray(drawn.astype(out[name].dtype))
    for name, factor in factors.items():
        out[name] = (out[name] * factor).astype(out[name].dtype)
    return out
```

```python
import concourse.bass as bass
from concourse import mybir
from contextlib import ExitStack

DEPTH = 2
P = 128
D = 1024
KT = D // P
TILES = 3
COL = [0, P + 1, 2 * P + 1]
W = 3 * P + 1
LAT = COL[1]
SEGMENTS = [(0, 0, P), (1, LAT, W)]
EPS = 1e-6
GN_EPS = 64e-5
DECAY = 0.606531
NEG = -1e30

UQ, UK, UV, UR, URK, URV, ULORA, UZ, UX, UB, UC, UDT = 0, 4, 5, 6, 8, 10, 12, 13, 15, 17, 18, 19
U_TILES = 20
DT_ROWS = 64
EXPERTS = 16
GROUPS = 4
EXPERT_ITEMS = 3
ITEM = 2048
MOD_ITEMS, IN_ITEMS, OUT_ITEMS = 24, 10, 4
LAYER_ITEMS = MOD_ITEMS + IN_ITEMS + OUT_ITEMS + EXPERTS * EXPERT_ITEMS
SLOTS = 5

RW_BATCHES = [(0, 0), (0, 1), (1, 0), (2, 1), (2, 0), (1, 1)]
STATE_BATCHES = 4
SSD_STATES = [(0, 0), (0, 1), (1, 0), (2, 1)]


def columns(names):
    at, out = 0, {}
    for name, n in names:
        out[name] = (at, at + n)
        at += n
    return out, at


LAYER_COLS, LAYER_N = columns([
    ("n1", 8), ("n2", 8), ("bmod", 48), ("qw", 1), ("kw", 1), ("sink", 8), ("mu0", 7), ("mu1", 7),
    ("w0", 4), ("a0", 4), ("kk", 2), ("ka", 2), ("rk", 2), ("lnw", 2), ("lnb", 2), ("cw", 12), ("cb", 4),
    ("dtb", 1), ("alog", 1), ("dskip", 2), ("nw", 2), ("lora", 512), ("kc", 128), ("vc", 128),
    ("srw", 256), ("sssd", 256)])
CONST_COLS, CONST_N = columns([
    ("mean1024", 128), ("mean64", 128), ("sum64", 128), ("mean256", 128), ("ident", 128), ("rot", 128),
    ("inv", 512), ("rw0", 512), ("rw1", 512), ("nd0", 128), ("nd1", 128), ("att", 512), ("ssd0", 128),
    ("ssd1", 128), ("cos", 256), ("sin", 256), ("restart", W), ("rank16", 16), ("rank4", 4),
    ("router", 128), ("rbias", 16), ("eps", 1), ("eps_kk", 1), ("eps_gn", 1)])


def psum_plan():
    plan = []

    def g(consumer, *key):
        plan.append((key, consumer))

    for l in range(DEPTH):
        for i in range(MOD_ITEMS):
            g("v", "mod", l, i)
        g("a", "ms", l, 1)
        for c in range(U_TILES):
            g("va"[c % 2], "u", l, c)
        for i in range(5):
            g("a", "qkms", l, i)
        g("a", "vt", l)
        for i in range(5):
            g("v", "rope", l, i)
        for t in range(TILES):
            for h in range(8):
                g("v", "sc", l, t, h)
            for h in range(8):
                g("a", "pT", l, t, h)
            g("a", "pv", l, t)
        for d in range(2):
            for i in range(2):
                g("a", "wl", l, d, i)
        for d in range(2):
            for i in range(2):
                g("a", "al", l, d, i)
        for i in range(2):
            g("a", "gg", l, i)
        for i in range(2):
            g("a", "kkn", l, i)
        for i in range(2):
            g("v", "bon", l, i)
        for i in range(2):
            g("a", "rvt", l, i)
        for b in range(len(RW_BATCHES)):
            for j in range(4):
                g("v", "g4", l, b, j)
            for half in range(2):
                g("v", "nd", l, b, half)
            for k in range(1, 5):
                if k < 4:
                    g("a", "p", l, b, k)
                    g("a", "pt", l, b, k)
                if k > 1:
                    g("v", "t", l, b, k)
                    g("v", "tt", l, b, k)
            for m in range(3):
                g("a", "m", l, b, m)
                if m < 2:
                    g("v", "t", l, b, 5 + m)
                g("v", "tt", l, b, 5 + m)
            g("a", "rhs", l, b)
            g("v", "x", l, b)
            g("v", "y", l, b)
            if b < STATE_BATCHES:
                g("a", "kbt", l, b)
                g("v", "st", l, b)
        for i in range(2):
            g("v", "gnm", l, i)
        for i in range(2):
            g("a", "gnv", l, i)
        g("a", "dtt", l)
        for r in range(8):
            g("a", "cs", l, r)
        for t in range(TILES):
            g("a", "xt", l, t)
            for grp in range(2):
                g("v", "gt", l, t, grp)
        for s in range(4):
            g("v", "hst", l, s)
        for t in range(TILES):
            for grp in range(2):
                g("v", "ys", l, t, grp)
        g("a", "yms", l)
        for n in range(KT):
            g("v", "out", l, n)
        g("a", "ms", l, 2)
        g("a", "lg", l)
        g("a", "ct", l)
        for e in range(EXPERTS):
            g("v", "cb", l, e)
            for f in range(2):
                g("a", "gate", l, e, f)
                g("v", "up", l, e, f)
            for n in range(KT):
                g("v", "down", l, e, n)
    return plan


def last_groups():
    out = []
    for l in range(DEPTH):
        out += [("mod", l, i) for i in range(MOD_ITEMS)]
        out += [("u", l, 2 * i + 1) for i in range(IN_ITEMS)]
        out += [("out", l, 2 * i + 1) for i in range(OUT_ITEMS)]
        for e in range(EXPERTS):
            out += [("gate", l, e, 1), ("up", l, e, 1), ("down", l, e, KT - 1)]
    return out


LAST_GROUP = last_groups()


def program(nc, a):
    fp32 = mybir.dt.float32
    ALU = mybir.AluOpType
    ACT = mybir.ActivationFunctionType
    X = mybir.AxisListType.X

    ctx = ExitStack()
    with ctx:
        def sb(name, n):
            return ctx.enter_context(nc.sbuf_tensor("sb_" + name, [P, n], fp32))

        def sem(name):
            return ctx.enter_context(nc.semaphore(name))

        def shaped(ap, *dims):
            names = [f"d{i}" for i in range(len(dims))]
            sizes = {k: v for k, v in zip(names[1:], dims[1:])}
            return ap.rearrange(f"p ({' '.join(names)}) -> p {' '.join(names)}", **sizes)

        ring = sb("ring", SLOTS * ITEM)
        xT = shaped(sb("xT", KT * W)[:, :], KT, W)
        hT_flat = sb("hT", KT * W)[:, :]
        hT = shaped(hT_flat, KT, W)
        u_flat = sb("u", U_TILES * (W + 2))[:, :]
        u = shaped(u_flat, U_TILES, W + 2)
        sq_flat = sb("sq", KT * W)[:, :]
        sq = shaped(sq_flat, KT, W)
        o = shaped(sb("o", KT * W)[:, :], KT, W)
        small = sb("small", LAYER_N)
        consts = sb("consts", CONST_N)
        cond = sb("cond", 16)
        scond = sb("scond", 16)
        mod = shaped(sb("mod", 96)[:, :], 48, 2)
        scale1 = shaped(sb("scale1", 16)[:, :], 8, 2)
        scale2 = shaped(sb("scale2", 16)[:, :], 8, 2)
        tmp = sb("tmp", 2 * W)
        cols = sb("cols", 256)
        AREN = 13776
        arena = sb("arena", AREN)
        state_rw = [shaped(sb(f"state_rw{l}", 256)[:, :], 4, 64) for l in range(DEPTH)]
        state_ssd = [shaped(sb(f"state_ssd{l}", 256)[:, :], 4, 64) for l in range(DEPTH)]
        new_k = [sb(f"new_k{l}", P) for l in range(DEPTH)]
        new_v = [sb(f"new_v{l}", P) for l in range(DEPTH)]

        banks = [ctx.enter_context(nc.psum_tensor(f"bank{i}", [P, 512], fp32)) for i in range(8)]

        def carve(base, *dims):
            n = 1
            for x in dims:
                n *= x
            assert base[1] + n <= base[2], (base, dims)
            ap = base[0][:, base[1]:base[1] + n]
            base[1] += n
            return shaped(ap, *dims) if len(dims) > 1 else ap

        at = [arena, 0, AREN]
        qn = carve(at, 5, W)
        scores = [carve(at, 8, 3 * P) for _ in range(2)]
        probsT = carve(at, 8, 3 * P)
        v_tm = carve(at, TILES, P)
        att_cols = carve(at, 64)
        rw = [arena, 0, AREN]
        mixed = carve(rw, 7, W)
        kdir = carve(rw, 2, W)
        gate_rw = carve(rw, 2, W)
        bonus = carve(rw, 2, W)
        y_rw = carve(rw, 2, W)
        rv_tm = carve(rw, 2, TILES, P)
        S_til = carve(rw, 4, 64)
        S_diag = carve(rw, 4, 2, 64)
        S_lat = carve(rw, 4, 64)
        decay_half = carve(rw, 4, TILES)
        half_total = carve(rw, 4, TILES)
        r_rhs = carve(rw, 4, 64)
        x_sol = carve(rw, 4, 64)
        kb_tm = carve(rw, 4, P)
        merged = carve(rw, 4, P)
        reuse = rw[1]
        sgw = carve(rw, 4, W)
        asig = carve(rw, 4, W)
        csum = carve(rw, 4, W)
        rw2 = [arena, reuse, AREN]
        g4 = carve(rw2, 4, 4, P)
        nT4 = carve(rw2, 4, 4, P)
        ar = shaped(hT_flat, 2, 2, 2, W)
        kb = shaped(sq_flat, 2, 2, 2, W)
        tail = [u_flat, 0, 13 * (W + 2)]
        pw = [carve(tail, 4, P) for _ in range(2)]
        pwT = [carve(tail, 4, P) for _ in range(2)]
        inv = [carve(tail, 4, P) for _ in range(2)]
        invT = [carve(tail, 4, P) for _ in range(2)]
        nd = carve(tail, 4, P)
        ss = [arena, 0, AREN]
        le = carve(ss, 8, W)
        ce = carve(ss, 8, 2 * P)
        x_tm = carve(ss, TILES, 3 * P)
        xdt = carve(ss, TILES, 2, 4, 64)
        xdd = carve(ss, 4, 4, 64)
        dtc = carve(ss, TILES, 2, DT_ROWS)
        total_b = carve(ss, 8, TILES)
        decay_in = carve(ss, TILES, 8)
        chunk_decay = carve(ss, 8, TILES)
        dt_t = carve(ss, W)
        dta = carve(ss, W)
        cs = carve(ss, W)
        dtmp = carve(ss, W)
        y_ssd = carve(ss, 2, W)
        neg_a = carve(ss, 4)
        h_mid = carve(ss, 4, 64)
        mo = [arena, 0, AREN]
        rt = carve(mo, 24, 48)
        comb_T = carve(mo, W)
        sg = carve(mo, 2, W)
        hid = [carve(mo, 2, W) for _ in range(2)]
        moe_out = o

        def C(name, rows=slice(0, P)):
            lo, hi = CONST_COLS[name]
            return consts[rows, lo:hi]

        def Lp(name, rows=slice(0, P)):
            lo, hi = LAYER_COLS[name]
            return small[rows, lo:hi]

        def Lc(name, i, rows=slice(0, P)):
            lo = LAYER_COLS[name][0]
            return small[rows, lo + i:lo + i + 1]

        def bc(ap, dim, n):
            ap = ap.unsqueeze(dim)
            shape = list(ap.shape)
            shape[dim] = n
            return ap.broadcast_to(shape)

        plan = psum_plan()
        index = {key: n for n, (key, _) in enumerate(plan)}
        read_no = {}
        count = {"a": 0, "v": 0}
        for key, consumer in plan:
            count[consumer] += 1
            read_no[key] = count[consumer]
        psum_filled = sem("psum_filled")
        psum_read = {"a": sem("psum_read_by_scalar"), "v": sem("psum_read_by_vector")}
        opened = [0]
        released = {"a": 0, "v": 0}

        def open_bank(pe, *key):
            n = index[key]
            assert n == opened[0], (key, plan[opened[0]])
            opened[0] += 1
            if n >= 8:
                old, consumer = plan[n - 8]
                pe.wait_ge(psum_read[consumer], read_no[old])
            return banks[n % 8]

        def filled(eng, *key):
            eng.wait_ge(psum_filled, index[key] + 1)
            return banks[index[key] % 8]

        def read(*key):
            consumer = plan[index[key]][1]
            released[consumer] += 1
            assert read_no[key] == released[consumer], key
            return psum_read[consumer]

        def taken(eng, *key):
            eng.wait_ge(psum_read[plan[index[key]][1]], read_no[key])

        item_ready = [sem(f"weights_ready{i}") for i in range(SLOTS)]
        consts_loaded = sem("consts_loaded")
        small_loaded = sem("small_loaded")
        out_written = sem("out_written")
        gaps_cleared = sem("gaps_cleared")
        cond_ready = sem("cond_ready")
        xsq_ready = sem("xsq_ready")
        h_ready = sem("h_ready")
        qk_sq_ready = sem("qk_sq_ready")
        qn_ready = sem("qn_ready")
        rope_ready = sem("rope_ready")
        shifted_ready = sem("shifted_ready")
        exps_ready = sem("exps_ready")
        probs_ready = sem("probs_ready")
        kv_copied = sem("kv_copied")
        mixed_ready = sem("mixed_ready")
        lora_ready = sem("lora_ready")
        kk_sq_ready = sem("kk_sq_ready")
        bonus_in_ready = sem("bonus_in_ready")
        decay_arg_ready = sem("decay_arg_ready")
        decay_exp_ready = sem("decay_exp_ready")
        factors_ready = sem("factors_ready")
        state_ready = sem("state_ready")
        matrices_ready = sem("matrices_ready")
        gn_in_ready = sem("gn_in_ready")
        gn_sq_ready = sem("gn_sq_ready")
        rwkv_done = sem("rwkv_done")
        conv_ready = sem("conv_ready")
        silu_ready = sem("silu_ready")
        dt_parts = sem("dt_parts")
        dt_ready = sem("dt_ready")
        cs_ready = sem("cs_ready")
        lat_decay_ready = sem("lat_decay_ready")
        le_arg_ready = sem("le_arg_ready")
        din_arg_ready = sem("din_arg_ready")
        le_ready = sem("le_ready")
        din_ready = sem("din_ready")
        xdd_ready = sem("xdd_ready")
        gated_sq_ready = sem("gated_sq_ready")
        z_ready = sem("z_ready")
        mix_ready = sem("mix_ready")
        x_ready = sem("x_ready")
        comb_ready = sem("comb_ready")
        chain_v = sem("vector_chain")
        chain_a = sem("scalar_chain")

        block = ctx.enter_context(nc.Block())

        @block.sync
        def _(sp):
            sp.dma_start(consts[:, :], a["consts"][:, :]).then_inc(consts_loaded, 16)
            sp.dma_start(cond[:, :], a["cond"][:, :]).then_inc(consts_loaded, 16)
            sp.dma_start(small[:, :], a["small"][0]).then_inc(small_loaded, 16)
            for n in range(DEPTH * LAYER_ITEMS):
                if n >= SLOTS:
                    filled(sp, *LAST_GROUP[n - SLOTS])
                s = n % SLOTS
                if n == 4:
                    sp.dma_start(xT, shaped(a["x"][:, :], KT, W)).then_inc(consts_loaded, 16)
                sp.dma_start(ring[:, s * ITEM:(s + 1) * ITEM], a["weights"][n]).then_inc(item_ready[s], 16)
                if n == LAYER_ITEMS - 20:
                    sp.wait_ge(mix_ready, 1)
                    sp.dma_start(small[:, :], a["small"][1]).then_inc(small_loaded, 16)

        @block.gpsimd
        def _(pool):
            for l in range(DEPTH):
                pool.wait_ge(kv_copied, 2 * (l + 1))
                pool.dma_start(a["new_k"][l], new_k[l][:, :]).then_inc(out_written, 16)
                pool.dma_start(a["new_v"][l], new_v[l][:, :]).then_inc(out_written, 16)
                taken(pool, "st", l, 1)
                pool.dma_start(shaped(a["new_rw"][l], 4, 64), state_rw[l]).then_inc(out_written, 16)
                taken(pool, "hst", l, 1)
                pool.dma_start(shaped(a["new_ssd"][l], 4, 64), state_ssd[l]).then_inc(out_written, 16)
            pool.wait_ge(x_ready, DEPTH)
            pool.dma_start(shaped(a["y"][:, :], KT, W), xT).then_inc(out_written, 16)
            pool.wait_ge(out_written, 16 * (4 * DEPTH + 1))

        @block.tensor
        def _(pe):
            items = [0]

            def next_item():
                n = items[0]
                pe.wait_ge(item_ready[n % SLOTS], 16 * (n // SLOTS + 1))
                items[0] += 1
                return ring[:, (n % SLOTS) * ITEM:(n % SLOTS + 1) * ITEM]

            def mm(out, lhsT, rhs, start=True, stop=True):
                return nc.tensor.matmul(out, lhsT, rhs, start=start, stop=stop, skip_group_check=True)

            def tr(out, in_, n=P):
                return nc.tensor.transpose(out, in_, C("ident")[0:n, 0:n])

            def mean_square(l, which):
                bank = open_bank(pe, "ms", l, which)
                pe.wait_ge(xsq_ready, 2 * l + which)
                for k in range(KT):
                    last = mm(bank[:, 0:W], C("mean1024"), sq[:, k, :], k == 0, k == KT - 1)
                last.then_inc(psum_filled, 1)

            def project(item, off, src, kts, out, m=P):
                for k in range(kts):
                    last = mm(out, item[:, off + k * m:off + (k + 1) * m], src[:, k, :], k == 0, k == kts - 1)
                return last

            def modulation(l):
                if l == 0:
                    pe.wait_ge(cond_ready, 1)
                cv = shaped(scond[:, :], KT, 2)
                for i in range(MOD_ITEMS):
                    item = next_item()
                    bank = open_bank(pe, "mod", l, i)
                    for c in range(2):
                        last = project(item, c * KT * P, cv, KT, bank[:, 2 * c:2 * c + 2])
                    last.then_inc(psum_filled, 1)

            def in_projection(l):
                pe.wait_ge(h_ready, 4 * l + 2)
                for c in range(U_TILES):
                    if c % 2 == 0:
                        item = next_item()
                    bank = open_bank(pe, "u", l, c)
                    m = DT_ROWS if c == UDT else P
                    project(item, (c % 2) * KT * P, hT, KT, bank[0:m, 0:W], m).then_inc(psum_filled, 1)

            def attention(l):
                for i in range(5):
                    bank = open_bank(pe, "qkms", l, i)
                    pe.wait_ge(qk_sq_ready, l + 1)
                    mm(bank[:, 0:W], C("mean64"), sq[:, i, :]).then_inc(psum_filled, 1)
                bank = open_bank(pe, "vt", l)
                taken(pe, "u", l, UV)
                for t in range(TILES):
                    last = tr(bank[:, t * P:(t + 1) * P], u[:, UV, 1 + COL[t]:1 + COL[t] + P])
                last.then_inc(psum_filled, 1)
                for i in range(5):
                    bank = open_bank(pe, "rope", l, i)
                    pe.wait_ge(qn_ready, 5 * l + i + 1)
                    mm(bank[:, 0:2 * P], C("rot"), qn[:, i, LAT:W]).then_inc(psum_filled, 1)
                for t in range(TILES):
                    c0 = COL[t]
                    for h in range(8):
                        m, p = h % 4, 64 * (h // 4)
                        bank = open_bank(pe, "sc", l, t, h)
                        if t == 0 and h == 0:
                            pe.wait_ge(rope_ready, l + 1)
                        q = qn[p:p + 64, m, c0:c0 + P]
                        if t == 0:
                            last = mm(bank[:, 0:P], q, qn[p:p + 64, 4, 0:P])
                        else:
                            mm(bank[:, 0:2 * P], q, qn[p:p + 64, 4, LAT:W])
                            last = mm(bank[:, 2 * P:3 * P], q, Lp("kc", slice(p, p + 64)))
                        last.then_inc(psum_filled, 1)
                    blocks = 1 if t == 0 else 3
                    for h in range(8):
                        bank = open_bank(pe, "pT", l, t, h)
                        if h == 0:
                            pe.wait_ge(probs_ready, TILES * l + t + 1)
                        for b in range(blocks):
                            last = tr(bank[:, b * P:(b + 1) * P], scores[t % 2][:, h, b * P:(b + 1) * P])
                        last.then_inc(psum_filled, 1)
                    bank = open_bank(pe, "pv", l, t)
                    taken(pe, "pT", l, t, 7)
                    for h in range(8):
                        m, p = h % 4, 64 * (h // 4)
                        for b in range(blocks):
                            if t == 0:
                                v = v_tm[:, 0, p:p + 64]
                            elif b < 2:
                                v = v_tm[:, 1 + b, p:p + 64]
                            else:
                                v = Lp("vc")[:, p:p + 64]
                            last = mm(bank[p:p + 64, m * P:(m + 1) * P], v, probsT[:, h, b * P:(b + 1) * P],
                                      b == 0, b == blocks - 1)
                    last.then_inc(psum_filled, 1)

            def rwkv_inputs(l):
                for name, r0, r1 in (("wl", 0, 32), ("al", 32, 64)):
                    for d in range(2):
                        for i in range(2):
                            bank = open_bank(pe, name, l, d, i)
                            pe.wait_ge(lora_ready, l + 1)
                            c = d * 256 + i * P
                            mm(bank[:, 0:W], Lp("lora", slice(r0, r1))[:, c:c + P], mixed[r0:r1, 6, :])\
                                .then_inc(psum_filled, 1)
                for i in range(2):
                    bank = open_bank(pe, "gg", l, i)
                    mm(bank[:, 0:W], Lp("lora", slice(64, P))[:, i * P:(i + 1) * P], mixed[64:P, 6, :])\
                        .then_inc(psum_filled, 1)
                for i in range(2):
                    bank = open_bank(pe, "kkn", l, i)
                    pe.wait_ge(kk_sq_ready, l + 1)
                    mm(bank[:, 0:W], C("sum64"), sq[:, i, :]).then_inc(psum_filled, 1)
                for i in range(2):
                    bank = open_bank(pe, "bon", l, i)
                    pe.wait_ge(bonus_in_ready, l + 1)
                    mm(bank[:, 0:W], C("sum64"), sq[:, 2 + i, :]).then_inc(psum_filled, 1)
                for i in range(2):
                    bank = open_bank(pe, "rvt", l, i)
                    for t in range(TILES):
                        last = tr(bank[:, t * P:(t + 1) * P], mixed[:, 4 + i, COL[t]:COL[t] + P])
                    last.then_inc(psum_filled, 1)

            def four(bank, lhsT, rhs):
                for j in range(4):
                    last = mm(bank[:, j * P:(j + 1) * P], lhsT[:, j, :], rhs[:, j, :])
                last.then_inc(psum_filled, 1)

            def rwkv_batch(l, b):
                t, d = RW_BATCHES[b]
                c0, c1 = COL[t], COL[t] + P
                if b == 0:
                    pe.wait_ge(factors_ready, l + 1)
                for j in range(4):
                    i, p = j // 2, 64 * (j % 2)
                    bank = open_bank(pe, "g4", l, b, j)
                    both = ar[p:p + 64, d, i, :, c0:c1]
                    mm(bank[:, 0:2 * P], kb[p:p + 64, 0, d, i, c0:c1], both)
                    mm(bank[:, 2 * P:4 * P], kb[p:p + 64, 1, d, i, c0:c1], both).then_inc(psum_filled, 1)
                for half in range(2):
                    bank = open_bank(pe, "nd", l, b, half)
                    p = 64 * half
                    for i in range(2):
                        last = mm(bank[:, i * P:(i + 1) * P], ar[p:p + 64, d, i, 0, c0:c1],
                                  kb[p:p + 64, 1, d, i, c0:c1])
                    last.then_inc(psum_filled, 1)
                pe.wait_ge(matrices_ready, len(RW_BATCHES) * l + b + 1)
                n1, n1T = nd, nT4[:, :, 0, :]
                for k in range(1, 5):
                    if k > 1:
                        taken(pe, "pt", l, b, k - 1)
                        n1, n1T = pw[(k - 1) % 2], pwT[(k - 1) % 2]
                    if k < 4:
                        four(open_bank(pe, "p", l, b, k), n1T, n1)
                        four(open_bank(pe, "pt", l, b, k), n1, n1T)
                    if k > 1:
                        if k > 2:
                            taken(pe, "tt", l, b, k - 1)
                        s = k % 2
                        four(open_bank(pe, "t", l, b, k), n1T, inv[s])
                        four(open_bank(pe, "tt", l, b, k), inv[s], n1T)
                for m in range(3):
                    s = (5 + m) % 2
                    bank = open_bank(pe, "m", l, b, m)
                    taken(pe, "tt", l, b, 4 + m)
                    four(bank, nT4[:, :, 1 + m, :], inv[s])
                    if m < 2:
                        bank = open_bank(pe, "t", l, b, 5 + m)
                        taken(pe, "m", l, b, m)
                        four(bank, invT[s], merged)
                    bank = open_bank(pe, "tt", l, b, 5 + m)
                    taken(pe, "m", l, b, m)
                    four(bank, merged, invT[s])
                bank = open_bank(pe, "rhs", l, b)
                if t > 0:
                    pe.wait_ge(state_ready, 4 * l + b - 1)
                for i in range(2):
                    if t > 0:
                        mm(bank[:, i * P:(i + 1) * P], ar[:, d, i, 0, c0:c1], S_diag[:, 2 * d + i, :, :],
                           True, False)
                    for j in (2 * i, 2 * i + 1):
                        p = 64 * (j % 2)
                        last = mm(bank[:, j * 64:(j + 1) * 64], g4[:, j, 0, :], rv_tm[:, i, t, p:p + 64],
                                  t == 0, True)
                last.then_inc(psum_filled, 1)
                bank = open_bank(pe, "x", l, b)
                taken(pe, "rhs", l, b)
                taken(pe, "tt", l, b, 7)
                for j in range(4):
                    last = mm(bank[:, j * 64:(j + 1) * 64], invT[0][:, j, :], r_rhs[:, j, :])
                last.then_inc(psum_filled, 1)
                bank = open_bank(pe, "y", l, b)
                taken(pe, "x", l, b)
                for i in range(2):
                    if t > 0:
                        mm(bank[:, i * P:(i + 1) * P], S_diag[:, 2 * d + i, :, :], ar[:, d, i, 1, c0:c1],
                           True, False)
                    for j in (2 * i, 2 * i + 1):
                        p = 64 * (j % 2)
                        out = bank[p:p + 64, i * P:(i + 1) * P]
                        mm(out, rv_tm[:, i, t, p:p + 64], g4[:, j, 1, :], t == 0, False)
                        last = mm(out, x_sol[:, j, :], g4[:, j, 3, :], False, True)
                last.then_inc(psum_filled, 1)
                if b < STATE_BATCHES:
                    bank = open_bank(pe, "kbt", l, b)
                    for i in range(2):
                        tr(bank[:, (2 * i) * P:(2 * i + 1) * P], kb[:, 0, d, i, c0:c1])
                        last = tr(bank[:, (2 * i + 1) * P:(2 * i + 2) * P], kb[:, 1, d, i, c0:c1])
                    last.then_inc(psum_filled, 1)
                    bank = open_bank(pe, "st", l, b)
                    taken(pe, "kbt", l, b)
                    for j in range(4):
                        i, p = j // 2, 64 * (j % 2)
                        out = bank[p:p + 64, i * 64:(i + 1) * 64]
                        mm(out, kb_tm[:, 2 * i, p:p + 64], rv_tm[:, i, t, p:p + 64], True, False)
                        last = mm(out, kb_tm[:, 2 * i + 1, p:p + 64], x_sol[:, j, :], False, True)
                    last.then_inc(psum_filled, 1)

            def rwkv_norm(l):
                for i in range(2):
                    bank = open_bank(pe, "gnm", l, i)
                    pe.wait_ge(gn_in_ready, l + 1)
                    mm(bank[:, 0:W], C("mean64"), y_rw[:, i, :]).then_inc(psum_filled, 1)
                for i in range(2):
                    bank = open_bank(pe, "gnv", l, i)
                    pe.wait_ge(gn_sq_ready, l + 1)
                    mm(bank[:, 0:W], C("mean64"), sq[:, i, :]).then_inc(psum_filled, 1)

            def ssd(l):
                bank = open_bank(pe, "dtt", l)
                pe.wait_ge(cs_ready, l + 1)
                for t in range(TILES):
                    for k, src in ((0, dt_t), (1, cs)):
                        c = (2 * t + k) * DT_ROWS
                        last = tr(bank[:, c:c + DT_ROWS], src[0:DT_ROWS, COL[t]:COL[t] + P], DT_ROWS)
                last.then_inc(psum_filled, 1)
                for r in range(8):
                    bank = open_bank(pe, "cs", l, r)
                    row = 32 * (r // 4) + r % 4
                    pick = C("ident")[0:DT_ROWS, row:row + 1].broadcast_to([DT_ROWS, P])
                    mm(bank[:, 0:W], pick, cs[0:DT_ROWS, :]).then_inc(psum_filled, 1)
                for t in range(TILES):
                    bank = open_bank(pe, "xt", l, t)
                    pe.wait_ge(silu_ready, l + 1)
                    for i in range(3):
                        last = tr(bank[:, i * P:(i + 1) * P], u[:, UX + i, 1 + COL[t]:1 + COL[t] + P])
                    last.then_inc(psum_filled, 1)
                    for g in range(2):
                        bank = open_bank(pe, "gt", l, t, g)
                        p = 64 * g
                        mm(bank[:, 0:P], u[p:p + 64, UB, 1 + COL[t]:1 + COL[t] + P],
                           u[p:p + 64, UC, 1 + COL[t]:1 + COL[t] + P]).then_inc(psum_filled, 1)
                for s, (t, d) in enumerate(SSD_STATES):
                    bank = open_bank(pe, "hst", l, s)
                    pe.wait_ge(xdd_ready, l + 1)
                    for g in range(2):
                        p = 64 * g
                        last = mm(bank[p:p + 64, 0:P], x_tm[:, t, 2 * P + p:2 * P + p + 64],
                                  xdd[:, s, 2 * g:2 * g + 2, :])
                    last.then_inc(psum_filled, 1)
                for t in range(TILES):
                    c0, c1 = COL[t], COL[t] + P
                    if t == 0:
                        taken(pe, "gt", l, 2, 1)
                    if t == 1:
                        taken(pe, "hst", l, 3)
                    for g in range(2):
                        bank = open_bank(pe, "ys", l, t, g)
                        for hh in range(2):
                            h, p = 2 * g + hh, 64 * hh
                            out = bank[p:p + 64, 0:P]
                            for d in range(2):
                                r = 4 * d + h
                                last = mm(out, xdt[:, t, d, h, :], le[:, r, c0:c1], d == 0, d == 1 and t == 0)
                            if t > 0:
                                for d in range(2):
                                    r, q = 4 * d + h, 64 * g
                                    first = t == 1 + d
                                    src = shaped(Lp("sssd"), 4, 64) if first else h_mid
                                    hs = src[q:q + 64, 2 * d + hh, :]
                                    last = mm(out, hs, ce[q:q + 64, r, (t - 1) * P:t * P], False, d == 1)
                        last.then_inc(psum_filled, 1)
                bank = open_bank(pe, "yms", l)
                pe.wait_ge(gated_sq_ready, l + 1)
                for i in range(2):
                    last = mm(bank[:, 0:W], C("mean256"), sq[:, i, :], i == 0, i == 1)
                last.then_inc(psum_filled, 1)

            def out_projection(l):
                taken(pe, "pv", l, 2)
                pe.wait_ge(mix_ready, l + 1)
                for n in range(KT):
                    if n % 2 == 0:
                        item = next_item()
                    bank = open_bank(pe, "out", l, n)
                    project(item, (n % 2) * KT * P, o, KT, bank[:, 0:W]).then_inc(psum_filled, 1)

            def moe(l):
                bank = open_bank(pe, "lg", l)
                pe.wait_ge(h_ready, 4 * l + 4)
                rw_ = shaped(C("router"), KT, 16)
                for t in range(TILES):
                    for k in range(KT):
                        last = mm(bank[:, 16 * t:16 * t + 16], hT[:, k, COL[t]:COL[t] + P], rw_[:, k, :],
                                  k == 0, k == KT - 1)
                last.then_inc(psum_filled, 1)
                bank = open_bank(pe, "ct", l)
                pe.wait_ge(comb_ready, l + 1)
                for t in range(TILES):
                    last = tr(bank[0:16, t * P:(t + 1) * P], rt[:, 0, 16 * t:16 * t + 16])
                last.then_inc(psum_filled, 1)
                for e in range(EXPERTS):
                    n = l * EXPERTS + e
                    bank = open_bank(pe, "cb", l, e)
                    if e == 0:
                        taken(pe, "ct", l)
                    pick = C("ident")[0:16, e:e + 1].broadcast_to([16, P])
                    mm(bank[:, 0:W], pick, comb_T[0:16, :]).then_inc(psum_filled, 1)
                    gate, up = next_item(), next_item()
                    for f in range(2):
                        for name, item in (("gate", gate), ("up", up)):
                            bank = open_bank(pe, name, l, e, f)
                            last = project(item, f * KT * P, hT, KT, bank[:, 0:W])
                            last.then_inc(psum_filled, 1)
                    down = next_item()
                    for c in range(KT):
                        bank = open_bank(pe, "down", l, e, c)
                        if c == 0:
                            taken(pe, "up", l, e, 1)
                        for f in range(2):
                            last = mm(bank[:, 0:W], down[:, (2 * c + f) * P:(2 * c + f + 1) * P],
                                      hid[n % 2][:, f, :], f == 0, f == 1)
                        last.then_inc(psum_filled, 1)

            pe.wait_ge(consts_loaded, 16)
            for l in range(DEPTH):
                modulation(l)
                mean_square(l, 1)
                in_projection(l)
                attention(l)
                rwkv_inputs(l)
                for b in range(len(RW_BATCHES)):
                    rwkv_batch(l, b)
                rwkv_norm(l)
                ssd(l)
                out_projection(l)
                mean_square(l, 2)
                moe(l)
            assert opened[0] == len(plan)

        @block.scalar
        def _(act):
            chain = [0]

            def link(ins):
                chain[0] += 1
                ins.then_inc(chain_a, 1)
                act.wait_ge(chain_a, chain[0])

            def f(out, in_, func, **kw):
                return nc.scalar.activation(out, in_, func, **kw)

            def root(out, eps, *key):
                bank = filled(act, *key)
                f(out, bank[:, 0:W], ACT.Sqrt, bias=C(eps)).then_inc(read(*key), 1)

            def squares(l, which):
                if which == 2:
                    taken(act, "out", l, KT - 1)
                elif l:
                    act.wait_ge(x_ready, l)
                f(sq, xT, ACT.Square).then_inc(xsq_ready, 1)
                root(tmp[:, 0:W], "eps", "ms", l, which)

            def attention(l):
                for c in range(5):
                    taken(act, "u", l, c)
                f(sq[:, 0:5, :], u[:, 0:5, 1:W + 1], ACT.Square).then_inc(qk_sq_ready, 1)
                for i in range(5):
                    root(qn[:, i, :], "eps", "qkms", l, i)
                bank = filled(act, "vt", l)
                f(v_tm, shaped(bank[:, 0:3 * P], 3, P), ACT.Copy).then_inc(read("vt", l), 1)
                for t in range(TILES):
                    n = 3 * P if t else P
                    act.wait_ge(shifted_ready, TILES * l + t + 1)
                    for h in range(8):
                        f(scores[t % 2][:, h, 0:n], scores[t % 2][:, h, 0:n], ACT.Exp,
                          bias=att_cols[:, 8 + h:9 + h], accum_out=att_cols[:, 16 + h:17 + h])
                    f(att_cols[:, 32:40], att_cols[:, 24:32], ACT.Exp).then_inc(exps_ready, 1)
                    if t:
                        filled(act, "pv", l, t - 1)
                    for h in range(8):
                        bank = filled(act, "pT", l, t, h)
                        f(probsT[:, h, 0:n], bank[:, 0:n], ACT.Copy).then_inc(read("pT", l, t, h), 1)
                    bank = filled(act, "pv", l, t)
                    f(o[:, 0:4, COL[t]:COL[t] + P], shaped(bank[:, :], 4, P), ACT.Copy)\
                        .then_inc(read("pv", l, t), 1)

            def rwkv_inputs(l):
                act.wait_ge(mixed_ready, l + 1)
                f(mixed[0:32, 6, :], mixed[0:32, 6, :], ACT.Tanh)
                f(mixed[64:P, 6, :], mixed[64:P, 6, :], ACT.Sigmoid).then_inc(lora_ready, 1)
                for name, out, bias in (("wl", sgw, "w0"), ("al", asig, "a0")):
                    for d in range(2):
                        for i in range(2):
                            bank = filled(act, name, l, d, i)
                            k = 2 * d + i
                            f(out[:, k, :], bank[:, 0:W], ACT.Sigmoid, bias=Lc(bias, k))\
                                .then_inc(read(name, l, d, i), 1)
                for i in range(2):
                    bank = filled(act, "gg", l, i)
                    f(gate_rw[:, i, :], bank[:, 0:W], ACT.Copy).then_inc(read("gg", l, i), 1)
                for i in range(2):
                    root(tmp[:, i * W:(i + 1) * W], "eps_kk", "kkn", l, i)
                for i in range(2):
                    bank = filled(act, "rvt", l, i)
                    f(rv_tm[:, i, :, :], shaped(bank[:, 0:3 * P], 3, P), ACT.Copy).then_inc(read("rvt", l, i), 1)
                act.wait_ge(decay_arg_ready, l + 1)
                for d in range(2):
                    Dd, Fd = csum[:, 2 * d:2 * d + 2, :], sgw[:, 2 * d:2 * d + 2, :]
                    incl, excl, s = (Dd, Fd, -DECAY) if d == 0 else (Fd, Dd, DECAY)
                    f(ar[:, d, :, 0, :], excl, ACT.Exp, scale=s)
                    f(ar[:, d, :, 1, :], incl, ACT.Exp, scale=s)
                    f(kb[:, 0, d, :, :], incl, ACT.Exp, scale=-s)
                f(decay_half, half_total, ACT.Exp, scale=DECAY).then_inc(decay_exp_ready, 1)

            def rwkv_batch(l, b):
                def copy(out, *key):
                    bank = filled(act, *key)
                    n = out.shape[1] * out.shape[2]
                    f(out, shaped(bank[:, 0:n], out.shape[1], out.shape[2]), ACT.Copy).then_inc(read(*key), 1)
                for k in range(1, 4):
                    copy(pw[k % 2], "p", l, b, k)
                    copy(pwT[k % 2], "pt", l, b, k)
                for m in range(3):
                    copy(merged, "m", l, b, m)
                copy(r_rhs, "rhs", l, b)
                if b < STATE_BATCHES:
                    copy(kb_tm, "kbt", l, b)

            def ssd(l):
                act.wait_ge(rwkv_done, l + 1)
                z = dt_t[0:DT_ROWS, :]
                raw = u[0:DT_ROWS, UDT, 1:W + 1]
                b1 = Lc("dtb", 0, slice(0, DT_ROWS))
                taken(act, "u", l, UDT)
                link(f(dta[0:DT_ROWS, :], raw, ACT.Abs, bias=b1))
                f(z, raw, ACT.Relu, bias=b1)
                f(neg_a[0:DT_ROWS, 0:1], Lc("alog", 0, slice(0, DT_ROWS)), ACT.Exp)
                link(f(dta[0:DT_ROWS, :], dta[0:DT_ROWS, :], ACT.Exp, scale=-1.0))
                f(dta[0:DT_ROWS, :], dta[0:DT_ROWS, :], ACT.Ln, bias=1.0).then_inc(dt_parts, 1)
                act.wait_ge(conv_ready, l + 1)
                f(u[:, UX:UDT, 1:W + 1], u[:, UX:UDT, 1:W + 1], ACT.Silu).then_inc(silu_ready, 1)
                f(u[:, UZ:UZ + 2, 1:W + 1], u[:, UZ:UZ + 2, 1:W + 1], ACT.Silu).then_inc(z_ready, 1)
                bank = filled(act, "dtt", l)
                f(dtc, bank[:, 0:6 * DT_ROWS].rearrange("p (t k r) -> p t k r", t=TILES, k=2), ACT.Copy)\
                    .then_inc(read("dtt", l), 1)
                for r in range(8):
                    bank = filled(act, "cs", l, r)
                    f(le[:, r, :], bank[:, 0:W], ACT.Copy).then_inc(read("cs", l, r), 1)
                taken(act, "cs", l, 7)
                f(ce, le[:, :, LAT:W], ACT.Exp).then_inc(lat_decay_ready, 1)
                for t in range(TILES):
                    bank = filled(act, "xt", l, t)
                    f(x_tm[:, t, :], bank[:, 0:3 * P], ACT.Copy).then_inc(read("xt", l, t), 1)
                act.wait_ge(din_arg_ready, l + 1)
                f(decay_in, decay_in, ACT.Exp)
                f(chunk_decay, total_b, ACT.Exp).then_inc(din_ready, 1)
                act.wait_ge(le_arg_ready, l + 1)
                f(le, le, ACT.Exp).then_inc(le_ready, 1)

            def moe(l):
                bank = filled(act, "lg", l)
                f(rt[:, 1, :], bank[:, 0:48], ACT.Sigmoid).then_inc(read("lg", l), 1)
                bank = filled(act, "ct", l)
                f(comb_T[0:16, 0:P], bank[0:16, 0:P], ACT.Copy)
                f(comb_T[0:16, LAT:W], bank[0:16, P:3 * P], ACT.Copy).then_inc(read("ct", l), 1)
                for e in range(EXPERTS):
                    for k in range(2):
                        bank = filled(act, "gate", l, e, k)
                        if e:
                            taken(act, "up", l, e - 1, k)
                        f(sg[:, k, :], bank[:, 0:W], ACT.Silu).then_inc(read("gate", l, e, k), 1)

            act.wait_ge(consts_loaded, 48)
            f(scond[:, :], cond[:, :], ACT.Silu).then_inc(cond_ready, 1)
            for l in range(DEPTH):
                squares(l, 1)
                if l == 0:
                    act.wait_ge(gaps_cleared, 1)
                for c in range(1, U_TILES, 2):
                    bank = filled(act, "u", l, c)
                    m = DT_ROWS if c == UDT else P
                    f(u[0:m, c, 1:W + 1], bank[0:m, 0:W], ACT.Copy).then_inc(read("u", l, c), 1)
                attention(l)
                rwkv_inputs(l)
                for b in range(len(RW_BATCHES)):
                    rwkv_batch(l, b)
                for i in range(2):
                    root(tmp[:, i * W:(i + 1) * W], "eps_gn", "gnv", l, i)
                ssd(l)
                root(tmp[:, 0:W], "eps", "yms", l)
                squares(l, 2)
                moe(l)

        @block.vector
        def _(dve):
            v = nc.vector
            chain = [0]

            def link(ins):
                chain[0] += 1
                ins.then_inc(chain_v, 1)
                dve.wait_ge(chain_v, chain[0])

            def tt(out, x, y, op):
                return v.tensor_tensor(out, x, y, op)

            def stt(out, x, s, y, op0, op1):
                return v.scalar_tensor_tensor(out, x, s, y, op0, op1)

            def ts(out, x, s1, s2, op0, op1=None):
                return v.tensor_scalar(out, x, s1, s2, op0, op1) if op1 is not None else \
                    v.tensor_scalar(out, x, s1, None, op0)

            def norm(l, which):
                scale, shift = (scale1, 0) if which == 1 else (scale2, 24)
                taken(dve, "ms", l, which)
                link(v.reciprocal(tmp[:, 0:W], tmp[:, 0:W]))
                link(tt(hT, xT, bc(tmp[:, 0:W], 1, KT), ALU.mult))
                for g, lo, hi in SEGMENTS:
                    for k in range(KT):
                        last = ts(hT[:, k, lo:hi], hT[:, k, lo:hi], scale[:, k, g:g + 1],
                                  mod[:, shift + k, g:g + 1], ALU.mult, ALU.add)
                    last.then_inc(h_ready, 1)

            def modulation(l):
                dve.wait_ge(small_loaded, 16 * (l + 1))
                bm = bc(Lp("bmod"), 2, 2)
                for i in range(MOD_ITEMS):
                    bank = filled(dve, "mod", l, i)
                    tt(mod[:, 2 * i:2 * i + 2, :], shaped(bank[:, 0:4], 2, 2), bm[:, 2 * i:2 * i + 2, :], ALU.add)\
                        .then_inc(read("mod", l, i), 1)
                taken(dve, "mod", l, MOD_ITEMS - 1)
                for scale, first, name in ((scale1, 8, "n1"), (scale2, 32, "n2")):
                    last = stt(scale, mod[:, first:first + 8, :], 1.0, bc(Lp(name), 2, 2), ALU.add, ALU.mult)
                link(last)

            def attention(l):
                for i in range(5):
                    taken(dve, "qkms", l, i)
                    link(v.reciprocal(qn[:, i, :], qn[:, i, :]))
                    stt(qn[:, i, :], u[:, i, 1:W + 1], Lc("kw" if i == 4 else "qw", 0), qn[:, i, :],
                        ALU.mult, ALU.mult).then_inc(qn_ready, 1)
                dve.wait_ge(qn_ready, 5 * (l + 1))
                v.tensor_copy(new_k[l][:, :], qn[:, 4, 0:P]).then_inc(kv_copied, 1)
                taken(dve, "u", l, UV)
                v.tensor_copy(new_v[l][:, :], u[:, UV, 1:P + 1]).then_inc(kv_copied, 1)
                for i in range(5):
                    bank = filled(dve, "rope", l, i)
                    link(tt(tmp[:, 0:2 * P], bank[:, 0:2 * P], C("sin"), ALU.mult))
                    tt(qn[:, i, LAT:W], qn[:, i, LAT:W], C("cos"), ALU.mult).then_inc(read("rope", l, i), 1)
                    taken(dve, "rope", l, i)
                    last = tt(qn[:, i, LAT:W], qn[:, i, LAT:W], tmp[:, 0:2 * P], ALU.add)
                    if i < 4:
                        link(last)
                last.then_inc(rope_ready, 1)
                for t in range(TILES):
                    n = 3 * P if t else P
                    sc = scores[t % 2]
                    if t == 2:
                        filled(dve, "pT", l, 0, 7)
                    for h in range(8):
                        bank = filled(dve, "sc", l, t, h)
                        scale = 64 ** -0.5
                        if t:
                            m = C("att")[:, (t - 1) * 256:t * 256]
                            stt(sc[:, h, 0:256], bank[:, 0:256], scale, m, ALU.mult, ALU.add)
                            last = ts(sc[:, h, 256:384], bank[:, 256:384], scale, None, ALU.mult)
                        else:
                            last = ts(sc[:, h, 0:P], bank[:, 0:P], scale, None, ALU.mult)
                        last.then_inc(read("sc", l, t, h), 1)
                    taken(dve, "sc", l, t, 7)
                    link(v.tensor_reduce(att_cols[:, 0:8], sc[:, :, 0:n], X, ALU.max))
                    link(tt(att_cols[:, 0:8], att_cols[:, 0:8], Lp("sink"), ALU.max))
                    ts(att_cols[:, 8:16], att_cols[:, 0:8], -1.0, None, ALU.mult)
                    tt(att_cols[:, 24:32], Lp("sink"), att_cols[:, 0:8], ALU.subtract).then_inc(shifted_ready, 1)
                    dve.wait_ge(exps_ready, TILES * l + t + 1)
                    link(tt(att_cols[:, 40:48], att_cols[:, 16:24], att_cols[:, 32:40], ALU.add))
                    link(v.reciprocal(att_cols[:, 48:56], att_cols[:, 40:48]))
                    tt(sc[:, :, 0:n], sc[:, :, 0:n], bc(att_cols[:, 48:56], 2, n), ALU.mult)\
                        .then_inc(probs_ready, 1)

            def rwkv_inputs(l):
                taken(dve, "pv", l, 2)
                for c in range(6, 13):
                    taken(dve, "u", l, c)
                keep = cols[:, 0:7]
                link(tt(keep, Lp("mu0"), Lp("mu1"), ALU.add))
                link(ts(keep, keep, -1.0, 1.0, ALU.mult, ALU.add))
                for j in range(7):
                    last = ts(mixed[:, j, :], u[:, UR + j, 1:W + 1], cols[:, j:j + 1], None, ALU.mult)
                link(last)
                for j in range(7):
                    last = stt(mixed[:, j, :], u[:, UR + j, 0:W], Lc("mu0", j), mixed[:, j, :], ALU.mult, ALU.add)
                link(last)
                for j in range(7):
                    last = stt(mixed[:, j, :], u[:, UR + j, 2:W + 2], Lc("mu1", j), mixed[:, j, :],
                               ALU.mult, ALU.add)
                last.then_inc(mixed_ready, 1)
                dve.wait_ge(mixed_ready, l + 1)
                for i in range(2):
                    ts(kdir[:, i, :], mixed[:, 2 + i, :], Lc("kk", i), None, ALU.mult)
                    last = stt(sq[:, 2 + i, :], mixed[:, i, :], Lc("rk", i), mixed[:, 2 + i, :],
                               ALU.mult, ALU.mult)
                last.then_inc(bonus_in_ready, 1)
                dve.wait_ge(bonus_in_ready, l + 1)
                tt(sq[:, 0:2, :], kdir, kdir, ALU.mult).then_inc(kk_sq_ready, 1)
                taken(dve, "kkn", l, 1)
                link(v.reciprocal(tmp[:, :], tmp[:, :]))
                link(tt(kdir, kdir, shaped(tmp[:, :], 2, W), ALU.mult))
                for i in range(2):
                    bank = filled(dve, "bon", l, i)
                    tt(bonus[:, i, :], bank[:, 0:W], mixed[:, 4 + i, :], ALU.mult).then_inc(read("bon", l, i), 1)
                for k in range(4):
                    taken(dve, "wl", l, k // 2, k % 2)
                    last = v.tensor_tensor_scan(csum[:, k, :], C("restart"), sgw[:, k, :], 0.0, ALU.mult, ALU.add)
                link(last)
                for t in range(TILES):
                    e = COL[t] + P - 1
                    last = ts(half_total[:, :, t:t + 1], csum[:, :, e:e + 1], -0.5, None, ALU.mult)
                link(last)
                for t in range(TILES):
                    c0 = COL[t]
                    last = tt(csum[:, :, c0:c0 + P], csum[:, :, c0:c0 + P],
                              half_total[:, :, t:t + 1].broadcast_to([P, 4, P]), ALU.add)
                link(last)
                tt(sgw, csum, sgw, ALU.subtract).then_inc(decay_arg_ready, 1)
                taken(dve, "al", l, 1, 1)
                for d in range(2):
                    last = stt(kb[:, 1, d, :, :], kdir, -1.0, asig[:, 2 * d:2 * d + 2, :], ALU.mult, ALU.mult)
                link(last)
                link(ts(cols[:, 8:10], Lp("ka"), -1.0, 1.0, ALU.mult, ALU.add))
                for k in range(4):
                    last = ts(asig[:, k, :], asig[:, k, :], Lc("ka", k % 2), cols[:, 8 + k % 2:9 + k % 2],
                              ALU.mult, ALU.add)
                link(last)
                for d in range(2):
                    last = tt(asig[:, 2 * d:2 * d + 2, :], asig[:, 2 * d:2 * d + 2, :], mixed[:, 2:4, :], ALU.mult)
                link(last)
                dve.wait_ge(decay_exp_ready, l + 1)
                for d in range(2):
                    tt(ar[:, d, :, 0, :], ar[:, d, :, 0, :], kdir, ALU.mult)
                    tt(ar[:, d, :, 1, :], ar[:, d, :, 1, :], mixed[:, 0:2, :], ALU.mult)
                    last = tt(kb[:, 1, d, :, :], kb[:, 1, d, :, :], kb[:, 0, d, :, :], ALU.mult)
                link(last)
                for d in range(2):
                    last = tt(kb[:, 0, d, :, :], kb[:, 0, d, :, :], asig[:, 2 * d:2 * d + 2, :], ALU.mult)
                last.then_inc(factors_ready, 1)
                dve.wait_ge(factors_ready, l + 1)

            def scale_state(t, d, src):
                for i in range(2):
                    k = 2 * d + i
                    ts(S_til[:, k, :], src[:, k, :], decay_half[:, k, t:t + 1], None, ALU.mult)
                    for half in range(2):
                        q = slice(64 * half, 64 * half + 64)
                        last = ts(S_diag[q, k, half, :], src[q, k, :], decay_half[q, k, t:t + 1], None, ALU.mult)
                return last

            def rwkv_batch(l, b):
                t, d = RW_BATCHES[b]
                if t > 0:
                    src = shaped(Lp("srw"), 4, 64) if b < STATE_BATCHES else S_lat
                    scale_state(t, d, src).then_inc(state_ready, 1)
                if b == 0:
                    v.memset(S_diag, 0.0)
                    dve.wait_ge(decay_exp_ready, l + 1)
                for j in range(4):
                    bank = filled(dve, "g4", l, b, j)
                    tt(g4[:, j, :, :], shaped(bank[:, :], 4, P), shaped(C(f"rw{d}"), 4, P), ALU.mult)\
                        .then_inc(read("g4", l, b, j), 1)
                for half in range(2):
                    bank = filled(dve, "nd", l, b, half)
                    tt(nd[:, half::2, :], shaped(bank[:, 0:2 * P], 2, P), bc(C(f"nd{d}"), 1, 2), ALU.mult)\
                        .then_inc(read("nd", l, b, half), 1)
                taken(dve, "nd", l, b, 1)
                for j in range(4):
                    last = tt(nT4[:, j, :, :], bc(g4[:, j, 2, :], 1, 4), shaped(C("inv"), 4, P), ALU.mult)
                link(last)
                tt(inv[0], nd, bc(C("ident"), 1, 4), ALU.add)
                tt(invT[0], nT4[:, :, 0, :], bc(C("ident"), 1, 4), ALU.add).then_inc(matrices_ready, 1)
                dve.wait_ge(matrices_ready, len(RW_BATCHES) * l + b + 1)
                for k in range(2, 8):
                    s = k % 2
                    if k < 7:
                        bank = filled(dve, "t", l, b, k)
                        tt(inv[1 - s], inv[s], shaped(bank[:, :], 4, P), ALU.add).then_inc(read("t", l, b, k), 1)
                    bank = filled(dve, "tt", l, b, k)
                    tt(invT[1 - s], invT[s], shaped(bank[:, :], 4, P), ALU.add).then_inc(read("tt", l, b, k), 1)
                    taken(dve, "tt", l, b, k)
                bank = filled(dve, "x", l, b)
                v.tensor_copy(x_sol, shaped(bank[:, 0:256], 4, 64)).then_inc(read("x", l, b), 1)
                bank = filled(dve, "y", l, b)
                src, out = shaped(bank[:, 0:2 * P], 2, P), y_rw[:, :, COL[t]:COL[t] + P]
                if b in (0, 2, 3):
                    last = v.tensor_copy(out, src)
                else:
                    last = tt(out, out, src, ALU.add)
                last.then_inc(read("y", l, b), 1)
                if b < STATE_BATCHES:
                    bank = filled(dve, "st", l, b)
                    if t > 0:
                        link(tt(S_lat[:, 2 * d:2 * d + 2, :], S_til[:, 2 * d:2 * d + 2, :],
                                shaped(bank[:, 0:P], 2, 64), ALU.add))
                    for i in range(2):
                        k = 2 * d + i
                        x = S_lat[:, k, :] if t > 0 else bank[:, i * 64:(i + 1) * 64]
                        out = S_lat[:, k, :] if t > 0 else state_rw[l][:, k, :]
                        last = ts(out, x, decay_half[:, k, t:t + 1], None, ALU.mult)
                    last.then_inc(read("st", l, b), 1)
                    taken(dve, "st", l, b)

            def rwkv_norm(l):
                last = v.memset(y_rw[:, :, P:LAT], 0.0)
                last.then_inc(gn_in_ready, 1)
                dve.wait_ge(gn_in_ready, l + 1)
                for i in range(2):
                    bank = filled(dve, "gnm", l, i)
                    tt(y_rw[:, i, :], y_rw[:, i, :], bank[:, 0:W], ALU.subtract).then_inc(read("gnm", l, i), 1)
                taken(dve, "gnm", l, 1)
                tt(sq[:, 0:2, :], y_rw, y_rw, ALU.mult).then_inc(gn_sq_ready, 1)
                taken(dve, "gnv", l, 1)
                link(v.reciprocal(tmp[:, :], tmp[:, :]))
                link(tt(y_rw, y_rw, shaped(tmp[:, :], 2, W), ALU.mult))
                for i in range(2):
                    last = ts(y_rw[:, i, :], y_rw[:, i, :], Lc("lnw", i), Lc("lnb", i), ALU.mult, ALU.add)
                link(last)
                link(tt(y_rw, y_rw, bonus, ALU.add))
                for lo, hi in ((0, P), (LAT, W)):
                    last = tt(o[:, 4:6, lo:hi], y_rw[:, :, lo:hi], gate_rw[:, :, lo:hi], ALU.mult)
                last.then_inc(rwkv_done, 1)
                dve.wait_ge(rwkv_done, l + 1)

            def ssd(l):
                R = slice(0, DT_ROWS)
                for c in range(13, 20):
                    taken(dve, "u", l, c)
                cw = Lp("cw")
                conv = shaped(sq_flat[:, 0:4 * W], 4, W)
                for j in range(4):
                    last = ts(conv[:, j, :], u[:, UX + j, 1:W + 1], cw[:, 4 + j:5 + j], Lc("cb", j),
                              ALU.mult, ALU.add)
                link(last)
                for j in range(4):
                    last = stt(conv[:, j, :], u[:, UX + j, 0:W], cw[:, j:j + 1], conv[:, j, :], ALU.mult, ALU.add)
                link(last)
                for j in range(4):
                    last = stt(conv[:, j, :], u[:, UX + j, 2:W + 2], cw[:, 8 + j:9 + j], conv[:, j, :],
                               ALU.mult, ALU.add)
                link(last)
                v.tensor_copy(u[:, UX:UDT, 1:W + 1], conv).then_inc(conv_ready, 1)
                dve.wait_ge(dt_parts, l + 1)
                link(tt(dt_t[R, :], dt_t[R, :], dta[R, :], ALU.add))
                link(ts(dta[R, :], dt_t[R, :], neg_a[R, 0:1], -1.0, ALU.mult, ALU.mult))
                link(v.tensor_tensor_scan(cs[R, :], C("restart", R), dta[R, :], 0.0, ALU.mult, ALU.add))
                B = slice(32, 64)
                link(tt(dtmp[B, :], dta[B, :], cs[B, :], ALU.subtract))
                for t in range(TILES):
                    e = COL[t] + P - 1
                    last = v.tensor_copy(cols[B, 16 + t:17 + t], cs[B, e:e + 1])
                link(last)
                for t in range(TILES):
                    c0 = COL[t]
                    last = ts(cs[B, c0:c0 + P], dtmp[B, c0:c0 + P], cols[B, 16 + t:17 + t], None, ALU.add)
                last.then_inc(cs_ready, 1)
                taken(dve, "cs", l, 7)
                taken(dve, "dtt", l)
                for t in range(TILES):
                    for d in range(2):
                        e = COL[t] + (P - 1 if d == 0 else 0)
                        last = v.tensor_copy(total_b[:, 4 * d:4 * d + 4, t:t + 1], le[:, 4 * d:4 * d + 4, e:e + 1])
                link(last)
                for t in range(TILES):
                    for d in range(2):
                        last = tt(decay_in[:, t, 4 * d:4 * d + 4], total_b[:, 4 * d:4 * d + 4, t],
                                  dtc[:, t, 1, 32 * d:32 * d + 4], ALU.subtract)
                last.then_inc(din_arg_ready, 1)
                dve.wait_ge(lat_decay_ready, l + 1)
                for r in range(8):
                    d, row = r // 4, 32 * (r // 4) + r % 4
                    for t in range(TILES):
                        last = stt(le[:, r, COL[t]:COL[t] + P], le[:, r, COL[t]:COL[t] + P],
                                   dtc[:, t, 1, row:row + 1], C(f"ssd{d}"), ALU.subtract, ALU.add)
                last.then_inc(le_arg_ready, 1)
                taken(dve, "xt", l, 2)
                for t in range(TILES):
                    xv = x_tm[:, t, 0:2 * P].rearrange("p (h c) -> p h c", h=4)
                    for d in range(2):
                        last = tt(xdt[:, t, d, :, :], xv, bc(dtc[:, t, 0, 32 * d:32 * d + 4], 2, 64), ALU.mult)
                link(last)
                dve.wait_ge(din_ready, l + 1)
                for s, (t, d) in enumerate(SSD_STATES):
                    last = tt(xdd[:, s, :, :], xdt[:, t, d, :, :], bc(decay_in[:, t, 4 * d:4 * d + 4], 2, 64),
                              ALU.mult)
                last.then_inc(xdd_ready, 1)
                dve.wait_ge(silu_ready, l + 1)
                for g in range(2):
                    q = slice(64 * g, 64 * g + 64)
                    for d in range(2):
                        r = 4 * d + 2 * g
                        last = tt(ce[q, r:r + 2, :], ce[q, r:r + 2, :], bc(u[q, UC, 1 + LAT:1 + W], 1, 2), ALU.mult)
                dve.wait_ge(le_ready, l + 1)
                for t in range(TILES):
                    for g in range(2):
                        bank = filled(dve, "gt", l, t, g)
                        for r in (2 * g, 4 + 2 * g):
                            x = le[:, r:r + 2, COL[t]:COL[t] + P]
                            last = tt(x, x, bc(bank[:, 0:P], 1, 2), ALU.mult)
                        last.then_inc(read("gt", l, t, g), 1)
                init = shaped(Lp("sssd"), 4, 64)
                for s, (t, d) in enumerate(SSD_STATES):
                    bank = filled(dve, "hst", l, s)
                    src = shaped(bank[:, 0:P], 2, 64)
                    if t == 0:
                        last = v.tensor_copy(state_ssd[l][:, 2 * d:2 * d + 2, :], src)
                    else:
                        for g in range(2):
                            q = slice(64 * g, 64 * g + 64)
                            for hh in range(2):
                                r = 4 * d + 2 * g + hh
                                last = stt(h_mid[q, 2 * d + hh, :], init[q, 2 * d + hh, :],
                                           chunk_decay[q, r, t:t + 1], src[q, hh, :], ALU.mult, ALU.add)
                    last.then_inc(read("hst", l, s), 1)
                for t in range(TILES):
                    for i in range(2):
                        bank = filled(dve, "ys", l, t, i)
                        last = stt(y_ssd[:, i, COL[t]:COL[t] + P], u[:, UX + i, 1 + COL[t]:1 + COL[t] + P],
                                   Lc("dskip", i), bank[:, 0:P], ALU.mult, ALU.add)
                        last.then_inc(read("ys", l, t, i), 1)
                link(v.memset(y_ssd[:, :, P:LAT], 0.0))
                dve.wait_ge(z_ready, l + 1)
                link(tt(y_ssd, y_ssd, u[:, UZ:UZ + 2, 1:W + 1], ALU.mult))
                tt(sq[:, 0:2, :], y_ssd, y_ssd, ALU.mult).then_inc(gated_sq_ready, 1)
                taken(dve, "yms", l)
                link(v.reciprocal(tmp[:, 0:W], tmp[:, 0:W]))
                for i in range(2):
                    for lo, hi in ((0, P), (LAT, W)):
                        last = stt(o[:, 6 + i, lo:hi], y_ssd[:, i, lo:hi], Lc("nw", i), tmp[:, lo:hi],
                                   ALU.mult, ALU.mult)
                last.then_inc(mix_ready, 1)

            def add_gated(bank, n, first):
                for g, lo, hi in SEGMENTS:
                    last = stt(xT[:, n, lo:hi], bank[:, lo:hi], mod[:, first + n, g:g + 1], xT[:, n, lo:hi],
                               ALU.mult, ALU.add)
                return last

            def routing(l):
                taken(dve, "lg", l)
                s = rt[:, 1, :]
                sel = rt[:, 2, :]

                def g3(k):
                    return shaped(rt[:, k, :], TILES, 16)

                def g4v(k):
                    return shaped(rt[:, k, :], TILES, 4, 4)

                link(tt(g3(2), g3(1), bc(C("rbias"), 1, TILES), ALU.add))
                q = g4v(2)

                def small4(k):
                    return rt[:, k, 0:12].rearrange("p (t g) -> p t g", t=TILES)
                tt(small4(3), q[:, :, :, 0], q[:, :, :, 1], ALU.max)
                tt(small4(4), q[:, :, :, 2], q[:, :, :, 3], ALU.max)
                tt(small4(5), q[:, :, :, 0], q[:, :, :, 1], ALU.min)
                link(tt(small4(6), q[:, :, :, 2], q[:, :, :, 3], ALU.min))
                tt(small4(7), small4(3), small4(4), ALU.max)
                tt(small4(8), small4(3), small4(4), ALU.min)
                link(tt(small4(9), small4(5), small4(6), ALU.max))
                link(tt(small4(8), small4(8), small4(9), ALU.max))
                link(tt(small4(7), small4(7), small4(8), ALU.add))

                def first_max(x, rank, n, w1, w2, w3):
                    m = rt[:, w1, 0:TILES]
                    link(v.tensor_reduce(m, x, X, ALU.max))
                    link(tt(w2, x, bc(m, 2, n), ALU.is_equal))
                    link(tt(w2, w2, bc(C(rank), 1, TILES), ALU.mult))
                    link(v.tensor_reduce(m, w2, X, ALU.max))
                    link(tt(w3, w2, bc(m, 2, n), ALU.is_equal))

                first_max(small4(7), "rank4", 4, 10, small4(8), small4(9))
                inside = g4v(11)
                link(v.tensor_copy(inside, bc(small4(9), 3, 4)))
                link(ts(rt[:, 12, :], rt[:, 11, :], -NEG, NEG, ALU.mult, ALU.add))
                link(tt(rt[:, 2, :], rt[:, 2, :], rt[:, 11, :], ALU.mult))
                link(tt(rt[:, 2, :], rt[:, 2, :], rt[:, 12, :], ALU.add))
                first_max(g3(2), "rank16", 16, 10, g3(13), g3(14))
                link(stt(rt[:, 2, :], rt[:, 14, :], 2 * NEG, rt[:, 2, :], ALU.mult, ALU.add))
                first_max(g3(2), "rank16", 16, 10, g3(13), g3(15))
                link(tt(rt[:, 14, :], rt[:, 14, :], rt[:, 15, :], ALU.add))
                link(tt(rt[:, 14, :], rt[:, 14, :], rt[:, 1, :], ALU.mult))
                link(v.tensor_reduce(rt[:, 10, 0:TILES], g3(14), X, ALU.add))
                link(v.reciprocal(rt[:, 10, 4:4 + TILES], rt[:, 10, 0:TILES]))
                v.memset(comb_T[0:16, P:LAT], 0.0)
                tt(g3(0), g3(14), bc(rt[:, 10, 4:4 + TILES], 2, 16), ALU.mult).then_inc(comb_ready, 1)

            def moe(l):
                for e in range(EXPERTS):
                    n = l * EXPERTS + e
                    if e >= 2:
                        filled(dve, "down", l, e - 2, KT - 1)
                    cb = filled(dve, "cb", l, e)
                    v.tensor_copy(tmp[:, 0:W], cb[:, 0:W]).then_inc(read("cb", l, e), 1)
                    taken(dve, "cb", l, e)
                    for k in range(2):
                        taken(dve, "gate", l, e, k)
                        link(tt(hid[n % 2][:, k, :], sg[:, k, :], tmp[:, 0:W], ALU.mult))
                        bank = filled(dve, "up", l, e, k)
                        tt(hid[n % 2][:, k, :], hid[n % 2][:, k, :], bank[:, 0:W], ALU.mult)\
                            .then_inc(read("up", l, e, k), 1)
                    for c in range(KT):
                        bank = filled(dve, "down", l, e, c)
                        if e == 0:
                            last = v.tensor_copy(moe_out[:, c, :], bank[:, 0:W])
                        else:
                            last = tt(moe_out[:, c, :], moe_out[:, c, :], bank[:, 0:W], ALU.add)
                        last.then_inc(read("down", l, e, c), 1)
                    taken(dve, "down", l, e, KT - 1)
                for c in range(KT):
                    last = add_gated(moe_out[:, c, :], c, 40)
                last.then_inc(x_ready, 1)
                dve.wait_ge(x_ready, l + 1)

            v.memset(u[:, :, 0:1], 0.0)
            v.memset(u[:, :, W + 1:W + 2], 0.0)
            v.memset(csum, 0.0)
            link(v.memset(o[:, :, P:LAT], 0.0))
            v.memset(cols[:, :], 0.0).then_inc(gaps_cleared, 1)
            dve.wait_ge(gaps_cleared, 1)
            dve.wait_ge(consts_loaded, 48)
            for l in range(DEPTH):
                modulation(l)
                norm(l, 1)
                if l:
                    v.memset(u[:, 0:13, 0:1], 0.0)
                    v.memset(u[:, 0:13, W + 1:W + 2], 0.0)
                for c in range(0, U_TILES, 2):
                    bank = filled(dve, "u", l, c)
                    v.tensor_copy(u[:, c, 1:W + 1], bank[:, 0:W]).then_inc(read("u", l, c), 1)
                attention(l)
                rwkv_inputs(l)
                for b in range(len(RW_BATCHES)):
                    rwkv_batch(l, b)
                rwkv_norm(l)
                ssd(l)
                for n in range(KT):
                    bank = filled(dve, "out", l, n)
                    add_gated(bank, n, 16).then_inc(read("out", l, n), 1)
                taken(dve, "out", l, KT - 1)
                norm(l, 2)
                routing(l)
                moe(l)


def constants():
    import numpy as np
    i = np.arange(P)
    row, col = i[:, None], i[None, :]
    same = lambda n: (row // n == col // n).astype(np.float32)
    rot = np.zeros((P, P), np.float32)
    for m in range(P):
        if m % 32 < 16:
            rot[m + 16, m] = -1.0
        else:
            rot[m - 16, m] = 1.0
    strict = [(row < col), (row > col)]
    incl = [(row <= col), (row >= col)]
    c = {
        "mean1024": np.full((P, P), 1.0 / D), "mean64": same(64) / 64, "sum64": same(64),
        "mean256": np.full((P, P), 1.0 / 256), "ident": np.eye(P), "rot": rot,
        "inv": np.concatenate([same(16)] + [same(2 * n) - same(n) for n in (16, 32, 64)], 1),
    }
    for d in range(2):
        c[f"rw{d}"] = np.concatenate([strict[d], incl[d]] * 2, 1)
        c[f"nd{d}"] = strict[1 - d] * same(16)
        c[f"ssd{d}"] = np.where(incl[d], 0.0, NEG)
    key = np.arange(2 * P)[None, :]
    c["att"] = np.concatenate([np.where(np.abs(row + t * P - key) <= 128, 0.0, NEG) for t in range(2)], 1)
    tok = np.arange(2 * P)
    pos = np.stack([tok // 64, tok % 64]).astype(np.float32)
    freq = np.float32(10000.0) ** (-np.arange(16, dtype=np.float32) / np.float32(16))
    ang = np.stack([pos[(f % 64) // 32] * freq[f % 16] for f in range(P)]).astype(np.float32)
    c["cos"], c["sin"] = np.cos(ang), np.sin(ang)
    restart = np.ones((P, W), np.float32)
    restart[:, COL] = 0.0
    c["restart"] = restart
    c["rank16"] = np.broadcast_to(np.arange(16, 0, -1), (P, 16))
    c["eps"], c["eps_kk"], c["eps_gn"] = EPS, 1e-12, GN_EPS
    c["rank4"] = np.broadcast_to(np.arange(4, 0, -1), (P, 4))
    return c


def tokens(prompt, sample):
    import numpy as np
    out = np.zeros((P, KT, W), np.float32)
    out[:, :, 0:P] = prompt.T.reshape(KT, P, P).transpose(1, 0, 2)
    out[:, :, LAT:] = sample.T.reshape(KT, P, 2 * P).transpose(1, 0, 2)
    return out.reshape(P, KT * W)


def by_feature(v):
    return v.reshape(-1, P).T


def kernel(**inputs):
    import numpy as np
    import concourse.bacc as bacc
    from concourse.bass_utils import run_bass_kernel_spmd

    x = {k: np.asarray(v) for k, v in inputs.items()}

    def tiles_of(w):
        k, n = w.shape
        return w.reshape(k // P, P, n // P, P).transpose(2, 1, 0, 3).reshape(n // P, P, k)

    q_cols = np.concatenate([np.r_[64 * m:64 * m + 64, 64 * (m + 4):64 * (m + 4) + 64] for m in range(4)])
    in_cols = np.concatenate([q_cols, np.arange(512, 2432)])
    out_rows = np.concatenate([q_cols, np.arange(512, 1024)])
    weights = np.zeros((DEPTH * LAYER_ITEMS, P, ITEM), np.float32)
    n = 0
    for l in range(DEPTH):
        def put(t):
            nonlocal n
            t = t.reshape(-1, ITEM // t.shape[2], P, t.shape[2]).transpose(0, 2, 1, 3).reshape(-1, P, ITEM)
            weights[n:n + len(t)] = t
            n += len(t)
        put(tiles_of(x["w_mod"][l]))
        dt = np.zeros((KT, P, DT_ROWS), np.float32)
        for d in range(2):
            dt[:, :, 32 * d:32 * d + 4] = x["w_in"][l][:, 2432:2436].reshape(KT, P, 4)
        t = np.zeros((20, P, D), np.float32)
        t[:19] = tiles_of(x["w_in"][l][:, in_cols])
        t[19, :, :KT * DT_ROWS] = dt.transpose(1, 0, 2).reshape(P, -1)
        put(t)
        put(tiles_of(x["w_out"][l][out_rows]))
        for e in range(EXPERTS):
            put(tiles_of(x["exp_gate"][l, e]))
            put(tiles_of(x["exp_up"][l, e]))
            put(tiles_of(x["exp_down"][l, e]))
    assert n == len(weights)

    small = np.zeros((DEPTH, P, LAYER_N), np.float32)
    for l in range(DEPTH):
        def s(name, v, rows=slice(0, P)):
            lo, hi = LAYER_COLS[name]
            small[l][rows, lo:hi] = v
        s("n1", by_feature(x["norm1_w"][l]))
        s("n2", by_feature(x["norm2_w"][l]))
        s("bmod", by_feature(x["b_mod"][l]))
        s("qw", np.tile(x["q_norm_w"][l], 2)[:, None])
        s("kw", np.tile(x["k_norm_w"][l], 2)[:, None])
        s("sink", np.broadcast_to(x["attn_sink"][l], (P, 8)))
        s("mu0", by_feature(x["rw_mu"][l, 0]))
        s("mu1", by_feature(x["rw_mu"][l, 1]))
        s("w0", by_feature(x["rw_w0"][l].reshape(-1)))
        s("a0", by_feature(x["rw_a0"][l].reshape(-1)))
        s("kk", by_feature(x["rw_k_k"][l]))
        s("ka", by_feature(x["rw_k_a"][l]))
        s("rk", by_feature(x["rw_r_k"][l].reshape(-1)))
        s("lnw", by_feature(x["rw_ln_w"][l]))
        s("lnb", by_feature(x["rw_ln_b"][l]))
        s("cw", by_feature(x["ssd_conv_w"][l].reshape(-1)))
        s("cb", by_feature(x["ssd_conv_b"][l]))
        for d in range(2):
            r = slice(32 * d, 32 * d + 4)
            s("dtb", x["ssd_dt_bias"][l, d][:, None], r)
            s("alog", x["ssd_a_log"][l, d][:, None], r)
        s("dskip", by_feature(np.repeat(x["ssd_d"][l], 64)))
        s("nw", by_feature(x["ssd_norm_w"][l]))
        s("lora", x["rw_w_up"][l].transpose(1, 0, 2).reshape(32, 512), slice(0, 32))
        s("lora", x["rw_a_up"][l].transpose(1, 0, 2).reshape(32, 512), slice(32, 64))
        lo = LAYER_COLS["lora"][0]
        small[l][64:, lo:lo + 256] = x["rw_g_up"][l]
        s("kc", x["cache_k"][0, l].transpose(1, 2, 0).reshape(P, P))
        s("vc", x["cache_v"][0, l].reshape(P, P))
        s("srw", x["state_rwkv"][0, l].reshape(2, 2, 2, 64, 64).transpose(2, 4, 0, 1, 3).reshape(P, 256))
        s("sssd", x["state_ssd"][0, l].reshape(2, 2, 2, 64, 64).transpose(1, 4, 0, 2, 3).reshape(P, 256))

    consts = np.zeros((P, CONST_N), np.float32)
    table = constants()
    table["router"] = x["router_w"].reshape(KT, P, 16).transpose(1, 0, 2).reshape(P, P)
    table["rbias"] = np.broadcast_to(x["router_bias"], (P, 16))
    for name, (lo, hi) in CONST_COLS.items():
        consts[:, lo:hi] = table[name]
    cond = np.stack([by_feature(x["c_ctx"]), by_feature(x["c"][0])], 2).reshape(P, 16)

    nc = bacc.Bacc("TRN2", target_bir_lowering=False, num_devices=1)
    arrays = {"weights": weights, "small": small, "consts": consts, "cond": np.ascontiguousarray(cond),
              "x": tokens(x["x_prompt"][0], x["x_sample"][0])}
    shapes = {"y": (P, KT * W), "new_k": (DEPTH, P, P), "new_v": (DEPTH, P, P),
              "new_rw": (DEPTH, P, 256), "new_ssd": (DEPTH, P, 256)}
    f32 = mybir.dt.float32
    a = {k: nc.dram_tensor(k, v.shape, f32, kind="ExternalInput").ap() for k, v in arrays.items()}
    a.update({k: nc.dram_tensor(k, v, f32, kind="ExternalOutput").ap() for k, v in shapes.items()})
    program(nc, a)
    r = run_bass_kernel_spmd(nc, [arrays], core_ids=[0]).results[0]

    y = r["y"].reshape(P, KT, W).transpose(2, 1, 0).reshape(W, D)
    cache = lambda v: np.ascontiguousarray(v.transpose(0, 2, 1).reshape(1, DEPTH, P, 2, 64))
    rw = r["new_rw"].reshape(DEPTH, 2, 64, 2, 2, 64).transpose(0, 3, 4, 1, 5, 2).reshape(1, DEPTH, 2, 4, 64, 64)
    sd = r["new_ssd"].reshape(DEPTH, 2, 64, 2, 2, 64).transpose(0, 3, 1, 4, 5, 2).reshape(1, DEPTH, 2, 4, 64, 64)
    return (np.ascontiguousarray(y[None, 0:P]), np.ascontiguousarray(y[None, LAT:]), cache(r["new_k"]),
            cache(r["new_v"]), np.ascontiguousarray(rw), np.ascontiguousarray(sd))
```

```python
import concourse.bass as bass
from concourse import mybir
from contextlib import ExitStack

DEPTH = 2
P = 128
D = 1024
KT = D // P
TILES = 3
COL = [0, P + 1, 2 * P + 1]
W = 3 * P + 1
LAT = COL[1]
SEGMENTS = [(0, 0, P), (1, LAT, W)]
EPS = 1e-6
GN_EPS = 64e-5
DECAY = 0.606531
NEG = -1e30

UQ, UK, UV, UR, URK, URV, ULORA, UZ, UX, UB, UC, UDT = 0, 4, 5, 6, 8, 10, 12, 13, 15, 17, 18, 19
U_TILES = 20
DT_ROWS = 64
EXPERTS = 16
GROUPS = 4
EXPERT_ITEMS = 3
TOP_K = 2
SLOT = 96
BLOCKS = (TILES * P * TOP_K - EXPERTS) // SLOT + EXPERTS
ITEM = 2048
MOD_ITEMS, IN_ITEMS, OUT_ITEMS = 24, 10, 4
DENSE_ITEMS = MOD_ITEMS + IN_ITEMS + OUT_ITEMS
LAYER_ITEMS = DENSE_ITEMS + EXPERTS * EXPERT_ITEMS
SLOTS = 5

MOD_CHUNKS, EARLY_CHUNKS = 12, 4
MOD_PLACES = ["start", "qk", "sc0", "pv0", "pv1", "pv2", "inputs", "batches", "ssd", "ys", "router"]
MOD_AT = {(0, "start"): 4, (0, "qk"): 1, (0, "sc0"): 1, (0, "pv0"): 1, (0, "pv1"): 1, (0, "inputs"): 2,
          (0, "batches"): 3, (0, "ssd"): 1, (0, "ys"): 1, (0, "router"): 1,
          (1, "qk"): 1, (1, "sc0"): 1, (1, "inputs"): 2, (1, "batches"): 3, (1, "ssd"): 1}


def modulation_schedule():
    queue = [(l, c) for l in range(DEPTH) for c in range(MOD_CHUNKS)]
    out = {}
    for l in range(DEPTH):
        for place in MOD_PLACES:
            n = MOD_AT.get((l, place), 0)
            out[l, place], queue = queue[:n], queue[n:]
    assert not queue
    return out


MOD_SCHEDULE = modulation_schedule()

RW_BATCHES = [(0, 0), (0, 1), (1, 0), (2, 1), (2, 0), (1, 1)]
STATE_BATCHES = 4
RW_STEPS = ["matrices", "power1", "power2", "power3", "power4", "transpose", "cross0", "merge0", "cross1",
            "merge1", "cross2", "merge2", "rhs", "solve", "output", "factors", "state"]
RW_ORDER = [(step, b) for pair in ((0, 1), (2, 3), (4, 5)) for step in RW_STEPS for b in pair
            if b < STATE_BATCHES or step not in ("factors", "state")]
SSD_STATES = [(0, 0), (0, 1), (1, 0), (2, 1)]


ATT_STEPS = [("scores", 0), ("scores", 1), ("values", 0), ("scores", 2), ("values", 1), ("values", 2)]


def columns(names):
    at, out = 0, {}
    for name, n in names:
        out[name] = (at, at + n)
        at += n
    return out, at


LAYER_COLS, LAYER_N = columns([
    ("qw", 1), ("kw", 1), ("sink", 8), ("mu0", 7), ("mu1", 7),
    ("w0", 4), ("a0", 4), ("kk", 2), ("ka", 2), ("rk", 2), ("lnw", 2), ("lnb", 2), ("cw", 12), ("cb", 4),
    ("dtb", 1), ("alog", 1), ("dskip", 2), ("nw", 2), ("lora", 512), ("kc", 128), ("vc", 128),
    ("srw", 256), ("sssd", 256)])
CONST_COLS, CONST_N = columns([
    ("head", 128), ("ident", 128), ("rot", 128),
    ("inv", 512), ("rw0", 512), ("rw1", 512), ("nd0", 128), ("nd1", 128), ("ssd0", 128),
    ("ssd1", 128), ("cos", 256), ("sin", 256), ("restart", W), ("rank16", 16), ("rank4", 4),
    ("router", 128), ("rbias", 16), ("ones", 128), ("block", BLOCKS), ("bmod0", 48), ("bmod1", 48),
    ("n1_0", 8), ("n1_1", 8), ("n2_0", 8), ("n2_1", 8), ("eps", 1), ("eps_kk", 1), ("eps_gn", 1)])


def psum_plan():
    plan = []

    def g(consumer, *key):
        plan.append((key, consumer))

    def fill(l, place):
        for chunk in MOD_SCHEDULE[l, place]:
            g("a", "mod", *chunk)
            g("v", "modT", *chunk)

    for l in range(DEPTH):
        fill(l, "start")
        g("a", "ms", l, 1)
        for c in range(U_TILES):
            g("va"[c % 2], "u", l, c)
        for i in range(5):
            g("a", "qkms", l, i)
        g("a", "vt", l)
        fill(l, "qk")
        for i in range(5):
            g("v", "rope", l, i)
        for step, t in ATT_STEPS:
            if step == "scores":
                for h in range(8):
                    g("v", "sc", l, t, h)
                if t == 0:
                    fill(l, "sc0")
            else:
                for h in range(8):
                    g("a", "pT", l, t, h)
                g("a", "pv", l, t)
                fill(l, f"pv{t}")
        fill(l, "inputs")
        for d in range(2):
            for i in range(2):
                g("a", "wl", l, d, i)
        for d in range(2):
            for i in range(2):
                g("a", "al", l, d, i)
        for i in range(2):
            g("a", "gg", l, i)
        for i in range(2):
            g("a", "kkn", l, i)
        for i in range(2):
            g("v", "bon", l, i)
        for i in range(2):
            g("a", "rvt", l, i)
        fill(l, "batches")
        for step, b in RW_ORDER:
            kind, k = step[:5], step[-1]
            if kind == "matri":
                for j in range(4):
                    g("v", "g4", l, b, j)
                for half in range(2):
                    g("v", "nd", l, b, half)
            elif kind == "power":
                if k != "1":
                    g("v", "t", l, b, int(k))
                if k != "4":
                    g("a", "p", l, b, int(k))
                    g("a", "pt", l, b, int(k))
            elif kind == "trans":
                g("a", "tT", l, b)
            elif kind == "cross":
                g("v", "cross", l, b, int(k))
            elif kind == "merge":
                if k != "2":
                    g("v", "t", l, b, 5 + int(k))
                g("v", "tt", l, b, int(k))
            elif kind == "rhs":
                g("a", "rhs", l, b)
            elif kind == "solve":
                g("v", "x", l, b)
            elif kind == "outpu":
                g("v", "y", l, b)
            elif kind == "facto":
                g("a", "kbt", l, b)
            elif kind == "state":
                g("v", "st", l, b)
        for i in range(2):
            g("v", "gnm", l, i)
        for i in range(2):
            g("a", "gnv", l, i)
        fill(l, "ssd")
        g("a", "dtt", l)
        for r in range(8):
            g("a", "cs", l, r)
        for t in range(TILES):
            g("a", "xt", l, t)
            for grp in range(2):
                g("v", "gt", l, t, grp)
        for s in range(4):
            g("v", "hst", l, s)
        fill(l, "ys")
        for t in range(TILES):
            for grp in range(2):
                g("v", "ys", l, t, grp)
        g("a", "yms", l)
        for n in range(KT):
            g("v", "out", l, n)
        g("a", "ms", l, 2)
        g("a", "lg", l)
        for t in range(TILES):
            for k in range(2):
                g("a", "hm", l, t, k)
        fill(l, "router")
        g("v", "pos", l)
        for k in range(2):
            g("a", "xb", l, 0, k)
        for b in range(BLOCKS):
            g("a", "gate", l, b)
            g("v", "up", l, b)
            if b + 1 < BLOCKS:
                for k in range(2):
                    g("a", "xb", l, b + 1, k)
            g("a", "down", l, b, 0)
            g("v", "down", l, b, 1)
        for t in range(TILES):
            for k in range(2):
                g("v", "yt", l, t, k)
    return plan


def weight_stream(plan):
    out = []
    for key, _ in plan:
        kind, l, rest = key[0], key[1], key[2:]
        if kind == "mod":
            out += [(("fixed", l, 2 * rest[0] + i), key) for i in range(2)]
        elif kind == "u" and rest[0] % 2 == 0:
            out.append((("fixed", l, MOD_ITEMS + rest[0] // 2), ("u", l, rest[0] + 1)))
        elif kind == "out" and rest[0] % 2 == 0:
            out.append((("fixed", l, MOD_ITEMS + IN_ITEMS + rest[0] // 2), ("out", l, rest[0] + 1)))
        elif kind == "gate":
            out.append((("expert", l, rest[0], 0), key))
        elif kind == "up":
            out.append((("expert", l, rest[0], 1), key))
        elif kind == "down" and rest[1] == 0:
            out.append((("expert", l, rest[0], 2), ("down", l, rest[0], 1)))
    return out


BLOCKS_OF = [(BLOCKS + 1) // 2, BLOCKS // 2]


def program(nc, a):
    fp32 = mybir.dt.float32
    ALU = mybir.AluOpType
    ACT = mybir.ActivationFunctionType
    X = mybir.AxisListType.X

    ctx = ExitStack()
    with ctx:
        def sb(name, n):
            return ctx.enter_context(nc.sbuf_tensor("sb_" + name, [P, n], fp32))

        def sem(name):
            return ctx.enter_context(nc.semaphore(name))

        def shaped(ap, *dims):
            names = [f"d{i}" for i in range(len(dims))]
            sizes = {k: v for k, v in zip(names[1:], dims[1:])}
            return ap.rearrange(f"p ({' '.join(names)}) -> p {' '.join(names)}", **sizes)

        ring = sb("ring", SLOTS * ITEM)
        xT = shaped(sb("xT", KT * W)[:, :], KT, W)
        hT_flat = sb("hT", KT * W)[:, :]
        hT = shaped(hT_flat, KT, W)
        u_flat = sb("u", U_TILES * (W + 2))[:, :]
        u = shaped(u_flat, U_TILES, W + 2)
        sq_flat = sb("sq", KT * W)[:, :]
        sq = shaped(sq_flat, KT, W)
        o = shaped(sb("o", KT * W)[:, :], KT, W)
        small = sb("small", LAYER_N)
        consts = sb("consts", CONST_N)
        cond = sb("cond", 16)
        scond = sb("scond", 16)
        mod = shaped(sb("mod", 96)[:, :], 48, 2)
        scale1 = shaped(sb("scale1", 16)[:, :], 8, 2)
        scale2 = shaped(sb("scale2", 16)[:, :], 8, 2)
        tmp = sb("tmp", 2 * W)
        mod_rows = [sb(f"mod_rows{i}", 512) for i in range(2)]
        cols = sb("cols", 32)
        AREN = 13776
        arena = sb("arena", AREN)
        state_rw = [shaped(sb(f"state_rw{l}", 256)[:, :], 4, 64) for l in range(DEPTH)]
        state_ssd = [shaped(sb(f"state_ssd{l}", 256)[:, :], 4, 64) for l in range(DEPTH)]
        new_k = [sb(f"new_k{l}", P) for l in range(DEPTH)]
        new_v = [sb(f"new_v{l}", P) for l in range(DEPTH)]

        rows = ctx.enter_context(nc.sbuf_tensor("sb_rows", [P, 2 * TILES], mybir.dt.uint32))
        block_expert = ctx.enter_context(nc.sbuf_tensor("sb_block_expert", [P, BLOCKS + 1], mybir.dt.int32))
        x_slots = nc.dram_tensor("x_slots", (BLOCKS * SLOT, D), fp32, kind="Internal").ap()
        y_slots = nc.dram_tensor("y_slots", (BLOCKS * SLOT, D), fp32, kind="Internal").ap()

        banks = [ctx.enter_context(nc.psum_tensor(f"bank{i}", [P, 512], fp32)) for i in range(8)]

        def carve(base, *dims):
            n = 1
            for x in dims:
                n *= x
            assert base[1] + n <= base[2], (base, dims)
            ap = base[0][:, base[1]:base[1] + n]
            base[1] += n
            return shaped(ap, *dims) if len(dims) > 1 else ap

        at = [arena, 0, AREN]
        qn = carve(at, 5, W)
        scores = [carve(at, 8, 3 * P) for _ in range(2)]
        probsT = carve(at, 8, 3 * P)
        v_tm = carve(at, TILES, P)
        att_cols = carve(at, 3 * 64)
        rw = [arena, 0, AREN]
        mixed = carve(rw, 7, W)
        kdir = carve(rw, 2, W)
        gate_rw = carve(rw, 2, W)
        bonus = carve(rw, 2, W)
        y_rw = carve(rw, 2, W)
        rv_tm = carve(rw, 2, TILES, P)
        S_til = carve(rw, 4, 64)
        S_diag = carve(rw, 4, 2, 64)
        S_lat = carve(rw, 4, 64)
        decay_half = carve(rw, 4, TILES)
        half_total = carve(rw, 4, TILES)
        reuse = rw[1]
        sgw = carve(rw, 4, W)
        asig = carve(rw, 4, W)
        csum = carve(rw, 4, W)
        rw2 = [arena, reuse, AREN]
        tail = [u_flat, 0, 13 * (W + 2)]
        g4 = [carve(rw2, 4, 4, P) for _ in range(2)]
        r_rhs = [carve(rw2, 4, 64) for _ in range(2)]
        x_sol = [carve(rw2, 4, 64) for _ in range(2)]
        pw = [carve(tail, 4, P) for _ in range(2)]
        pwT = [carve(tail, 4, P) for _ in range(2)]
        inv = [carve(tail, 4, P) for _ in range(2)]
        invT = [carve(tail, 4, P) for _ in range(2)]
        cross = [carve(tail, 4, P), carve(rw2, 4, P)]
        kb_tm = cross
        ar = shaped(hT_flat, 2, 2, 2, W)
        kb = shaped(sq_flat, 2, 2, 2, W)
        ss = [arena, 0, AREN]
        le = carve(ss, 8, W)
        ce = carve(ss, 8, 2 * P)
        x_tm = carve(ss, TILES, 3 * P)
        xdt = carve(ss, TILES, 2, 4, 64)
        xdd = carve(ss, 4, 4, 64)
        dtc = carve(ss, TILES, 2, DT_ROWS)
        total_b = carve(ss, 8, TILES)
        decay_in = carve(ss, TILES, 8)
        chunk_decay = carve(ss, 8, TILES)
        dt_t = carve(ss, W)
        dta = carve(ss, W)
        cs = carve(ss, W)
        dtmp = carve(ss, W)
        y_ssd = carve(ss, 2, W)
        neg_a = carve(ss, 4)
        h_mid = carve(ss, 4, 64)
        mo = [arena, 0, AREN]
        rt = carve(mo, 24, 48)
        cmp = carve(mo, BLOCKS, EXPERTS)
        w12 = carve(mo, 2, TILES)
        sg = carve(mo, 2 * SLOT)
        hid = [carve(mo, 2, SLOT) for _ in range(2)]
        xb = [carve(mo, D) for _ in range(2)]
        xbT = [carve(mo, KT, SLOT) for _ in range(2)]
        ye = [carve(mo, D) for _ in range(2)]
        h_tm = carve(mo, TILES, D)
        mo2 = [u_flat, 0, U_TILES * (W + 2)]
        y1 = carve(mo2, TILES, D)
        y2 = carve(mo2, TILES, D)

        def C(name, rows=slice(0, P)):
            lo, hi = CONST_COLS[name]
            return consts[rows, lo:hi]

        def Lp(name, rows=slice(0, P)):
            lo, hi = LAYER_COLS[name]
            return small[rows, lo:hi]

        def Lc(name, i, rows=slice(0, P)):
            lo = LAYER_COLS[name][0]
            return small[rows, lo + i:lo + i + 1]

        def bc(ap, dim, n):
            ap = ap.unsqueeze(dim)
            shape = list(ap.shape)
            shape[dim] = n
            return ap.broadcast_to(shape)

        plan = psum_plan()
        stream = weight_stream(plan)
        index = {key: n for n, (key, _) in enumerate(plan)}
        read_no = {}
        count = {"a": 0, "v": 0}
        for key, consumer in plan:
            count[consumer] += 1
            read_no[key] = count[consumer]
        psum_filled = sem("psum_filled")
        psum_read = {"a": sem("psum_read_by_scalar"), "v": sem("psum_read_by_vector")}
        opened = [0]
        released = {"a": 0, "v": 0}

        def open_bank(pe, *key):
            n = index[key]
            assert n == opened[0], (key, plan[opened[0]])
            opened[0] += 1
            if n >= 8:
                old, consumer = plan[n - 8]
                pe.wait_ge(psum_read[consumer], read_no[old])
            return banks[n % 8]

        def filled(eng, *key):
            eng.wait_ge(psum_filled, index[key] + 1)
            return banks[index[key] % 8]

        def read(*key):
            consumer = plan[index[key]][1]
            released[consumer] += 1
            assert read_no[key] == released[consumer], key
            return psum_read[consumer]

        def taken(eng, *key):
            eng.wait_ge(psum_read[plan[index[key]][1]], read_no[key])

        def blocks_used(eng, l):
            eng.wait_ge(blocks_ready, l + 1)
            return eng.value_load(block_expert[0:1, BLOCKS:BLOCKS + 1], min_val=0, max_val=BLOCKS)

        def on_both_ways(eng, used, b, counters, body):
            if b < EXPERTS:
                body(b, True)
                return
            before = [(c, dict(c) if isinstance(c, dict) else list(c)) for c in counters]
            with eng.If(used > b):
                body(b, True)
            for c, old in before:
                if isinstance(c, dict):
                    c.update(old)
                else:
                    c[:] = old
            with eng.Else():
                body(b, False)

        item_ready = [sem(f"weights_ready{i}") for i in range(SLOTS)]
        consts_loaded = sem("consts_loaded")
        small_loaded = sem("small_loaded")
        out_written = sem("out_written")
        gaps_cleared = sem("gaps_cleared")
        cond_ready = sem("cond_ready")
        xsq_ready = sem("xsq_ready")
        h_ready = sem("h_ready")
        qk_sq_ready = sem("qk_sq_ready")
        qn_ready = sem("qn_ready")
        rope_ready = sem("rope_ready")
        shifted_ready = sem("shifted_ready")
        exps_ready = sem("exps_ready")
        probs_ready = sem("probs_ready")
        kv_copied = sem("kv_copied")
        mixed_ready = sem("mixed_ready")
        lora_ready = sem("lora_ready")
        kk_sq_ready = sem("kk_sq_ready")
        bonus_in_ready = sem("bonus_in_ready")
        decay_arg_ready = sem("decay_arg_ready")
        decay_exp_ready = sem("decay_exp_ready")
        factors_ready = sem("factors_ready")
        state_ready = sem("state_ready")
        matrices_ready = sem("matrices_ready")
        gn_in_ready = sem("gn_in_ready")
        gn_sq_ready = sem("gn_sq_ready")
        rwkv_done = sem("rwkv_done")
        conv_ready = sem("conv_ready")
        silu_ready = sem("silu_ready")
        dt_parts = sem("dt_parts")
        dt_ready = sem("dt_ready")
        cs_ready = sem("cs_ready")
        lat_decay_ready = sem("lat_decay_ready")
        le_arg_ready = sem("le_arg_ready")
        din_arg_ready = sem("din_arg_ready")
        le_ready = sem("le_ready")
        din_ready = sem("din_ready")
        xdd_ready = sem("xdd_ready")
        gated_sq_ready = sem("gated_sq_ready")
        z_ready = sem("z_ready")
        mix_ready = sem("mix_ready")
        zeros_set = sem("zeros_set")
        slots_cleared = sem("slots_cleared")
        assigned_ready = sem("assigned_ready")
        rows_ready = sem("rows_ready")
        blocks_ready = sem("blocks_ready")
        scattered = sem("scattered")
        xb_loaded = [sem(f"xb_loaded{i}") for i in range(2)]
        y_written = [sem(f"y_written{i}") for i in range(2)]
        y_gathered = [sem(f"y_gathered{t}") for t in range(TILES)]
        y_summed = sem("y_summed")
        chain_v = sem("vector_chain")
        chain_a = sem("scalar_chain")

        block = ctx.enter_context(nc.Block())

        @block.sync
        def _(sp):
            sp.dma_start(consts[:, :], a["consts"][:, :]).then_inc(consts_loaded, 16)
            sp.dma_start(cond[:, :], a["cond"][:, :]).then_inc(consts_loaded, 16)
            sp.dma_start(small[:, :], a["small"][0]).then_inc(small_loaded, 16)

            def load_block(l, b, first_item, used):
                expert = [None]

                def body(b, run):
                    if run:
                        expert[0] = sp.value_load(block_expert[0:1, b:b + 1], min_val=0, max_val=EXPERTS - 1)
                    for j in range(EXPERT_ITEMS):
                        n = first_item + j
                        slot = ring[:, (n % SLOTS) * ITEM:(n % SLOTS + 1) * ITEM]
                        filled(sp, *stream[n - SLOTS][1])
                        if run:
                            first = expert[0] * EXPERT_ITEMS + (l * LAYER_ITEMS + DENSE_ITEMS + j)
                            source = a["weights"][bass.ds(first, 1)].rearrange("a p n -> (a p) n")
                        else:
                            slot, source = slot[0:1, 0:P], a["weights"][0, 0:1, 0:P]
                        sp.dma_start(slot, source).then_inc(item_ready[n % SLOTS], 16)
                        if j == 1:
                            if b == 0:
                                sp.wait_ge(scattered, 6 * 16 * (l + 1))
                            if b >= 2:
                                filled(sp, "xb", l, b - 2, 1)
                            rows_, cols_ = (SLOT, D) if run else (1, P)
                            sp.dma_start(xb[b % 2][0:rows_, 0:cols_],
                                         x_slots[b * SLOT:b * SLOT + rows_, 0:cols_]).then_inc(xb_loaded[b % 2], 16)

                on_both_ways(sp, used, b, [], body)

            for n, (where, _) in enumerate(stream):
                kind, l = where[:2]
                if n == 4:
                    sp.dma_start(xT, shaped(a["x"][:, :], KT, W)).then_inc(consts_loaded, 16)
                if kind == "expert":
                    b, j = where[2:]
                    if j:
                        continue
                    if b == 0:
                        used = blocks_used(sp, l)
                    if b == BLOCKS // 2 and l < DEPTH - 1:
                        sp.wait_ge(mix_ready, l + 1)
                        sp.dma_start(small[:, :], a["small"][l + 1]).then_inc(small_loaded, 16)
                    load_block(l, b, n, used)
                else:
                    if n >= SLOTS:
                        filled(sp, *stream[n - SLOTS][1])
                    sp.dma_start(ring[:, (n % SLOTS) * ITEM:(n % SLOTS + 1) * ITEM],
                                 a["weights"][l * LAYER_ITEMS + where[2]]).then_inc(item_ready[n % SLOTS], 16)

        @block.gpsimd
        def _(pool):
            pool.wait_ge(zeros_set, 1)
            filled(pool, "ms", 0, 1)
            pool.dma_start(x_slots.rearrange("(b p) c -> p b c", p=SLOT),
                           bc(ye[0][0:SLOT, :], 1, BLOCKS)).then_inc(slots_cleared, 16)
            pool.dma_start(y_slots[EXPERTS * SLOT:, :].rearrange("(b p) c -> p b c", p=SLOT),
                           bc(ye[0][0:SLOT, :], 1, BLOCKS - EXPERTS)).then_inc(slots_cleared, 16)
            for l in range(DEPTH):
                pool.wait_ge(kv_copied, 2 * (l + 1))
                pool.dma_start(a["new_k"][l], new_k[l][:, :]).then_inc(out_written, 16)
                pool.dma_start(a["new_v"][l], new_v[l][:, :]).then_inc(out_written, 16)
                taken(pool, "st", l, 1)
                pool.dma_start(shaped(a["new_rw"][l], 4, 64), state_rw[l]).then_inc(out_written, 16)
                taken(pool, "hst", l, 1)
                pool.dma_start(shaped(a["new_ssd"][l], 4, 64), state_ssd[l]).then_inc(out_written, 16)
                pool.wait_ge(slots_cleared, 32)
                pool.wait_ge(rows_ready, l + 1)
                taken(pool, "hm", l, TILES - 1, 1)
                for k in range(2):
                    for t in range(TILES):
                        c = k * TILES + t
                        pool.indirect_dma_start(x_slots, bass.IndirectOffsetOnAxis(rows[:, c:c + 1], 0),
                                                h_tm[:, t, :], None).then_inc(scattered, 16)
                used = blocks_used(pool, l)

                def store_block(b, run):
                    taken(pool, "down", l, b, 0)
                    taken(pool, "down", l, b, 1)
                    rows_, cols_ = (SLOT, D) if run else (1, P)
                    pool.dma_start(y_slots[b * SLOT:b * SLOT + rows_, 0:cols_], ye[b % 2][0:rows_, 0:cols_])\
                        .then_inc(y_written[b % 2], 16)

                for b in range(BLOCKS):
                    on_both_ways(pool, used, b, [], store_block)
                for i in range(2):
                    pool.wait_ge(y_written[i], 16 * (l * BLOCKS_OF[i] + BLOCKS_OF[i]))
                for t in range(TILES):
                    for k, y in enumerate((y1, y2)):
                        c = k * TILES + t
                        pool.indirect_dma_start(y[:, t, :], None, y_slots,
                                                bass.IndirectOffsetOnAxis(rows[:, c:c + 1], 0))\
                            .then_inc(y_gathered[t], 16)
            taken(pool, "yt", DEPTH - 1, TILES - 1, 1)
            pool.dma_start(shaped(a["y"][:, :], KT, W), xT).then_inc(out_written, 16)
            pool.wait_ge(out_written, 16 * (4 * DEPTH + 1))

        @block.tensor
        def _(pe):
            items = [0]

            def next_item():
                n = items[0]
                pe.wait_ge(item_ready[n % SLOTS], 16 * (n // SLOTS + 1))
                items[0] += 1
                return ring[:, (n % SLOTS) * ITEM:(n % SLOTS + 1) * ITEM]

            def mm(out, lhsT, rhs, start=True, stop=True):
                return nc.tensor.matmul(out, lhsT, rhs, start=start, stop=stop, skip_group_check=True)

            def tr(out, in_, n=P):
                return nc.tensor.transpose(out, in_, C("ident")[0:n, 0:n])

            def mean_square(l, which):
                bank = open_bank(pe, "ms", l, which)
                pe.wait_ge(xsq_ready, 2 * l + which)
                for k in range(KT):
                    last = mm(bank[:, 0:W], C("ones"), sq[:, k, :], k == 0, k == KT - 1)
                last.then_inc(psum_filled, 1)

            def project(item, off, src, kts, out, m=P):
                for k in range(kts):
                    last = mm(out, item[:, off + k * m:off + (k + 1) * m], src[:, k, :], k == 0, k == kts - 1)
                return last

            def fill(l, place):
                cv = shaped(scond[:, :], KT, 2)
                for ml, c in MOD_SCHEDULE[l, place]:
                    if (ml, c) == (0, 0):
                        pe.wait_ge(cond_ready, 1)
                    bank = open_bank(pe, "mod", ml, c)
                    for i in range(2):
                        item = shaped(next_item(), 4, 512)
                        for k in range(4):
                            last = mm(bank[0:2, :], cv[:, 4 * i + k, :], item[:, k, :], i + k == 0, i + k == 4)
                    last.then_inc(psum_filled, 1)
                    bank = open_bank(pe, "modT", ml, c)
                    taken(pe, "mod", ml, c)
                    for i in range(4):
                        last = tr(bank[:, 2 * i:2 * i + 2], mod_rows[c % 2][0:2, i * P:(i + 1) * P], 2)
                    last.then_inc(psum_filled, 1)

            def in_projection(l):
                pe.wait_ge(h_ready, 4 * l + 2)
                for c in range(U_TILES):
                    if c % 2 == 0:
                        item = next_item()
                    bank = open_bank(pe, "u", l, c)
                    m = DT_ROWS if c == UDT else P
                    project(item, (c % 2) * KT * P, hT, KT, bank[0:m, 0:W], m).then_inc(psum_filled, 1)

            def attention(l):
                for i in range(5):
                    bank = open_bank(pe, "qkms", l, i)
                    pe.wait_ge(qk_sq_ready, l + 1)
                    mm(bank[:, 0:W], C("head"), sq[:, i, :]).then_inc(psum_filled, 1)
                bank = open_bank(pe, "vt", l)
                taken(pe, "u", l, UV)
                for t in range(TILES):
                    last = tr(bank[:, t * P:(t + 1) * P], u[:, UV, 1 + COL[t]:1 + COL[t] + P])
                last.then_inc(psum_filled, 1)
                fill(l, "qk")
                for i in range(5):
                    bank = open_bank(pe, "rope", l, i)
                    pe.wait_ge(qn_ready, 5 * l + i + 1)
                    mm(bank[:, 0:2 * P], C("rot"), qn[:, i, LAT:W]).then_inc(psum_filled, 1)
                def att_scores(t):
                    c0 = COL[t]
                    for h in range(8):
                        m, p = h % 4, 64 * (h // 4)
                        bank = open_bank(pe, "sc", l, t, h)
                        if t == 0 and h == 0:
                            pe.wait_ge(rope_ready, l + 1)
                        q = qn[p:p + 64, m, c0:c0 + P]
                        if t == 0:
                            last = mm(bank[:, 0:P], q, qn[p:p + 64, 4, 0:P])
                        else:
                            mm(bank[:, 0:2 * P], q, qn[p:p + 64, 4, LAT:W])
                            last = mm(bank[:, 2 * P:3 * P], q, Lp("kc", slice(p, p + 64)))
                        last.then_inc(psum_filled, 1)

                def att_values(t):
                    blocks = 1 if t == 0 else 3
                    for h in range(8):
                        bank = open_bank(pe, "pT", l, t, h)
                        if h == 0:
                            pe.wait_ge(probs_ready, TILES * l + t + 1)
                        for b in range(blocks):
                            last = tr(bank[:, b * P:(b + 1) * P], scores[t % 2][:, h, b * P:(b + 1) * P])
                        last.then_inc(psum_filled, 1)
                    bank = open_bank(pe, "pv", l, t)
                    taken(pe, "pT", l, t, 7)
                    for h in range(8):
                        m, p = h % 4, 64 * (h // 4)
                        for b in range(blocks):
                            if t == 0:
                                v = v_tm[:, 0, p:p + 64]
                            elif b < 2:
                                v = v_tm[:, 1 + b, p:p + 64]
                            else:
                                v = Lp("vc")[:, p:p + 64]
                            last = mm(bank[p:p + 64, m * P:(m + 1) * P], v, probsT[:, h, b * P:(b + 1) * P],
                                      b == 0, b == blocks - 1)
                    last.then_inc(psum_filled, 1)

                for step, t in ATT_STEPS:
                    if step == "scores":
                        att_scores(t)
                        if t == 0:
                            fill(l, "sc0")
                    else:
                        att_values(t)
                        fill(l, f"pv{t}")

            def rwkv_inputs(l):
                for name, r0, r1 in (("wl", 0, 32), ("al", 32, 64)):
                    for d in range(2):
                        for i in range(2):
                            bank = open_bank(pe, name, l, d, i)
                            pe.wait_ge(lora_ready, l + 1)
                            c = d * 256 + i * P
                            mm(bank[:, 0:W], Lp("lora", slice(r0, r1))[:, c:c + P], mixed[r0:r1, 6, :])\
                                .then_inc(psum_filled, 1)
                for i in range(2):
                    bank = open_bank(pe, "gg", l, i)
                    mm(bank[:, 0:W], Lp("lora", slice(64, P))[:, i * P:(i + 1) * P], mixed[64:P, 6, :])\
                        .then_inc(psum_filled, 1)
                for i in range(2):
                    bank = open_bank(pe, "kkn", l, i)
                    pe.wait_ge(kk_sq_ready, l + 1)
                    mm(bank[:, 0:W], C("head"), sq[:, i, :]).then_inc(psum_filled, 1)
                for i in range(2):
                    bank = open_bank(pe, "bon", l, i)
                    pe.wait_ge(bonus_in_ready, l + 1)
                    mm(bank[:, 0:W], C("head"), sq[:, 2 + i, :]).then_inc(psum_filled, 1)
                for i in range(2):
                    bank = open_bank(pe, "rvt", l, i)
                    for t in range(TILES):
                        last = tr(bank[:, t * P:(t + 1) * P], mixed[:, 4 + i, COL[t]:COL[t] + P])
                    last.then_inc(psum_filled, 1)

            def four(bank, lhsT, rhs):
                for j in range(4):
                    last = mm(bank[:, j * P:(j + 1) * P], lhsT[:, j, :], rhs[:, j, :])
                last.then_inc(psum_filled, 1)

            def rwkv_step(l, step, b):
                t, d = RW_BATCHES[b]
                c0, c1 = COL[t], COL[t] + P
                s = b % 2
                kind, k = step[:5], step[-1]
                if step == "matrices":
                    if b == 0:
                        pe.wait_ge(factors_ready, l + 1)
                    for j in range(4):
                        i, p = j // 2, 64 * (j % 2)
                        bank = open_bank(pe, "g4", l, b, j)
                        both = ar[p:p + 64, d, i, :, c0:c1]
                        mm(bank[:, 0:2 * P], kb[p:p + 64, 0, d, i, c0:c1], both)
                        mm(bank[:, 2 * P:4 * P], kb[p:p + 64, 1, d, i, c0:c1], both).then_inc(psum_filled, 1)
                    for half in range(2):
                        bank = open_bank(pe, "nd", l, b, half)
                        p = 64 * half
                        for i in range(2):
                            last = mm(bank[:, i * P:(i + 1) * P], ar[p:p + 64, d, i, 0, c0:c1],
                                      kb[p:p + 64, 1, d, i, c0:c1])
                        last.then_inc(psum_filled, 1)
                elif kind == "power":
                    k = int(k)
                    if k == 1:
                        pe.wait_ge(matrices_ready, len(RW_BATCHES) * l + b + 1)
                    else:
                        bank = open_bank(pe, "t", l, b, k)
                        taken(pe, "pt", l, b, k - 1)
                        if k > 2:
                            taken(pe, "t", l, b, k - 1)
                        four(bank, pwT[s], inv[s])
                    if k < 4:
                        four(open_bank(pe, "p", l, b, k), pwT[s], pw[s])
                        four(open_bank(pe, "pt", l, b, k), pw[s], pwT[s])
                elif step == "transpose":
                    bank = open_bank(pe, "tT", l, b)
                    taken(pe, "t", l, b, 4)
                    for j in range(4):
                        last = tr(bank[:, j * P:(j + 1) * P], inv[s][:, j, :])
                    last.then_inc(psum_filled, 1)
                elif kind == "cross":
                    bank = open_bank(pe, "cross", l, b, int(k))
                    if k != "0":
                        taken(pe, "t", l, b, 4 + int(k))
                    four(bank, g4[s][:, :, 2, :], inv[s])
                elif kind == "merge":
                    k = int(k)
                    if k < 2:
                        bank = open_bank(pe, "t", l, b, 5 + k)
                        taken(pe, "cross", l, b, k)
                        if k:
                            taken(pe, "tt", l, b, k - 1)
                        else:
                            taken(pe, "tT", l, b)
                        four(bank, invT[s], cross[s])
                    bank = open_bank(pe, "tt", l, b, k)
                    taken(pe, "cross", l, b, k)
                    if k:
                        taken(pe, "tt", l, b, k - 1)
                    four(bank, cross[s], invT[s])
                elif step == "rhs":
                    bank = open_bank(pe, "rhs", l, b)
                    if t > 0:
                        pe.wait_ge(state_ready, 4 * l + b - 1)
                    for i in range(2):
                        if t > 0:
                            mm(bank[:, i * P:(i + 1) * P], ar[:, d, i, 0, c0:c1], S_diag[:, 2 * d + i, :, :],
                               True, False)
                        for j in (2 * i, 2 * i + 1):
                            p = 64 * (j % 2)
                            last = mm(bank[:, j * 64:(j + 1) * 64], g4[s][:, j, 0, :],
                                      rv_tm[:, i, t, p:p + 64], t == 0, True)
                    last.then_inc(psum_filled, 1)
                elif step == "solve":
                    bank = open_bank(pe, "x", l, b)
                    taken(pe, "rhs", l, b)
                    taken(pe, "tt", l, b, 2)
                    for j in range(4):
                        last = mm(bank[:, j * 64:(j + 1) * 64], invT[s][:, j, :], r_rhs[s][:, j, :])
                    last.then_inc(psum_filled, 1)
                elif step == "output":
                    bank = open_bank(pe, "y", l, b)
                    taken(pe, "x", l, b)
                    for i in range(2):
                        if t > 0:
                            mm(bank[:, i * P:(i + 1) * P], S_diag[:, 2 * d + i, :, :], ar[:, d, i, 1, c0:c1],
                               True, False)
                        for j in (2 * i, 2 * i + 1):
                            p = 64 * (j % 2)
                            out = bank[p:p + 64, i * P:(i + 1) * P]
                            mm(out, rv_tm[:, i, t, p:p + 64], g4[s][:, j, 1, :], t == 0, False)
                            last = mm(out, x_sol[s][:, j, :], g4[s][:, j, 3, :], False, True)
                    last.then_inc(psum_filled, 1)
                elif step == "factors":
                    bank = open_bank(pe, "kbt", l, b)
                    for i in range(2):
                        tr(bank[:, (2 * i) * P:(2 * i + 1) * P], kb[:, 0, d, i, c0:c1])
                        last = tr(bank[:, (2 * i + 1) * P:(2 * i + 2) * P], kb[:, 1, d, i, c0:c1])
                    last.then_inc(psum_filled, 1)
                elif step == "state":
                    bank = open_bank(pe, "st", l, b)
                    taken(pe, "kbt", l, b)
                    for j in range(4):
                        i, p = j // 2, 64 * (j % 2)
                        out = bank[p:p + 64, i * 64:(i + 1) * 64]
                        mm(out, kb_tm[s][:, 2 * i, p:p + 64], rv_tm[:, i, t, p:p + 64], True, False)
                        last = mm(out, kb_tm[s][:, 2 * i + 1, p:p + 64], x_sol[s][:, j, :], False, True)
                    last.then_inc(psum_filled, 1)

            def rwkv_norm(l):
                for i in range(2):
                    bank = open_bank(pe, "gnm", l, i)
                    pe.wait_ge(gn_in_ready, l + 1)
                    mm(bank[:, 0:W], C("head"), y_rw[:, i, :]).then_inc(psum_filled, 1)
                for i in range(2):
                    bank = open_bank(pe, "gnv", l, i)
                    pe.wait_ge(gn_sq_ready, l + 1)
                    mm(bank[:, 0:W], C("head"), sq[:, i, :]).then_inc(psum_filled, 1)

            def ssd(l):
                fill(l, "ssd")
                bank = open_bank(pe, "dtt", l)
                pe.wait_ge(cs_ready, l + 1)
                for t in range(TILES):
                    for k, src in ((0, dt_t), (1, cs)):
                        c = (2 * t + k) * DT_ROWS
                        last = tr(bank[:, c:c + DT_ROWS], src[0:DT_ROWS, COL[t]:COL[t] + P], DT_ROWS)
                last.then_inc(psum_filled, 1)
                for r in range(8):
                    bank = open_bank(pe, "cs", l, r)
                    row = 32 * (r // 4) + r % 4
                    pick = C("ident")[0:DT_ROWS, row:row + 1].broadcast_to([DT_ROWS, P])
                    mm(bank[:, 0:W], pick, cs[0:DT_ROWS, :]).then_inc(psum_filled, 1)
                for t in range(TILES):
                    bank = open_bank(pe, "xt", l, t)
                    pe.wait_ge(silu_ready, l + 1)
                    for i in range(3):
                        last = tr(bank[:, i * P:(i + 1) * P], u[:, UX + i, 1 + COL[t]:1 + COL[t] + P])
                    last.then_inc(psum_filled, 1)
                    for g in range(2):
                        bank = open_bank(pe, "gt", l, t, g)
                        p = 64 * g
                        mm(bank[:, 0:P], u[p:p + 64, UB, 1 + COL[t]:1 + COL[t] + P],
                           u[p:p + 64, UC, 1 + COL[t]:1 + COL[t] + P]).then_inc(psum_filled, 1)
                for s, (t, d) in enumerate(SSD_STATES):
                    bank = open_bank(pe, "hst", l, s)
                    pe.wait_ge(xdd_ready, l + 1)
                    for g in range(2):
                        p = 64 * g
                        last = mm(bank[p:p + 64, 0:P], x_tm[:, t, 2 * P + p:2 * P + p + 64],
                                  xdd[:, s, 2 * g:2 * g + 2, :])
                    last.then_inc(psum_filled, 1)
                fill(l, "ys")
                for t in range(TILES):
                    c0, c1 = COL[t], COL[t] + P
                    if t == 0:
                        taken(pe, "gt", l, 2, 1)
                    if t == 1:
                        taken(pe, "hst", l, 3)
                    for g in range(2):
                        bank = open_bank(pe, "ys", l, t, g)
                        for hh in range(2):
                            h, p = 2 * g + hh, 64 * hh
                            out = bank[p:p + 64, 0:P]
                            for d in range(2):
                                r = 4 * d + h
                                last = mm(out, xdt[:, t, d, h, :], le[:, r, c0:c1], d == 0, d == 1 and t == 0)
                            if t > 0:
                                for d in range(2):
                                    r, q = 4 * d + h, 64 * g
                                    first = t == 1 + d
                                    src = shaped(Lp("sssd"), 4, 64) if first else h_mid
                                    hs = src[q:q + 64, 2 * d + hh, :]
                                    last = mm(out, hs, ce[q:q + 64, r, (t - 1) * P:t * P], False, d == 1)
                        last.then_inc(psum_filled, 1)
                bank = open_bank(pe, "yms", l)
                pe.wait_ge(gated_sq_ready, l + 1)
                for i in range(2):
                    last = mm(bank[:, 0:W], C("ones"), sq[:, i, :], i == 0, i == 1)
                last.then_inc(psum_filled, 1)

            def out_projection(l):
                taken(pe, "pv", l, 2)
                pe.wait_ge(mix_ready, l + 1)
                for n in range(KT):
                    if n % 2 == 0:
                        item = next_item()
                    bank = open_bank(pe, "out", l, n)
                    project(item, (n % 2) * KT * P, o, KT, bank[:, 0:W]).then_inc(psum_filled, 1)

            def moe(l):
                bank = open_bank(pe, "lg", l)
                pe.wait_ge(h_ready, 4 * l + 4)
                rw_ = shaped(C("router"), KT, 16)
                for t in range(TILES):
                    for k in range(KT):
                        last = mm(bank[:, 16 * t:16 * t + 16], hT[:, k, COL[t]:COL[t] + P], rw_[:, k, :],
                                  k == 0, k == KT - 1)
                last.then_inc(psum_filled, 1)
                for t in range(TILES):
                    for k in range(2):
                        bank = open_bank(pe, "hm", l, t, k)
                        for i in range(4):
                            last = tr(bank[:, i * P:(i + 1) * P], hT[:, 4 * k + i, COL[t]:COL[t] + P])
                        last.then_inc(psum_filled, 1)
                fill(l, "router")
                bank = open_bank(pe, "pos", l)
                pe.wait_ge(assigned_ready, l + 1)
                for t in range(TILES):
                    for i in range(t):
                        mm(bank[:, 16 * t:16 * t + 16], C("ones"), rt[:, 16, 16 * i:16 * i + 16], i == 0, False)
                    mm(bank[:, 16 * t:16 * t + 16], C("rw0")[:, 0:P], rt[:, 16, 16 * t:16 * t + 16], t == 0, True)
                for i in range(TILES):
                    last = mm(bank[:, 48:64], C("ones"), rt[:, 16, 16 * i:16 * i + 16], i == 0, i == 2)
                last.then_inc(psum_filled, 1)

                def nothing(bank):
                    return mm(bank[:, 0:1], C("ones"), C("ones")[:, 0:1])

                def transposed(b, run):
                    for k in range(2):
                        bank = open_bank(pe, "xb", l, b, k)
                        if k == 0:
                            pe.wait_ge(xb_loaded[b % 2], 16 * (l * BLOCKS_OF[b % 2] + b // 2 + 1))
                        for i in range(4 if run else 0):
                            c = (4 * k + i) * P
                            last = tr(bank[:, i * SLOT:(i + 1) * SLOT], xb[b % 2][0:SLOT, c:c + P], SLOT)
                        (last if run else nothing(bank)).then_inc(psum_filled, 1)

                def expert_block(b, run):
                    for name in ("gate", "up"):
                        item = next_item()
                        bank = open_bank(pe, name, l, b)
                        if name == "gate":
                            taken(pe, "xb", l, b, 1)
                        for f in range(2 if run else 0):
                            last = project(item, f * KT * P, xbT[b % 2], KT, bank[:, f * SLOT:(f + 1) * SLOT])
                        (last if run else nothing(bank)).then_inc(psum_filled, 1)
                    if b + 1 < BLOCKS:
                        transposed(b + 1, run)
                    item = next_item()
                    for k in range(2):
                        bank = open_bank(pe, "down", l, b, k)
                        if k == 0:
                            taken(pe, "up", l, b)
                        for f in range(2 if run else 0):
                            last = mm(bank[0:SLOT, :], hid[b % 2][:, f, :],
                                      item[:, f * D + k * 512:f * D + (k + 1) * 512], f == 0, f == 1)
                        (last if run else nothing(bank)).then_inc(psum_filled, 1)

                used = blocks_used(pe, l)
                transposed(0, True)
                for b in range(BLOCKS):
                    on_both_ways(pe, used, b, [opened, items], expert_block)
                for t in range(TILES):
                    for k in range(2):
                        bank = open_bank(pe, "yt", l, t, k)
                        if k == 0:
                            pe.wait_ge(y_summed, TILES * l + t + 1)
                        for i in range(4):
                            c = (4 * k + i) * P
                            last = tr(bank[:, i * P:(i + 1) * P], y1[:, t, c:c + P])
                        last.then_inc(psum_filled, 1)

            pe.wait_ge(consts_loaded, 16)
            for l in range(DEPTH):
                fill(l, "start")
                mean_square(l, 1)
                in_projection(l)
                attention(l)
                fill(l, "inputs")
                rwkv_inputs(l)
                fill(l, "batches")
                for step, b in RW_ORDER:
                    rwkv_step(l, step, b)
                rwkv_norm(l)
                ssd(l)
                out_projection(l)
                mean_square(l, 2)
                moe(l)
            assert opened[0] == len(plan)

        @block.scalar
        def _(act):
            chain = [0]

            def link(ins):
                chain[0] += 1
                ins.then_inc(chain_a, 1)
                act.wait_ge(chain_a, chain[0])

            def f(out, in_, func, **kw):
                return nc.scalar.activation(out, in_, func, **kw)

            def root(out, n, eps, *key):
                bank = filled(act, *key)
                f(out, bank[:, 0:W], ACT.Sqrt, bias=C(eps), scale=1.0 / n).then_inc(read(*key), 1)

            def fill(l, place):
                for ml, c in MOD_SCHEDULE[l, place]:
                    bank = filled(act, "mod", ml, c)
                    f(mod_rows[c % 2][0:2, :], bank[0:2, :], ACT.Copy).then_inc(read("mod", ml, c), 1)

            def squares(l, which):
                if which == 2:
                    taken(act, "out", l, KT - 1)
                elif l:
                    taken(act, "yt", l - 1, TILES - 1, 1)
                f(sq, xT, ACT.Square).then_inc(xsq_ready, 1)
                root(tmp[:, 0:W], D, "eps", "ms", l, which)

            def attention(l):
                if l == 0:
                    act.wait_ge(slots_cleared, 32)
                for c in range(5):
                    taken(act, "u", l, c)
                f(sq[:, 0:5, :], u[:, 0:5, 1:W + 1], ACT.Square).then_inc(qk_sq_ready, 1)
                for i in range(5):
                    root(qn[:, i, :], 64, "eps", "qkms", l, i)
                bank = filled(act, "vt", l)
                f(v_tm, shaped(bank[:, 0:3 * P], 3, P), ACT.Copy).then_inc(read("vt", l), 1)
                fill(l, "qk")

                def exps(t):
                    n, c = (3 * P if t else P), 64 * t
                    act.wait_ge(shifted_ready, TILES * l + t + 1)
                    for h in range(8):
                        f(scores[t % 2][:, h, 0:n], scores[t % 2][:, h, 0:n], ACT.Exp,
                          bias=att_cols[:, c + 8 + h:c + 9 + h], accum_out=att_cols[:, c + 16 + h:c + 17 + h])
                    f(att_cols[:, c + 32:c + 40], att_cols[:, c + 24:c + 32], ACT.Exp).then_inc(exps_ready, 1)

                def copies(t):
                    n = 3 * P if t else P
                    if t:
                        filled(act, "pv", l, t - 1)
                    for h in range(8):
                        bank = filled(act, "pT", l, t, h)
                        f(probsT[:, h, 0:n], bank[:, 0:n], ACT.Copy).then_inc(read("pT", l, t, h), 1)
                    bank = filled(act, "pv", l, t)
                    f(o[:, 0:4, COL[t]:COL[t] + P], shaped(bank[:, :], 4, P), ACT.Copy)\
                        .then_inc(read("pv", l, t), 1)

                for step, t in ATT_STEPS:
                    if step == "scores":
                        exps(t)
                        if t == 0:
                            fill(l, "sc0")
                    else:
                        copies(t)
                        fill(l, f"pv{t}")
                fill(l, "inputs")

            def rwkv_inputs(l):
                act.wait_ge(mixed_ready, l + 1)
                f(mixed[0:32, 6, :], mixed[0:32, 6, :], ACT.Tanh)
                f(mixed[64:P, 6, :], mixed[64:P, 6, :], ACT.Sigmoid).then_inc(lora_ready, 1)
                for name, out, bias in (("wl", sgw, "w0"), ("al", asig, "a0")):
                    for d in range(2):
                        for i in range(2):
                            bank = filled(act, name, l, d, i)
                            k = 2 * d + i
                            f(out[:, k, :], bank[:, 0:W], ACT.Sigmoid, bias=Lc(bias, k))\
                                .then_inc(read(name, l, d, i), 1)
                for i in range(2):
                    bank = filled(act, "gg", l, i)
                    f(gate_rw[:, i, :], bank[:, 0:W], ACT.Copy).then_inc(read("gg", l, i), 1)
                for i in range(2):
                    root(tmp[:, i * W:(i + 1) * W], 1, "eps_kk", "kkn", l, i)
                for i in range(2):
                    bank = filled(act, "rvt", l, i)
                    f(rv_tm[:, i, :, :], shaped(bank[:, 0:3 * P], 3, P), ACT.Copy).then_inc(read("rvt", l, i), 1)
                act.wait_ge(decay_arg_ready, l + 1)
                for d in range(2):
                    Dd, Fd = csum[:, 2 * d:2 * d + 2, :], sgw[:, 2 * d:2 * d + 2, :]
                    incl, excl, s = (Dd, Fd, -DECAY) if d == 0 else (Fd, Dd, DECAY)
                    f(ar[:, d, :, 0, :], excl, ACT.Exp, scale=s)
                    f(ar[:, d, :, 1, :], incl, ACT.Exp, scale=s)
                    f(kb[:, 0, d, :, :], incl, ACT.Exp, scale=-s)
                f(decay_half, half_total, ACT.Exp, scale=DECAY).then_inc(decay_exp_ready, 1)

            def rwkv_step(l, step, b):
                s = b % 2
                kind, k = step[:5], step[-1]

                def copy(out, *key):
                    bank = filled(act, *key)
                    n = out.shape[1] * out.shape[2]
                    f(out, shaped(bank[:, 0:n], out.shape[1], out.shape[2]), ACT.Copy).then_inc(read(*key), 1)
                if kind == "power" and k != "4":
                    filled(act, "pt", l, b, int(k))
                    copy(pw[s], "p", l, b, int(k))
                    copy(pwT[s], "pt", l, b, int(k))
                elif step == "transpose":
                    copy(invT[s], "tT", l, b)
                elif step == "rhs":
                    copy(r_rhs[s], "rhs", l, b)
                elif step == "factors":
                    copy(kb_tm[s], "kbt", l, b)

            def ssd(l):
                act.wait_ge(rwkv_done, l + 1)
                z = dt_t[0:DT_ROWS, :]
                raw = u[0:DT_ROWS, UDT, 1:W + 1]
                b1 = Lc("dtb", 0, slice(0, DT_ROWS))
                taken(act, "u", l, UDT)
                link(f(dta[0:DT_ROWS, :], raw, ACT.Abs, bias=b1))
                f(z, raw, ACT.Relu, bias=b1)
                f(neg_a[0:DT_ROWS, 0:1], Lc("alog", 0, slice(0, DT_ROWS)), ACT.Exp)
                link(f(dta[0:DT_ROWS, :], dta[0:DT_ROWS, :], ACT.Exp, scale=-1.0))
                f(dta[0:DT_ROWS, :], dta[0:DT_ROWS, :], ACT.Ln, bias=1.0).then_inc(dt_parts, 1)
                act.wait_ge(conv_ready, l + 1)
                f(u[:, UX:UDT, 1:W + 1], u[:, UX:UDT, 1:W + 1], ACT.Silu).then_inc(silu_ready, 1)
                f(u[:, UZ:UZ + 2, 1:W + 1], u[:, UZ:UZ + 2, 1:W + 1], ACT.Silu).then_inc(z_ready, 1)
                bank = filled(act, "dtt", l)
                f(dtc, bank[:, 0:6 * DT_ROWS].rearrange("p (t k r) -> p t k r", t=TILES, k=2), ACT.Copy)\
                    .then_inc(read("dtt", l), 1)
                for r in range(8):
                    bank = filled(act, "cs", l, r)
                    f(le[:, r, :], bank[:, 0:W], ACT.Copy).then_inc(read("cs", l, r), 1)
                taken(act, "cs", l, 7)
                f(ce, le[:, :, LAT:W], ACT.Exp).then_inc(lat_decay_ready, 1)
                for t in range(TILES):
                    bank = filled(act, "xt", l, t)
                    f(x_tm[:, t, :], bank[:, 0:3 * P], ACT.Copy).then_inc(read("xt", l, t), 1)
                act.wait_ge(din_arg_ready, l + 1)
                f(decay_in, decay_in, ACT.Exp)
                f(chunk_decay, total_b, ACT.Exp).then_inc(din_ready, 1)
                act.wait_ge(le_arg_ready, l + 1)
                f(le, le, ACT.Exp).then_inc(le_ready, 1)
                fill(l, "ys")

            def moe(l):
                bank = filled(act, "lg", l)
                f(rt[:, 1, :], bank[:, 0:48], ACT.Sigmoid).then_inc(read("lg", l), 1)
                for t in range(TILES):
                    for k in range(2):
                        bank = filled(act, "hm", l, t, k)
                        f(h_tm[:, t, 512 * k:512 * k + 512], bank[:, :], ACT.Copy).then_inc(read("hm", l, t, k), 1)
                fill(l, "router")

                def nothing(out, bank):
                    return f(out, bank[0:out.shape[0], 0:1], ACT.Copy)

                def copy_block(b, run):
                    for k in range(2):
                        bank = filled(act, "xb", l, b, k)
                        (f(xbT[b % 2][:, 4 * k:4 * k + 4, :], shaped(bank[:, 0:4 * SLOT], 4, SLOT), ACT.Copy)
                         if run else nothing(xbT[b % 2][:, 4 * k, 0:1], bank)).then_inc(read("xb", l, b, k), 1)

                def expert_block(b, run):
                    bank = filled(act, "gate", l, b)
                    if b:
                        taken(act, "up", l, b - 1)
                    (f(sg, bank[:, 0:2 * SLOT], ACT.Silu)
                     if run else nothing(sg[:, 0:1], bank)).then_inc(read("gate", l, b), 1)
                    if b + 1 < BLOCKS:
                        copy_block(b + 1, run)
                    bank = filled(act, "down", l, b, 0)
                    if b >= 2:
                        act.wait_ge(y_written[b % 2], 16 * (l * BLOCKS_OF[b % 2] + b // 2))
                    (f(ye[b % 2][0:SLOT, 0:512], bank[0:SLOT, :], ACT.Copy)
                     if run else nothing(ye[b % 2][0:SLOT, 0:1], bank))\
                        .then_inc(read("down", l, b, 0), 1)

                used = blocks_used(act, l)
                copy_block(0, True)
                for b in range(BLOCKS):
                    on_both_ways(act, used, b, [released], expert_block)

            act.wait_ge(consts_loaded, 48)
            f(scond[:, :], cond[:, :], ACT.Silu).then_inc(cond_ready, 1)
            for l in range(DEPTH):
                fill(l, "start")
                squares(l, 1)
                if l == 0:
                    act.wait_ge(gaps_cleared, 1)
                for c in range(1, U_TILES, 2):
                    bank = filled(act, "u", l, c)
                    m = DT_ROWS if c == UDT else P
                    f(u[0:m, c, 1:W + 1], bank[0:m, 0:W], ACT.Copy).then_inc(read("u", l, c), 1)
                attention(l)
                rwkv_inputs(l)
                fill(l, "batches")
                for step, b in RW_ORDER:
                    rwkv_step(l, step, b)
                for i in range(2):
                    root(tmp[:, i * W:(i + 1) * W], 64, "eps_gn", "gnv", l, i)
                fill(l, "ssd")
                ssd(l)
                root(tmp[:, 0:W], 256, "eps", "yms", l)
                squares(l, 2)
                moe(l)

        @block.vector
        def _(dve):
            v = nc.vector
            chain = [0]

            def link(ins):
                chain[0] += 1
                ins.then_inc(chain_v, 1)
                dve.wait_ge(chain_v, chain[0])

            def tt(out, x, y, op):
                return v.tensor_tensor(out, x, y, op)

            def stt(out, x, s, y, op0, op1):
                return v.scalar_tensor_tensor(out, x, s, y, op0, op1)

            def ts(out, x, s1, s2, op0, op1=None):
                return v.tensor_scalar(out, x, s1, s2, op0, op1) if op1 is not None else \
                    v.tensor_scalar(out, x, s1, None, op0)

            def norm(l, which):
                scale, shift = (scale1, 0) if which == 1 else (scale2, 24)
                taken(dve, "ms", l, which)
                link(v.reciprocal(tmp[:, 0:W], tmp[:, 0:W]))
                link(tt(hT, xT, bc(tmp[:, 0:W], 1, KT), ALU.mult))
                for g, lo, hi in SEGMENTS:
                    for k in range(KT):
                        last = ts(hT[:, k, lo:hi], hT[:, k, lo:hi], scale[:, k, g:g + 1],
                                  mod[:, shift + k, g:g + 1], ALU.mult, ALU.add)
                    last.then_inc(h_ready, 1)

            def fill(l, place):
                for ml, c in MOD_SCHEDULE[l, place]:
                    bank = filled(dve, "modT", ml, c)
                    out = mod[:, 4 * c:4 * c + 4, :]
                    bm = bc(C(f"bmod{ml}")[:, 4 * c:4 * c + 4], 2, 2)
                    tt(out, shaped(bank[:, 0:8], 4, 2), bm, ALU.add).then_inc(read("modT", ml, c), 1)
                    for scale, name, last_chunk in ((scale1, "n1", 3), (scale2, "n2", 9)):
                        if c == last_chunk:
                            taken(dve, "modT", ml, c)
                            sc = mod[:, 4 * c - 4:4 * c + 4, :]
                            link(stt(scale, sc, 1.0, bc(C(f"{name}_{ml}"), 2, 2), ALU.add, ALU.mult))

            def attention(l):
                if l == 0:
                    dve.wait_ge(slots_cleared, 32)
                for i in range(5):
                    taken(dve, "qkms", l, i)
                    link(v.reciprocal(qn[:, i, :], qn[:, i, :]))
                    stt(qn[:, i, :], u[:, i, 1:W + 1], Lc("kw" if i == 4 else "qw", 0), qn[:, i, :],
                        ALU.mult, ALU.mult).then_inc(qn_ready, 1)
                dve.wait_ge(qn_ready, 5 * (l + 1))
                v.tensor_copy(new_k[l][:, :], qn[:, 4, 0:P]).then_inc(kv_copied, 1)
                taken(dve, "u", l, UV)
                v.tensor_copy(new_v[l][:, :], u[:, UV, 1:P + 1]).then_inc(kv_copied, 1)
                fill(l, "qk")
                for i in range(5):
                    bank = filled(dve, "rope", l, i)
                    link(tt(tmp[:, 0:2 * P], bank[:, 0:2 * P], C("sin"), ALU.mult))
                    tt(qn[:, i, LAT:W], qn[:, i, LAT:W], C("cos"), ALU.mult).then_inc(read("rope", l, i), 1)
                    taken(dve, "rope", l, i)
                    last = tt(qn[:, i, LAT:W], qn[:, i, LAT:W], tmp[:, 0:2 * P], ALU.add)
                    if i < 4:
                        link(last)
                last.then_inc(rope_ready, 1)

                def maxima(t):
                    n, c = (3 * P if t else P), 64 * t
                    sc = scores[t % 2]
                    if t == 2:
                        filled(dve, "pT", l, 0, 7)
                    for h in range(8):
                        bank = filled(dve, "sc", l, t, h)
                        scale = 64 ** -0.5
                        if t:
                            cut, whole = (1, slice(0, 3, 2)) if t == 1 else (0, slice(1, 3))
                            src, out = shaped(bank[:, 0:3 * P], 3, P), shaped(sc[:, h, 0:3 * P], 3, P)
                            stt(out[:, cut, :], src[:, cut, :], scale, C(f"ssd{2 - t}"), ALU.mult, ALU.add)
                            last = ts(out[:, whole, :], src[:, whole, :], scale, None, ALU.mult)
                        else:
                            last = ts(sc[:, h, 0:P], bank[:, 0:P], scale, None, ALU.mult)
                        last.then_inc(read("sc", l, t, h), 1)
                    taken(dve, "sc", l, t, 7)
                    top = att_cols[:, c:c + 8]
                    link(v.tensor_reduce(top, sc[:, :, 0:n], X, ALU.max))
                    link(tt(top, top, Lp("sink"), ALU.max))
                    ts(att_cols[:, c + 8:c + 16], top, -1.0, None, ALU.mult)
                    tt(att_cols[:, c + 24:c + 32], Lp("sink"), top, ALU.subtract).then_inc(shifted_ready, 1)

                def probabilities(t):
                    n, c = (3 * P if t else P), 64 * t
                    sc = scores[t % 2]
                    dve.wait_ge(exps_ready, TILES * l + t + 1)
                    link(tt(att_cols[:, c + 40:c + 48], att_cols[:, c + 16:c + 24], att_cols[:, c + 32:c + 40],
                            ALU.add))
                    link(v.reciprocal(att_cols[:, c + 48:c + 56], att_cols[:, c + 40:c + 48]))
                    tt(sc[:, :, 0:n], sc[:, :, 0:n], bc(att_cols[:, c + 48:c + 56], 2, n), ALU.mult)\
                        .then_inc(probs_ready, 1)

                for step, t in ATT_STEPS:
                    if step == "scores":
                        maxima(t)
                        if t == 0:
                            fill(l, "sc0")
                    else:
                        probabilities(t)
                        fill(l, f"pv{t}")
                fill(l, "inputs")

            def rwkv_inputs(l):
                taken(dve, "pv", l, 2)
                for c in range(6, 13):
                    taken(dve, "u", l, c)
                keep = cols[:, 0:7]
                link(tt(keep, Lp("mu0"), Lp("mu1"), ALU.add))
                link(ts(keep, keep, -1.0, 1.0, ALU.mult, ALU.add))
                for j in range(7):
                    last = ts(mixed[:, j, :], u[:, UR + j, 1:W + 1], cols[:, j:j + 1], None, ALU.mult)
                link(last)
                for j in range(7):
                    last = stt(mixed[:, j, :], u[:, UR + j, 0:W], Lc("mu0", j), mixed[:, j, :], ALU.mult, ALU.add)
                link(last)
                for j in range(7):
                    last = stt(mixed[:, j, :], u[:, UR + j, 2:W + 2], Lc("mu1", j), mixed[:, j, :],
                               ALU.mult, ALU.add)
                last.then_inc(mixed_ready, 1)
                dve.wait_ge(mixed_ready, l + 1)
                for i in range(2):
                    ts(kdir[:, i, :], mixed[:, 2 + i, :], Lc("kk", i), None, ALU.mult)
                    last = stt(sq[:, 2 + i, :], mixed[:, i, :], Lc("rk", i), mixed[:, 2 + i, :],
                               ALU.mult, ALU.mult)
                last.then_inc(bonus_in_ready, 1)
                dve.wait_ge(bonus_in_ready, l + 1)
                tt(sq[:, 0:2, :], kdir, kdir, ALU.mult).then_inc(kk_sq_ready, 1)
                taken(dve, "kkn", l, 1)
                link(v.reciprocal(tmp[:, :], tmp[:, :]))
                link(tt(kdir, kdir, shaped(tmp[:, :], 2, W), ALU.mult))
                for i in range(2):
                    bank = filled(dve, "bon", l, i)
                    tt(bonus[:, i, :], bank[:, 0:W], mixed[:, 4 + i, :], ALU.mult).then_inc(read("bon", l, i), 1)
                for k in range(4):
                    taken(dve, "wl", l, k // 2, k % 2)
                    last = v.tensor_tensor_scan(csum[:, k, :], C("restart"), sgw[:, k, :], 0.0, ALU.mult, ALU.add)
                link(last)
                for t in range(TILES):
                    e = COL[t] + P - 1
                    last = ts(half_total[:, :, t:t + 1], csum[:, :, e:e + 1], -0.5, None, ALU.mult)
                link(last)
                for t in range(TILES):
                    c0 = COL[t]
                    last = tt(csum[:, :, c0:c0 + P], csum[:, :, c0:c0 + P],
                              half_total[:, :, t:t + 1].broadcast_to([P, 4, P]), ALU.add)
                link(last)
                tt(sgw, csum, sgw, ALU.subtract).then_inc(decay_arg_ready, 1)
                taken(dve, "al", l, 1, 1)
                for d in range(2):
                    last = stt(kb[:, 1, d, :, :], kdir, -1.0, asig[:, 2 * d:2 * d + 2, :], ALU.mult, ALU.mult)
                link(last)
                link(ts(cols[:, 8:10], Lp("ka"), -1.0, 1.0, ALU.mult, ALU.add))
                for k in range(4):
                    last = ts(asig[:, k, :], asig[:, k, :], Lc("ka", k % 2), cols[:, 8 + k % 2:9 + k % 2],
                              ALU.mult, ALU.add)
                link(last)
                for d in range(2):
                    last = tt(asig[:, 2 * d:2 * d + 2, :], asig[:, 2 * d:2 * d + 2, :], mixed[:, 2:4, :], ALU.mult)
                link(last)
                dve.wait_ge(decay_exp_ready, l + 1)
                for d in range(2):
                    tt(ar[:, d, :, 0, :], ar[:, d, :, 0, :], kdir, ALU.mult)
                    tt(ar[:, d, :, 1, :], ar[:, d, :, 1, :], mixed[:, 0:2, :], ALU.mult)
                    last = tt(kb[:, 1, d, :, :], kb[:, 1, d, :, :], kb[:, 0, d, :, :], ALU.mult)
                link(last)
                for d in range(2):
                    last = tt(kb[:, 0, d, :, :], kb[:, 0, d, :, :], asig[:, 2 * d:2 * d + 2, :], ALU.mult)
                last.then_inc(factors_ready, 1)
                dve.wait_ge(factors_ready, l + 1)

            def scale_state(t, d, src):
                for i in range(2):
                    k = 2 * d + i
                    ts(S_til[:, k, :], src[:, k, :], decay_half[:, k, t:t + 1], None, ALU.mult)
                    for half in range(2):
                        q = slice(64 * half, 64 * half + 64)
                        last = ts(S_diag[q, k, half, :], src[q, k, :], decay_half[q, k, t:t + 1], None, ALU.mult)
                return last

            def rwkv_step(l, step, b):
                t, d = RW_BATCHES[b]
                s = b % 2
                kind, k = step[:5], step[-1]
                if step == "matrices":
                    if t > 0:
                        src = shaped(Lp("srw"), 4, 64) if b < STATE_BATCHES else S_lat
                        scale_state(t, d, src).then_inc(state_ready, 1)
                    if b == 0:
                        v.memset(S_diag, 0.0)
                    for j in range(4):
                        bank = filled(dve, "g4", l, b, j)
                        tt(g4[s][:, j, :, :], shaped(bank[:, :], 4, P), shaped(C(f"rw{d}"), 4, P), ALU.mult)\
                            .then_inc(read("g4", l, b, j), 1)
                    for half in range(2):
                        bank = filled(dve, "nd", l, b, half)
                        tt(pw[s][:, half::2, :], shaped(bank[:, 0:2 * P], 2, P), bc(C(f"nd{d}"), 1, 2), ALU.mult)\
                            .then_inc(read("nd", l, b, half), 1)
                    taken(dve, "nd", l, b, 1)
                    tt(pwT[s], g4[s][:, :, 2, :], bc(C("inv")[:, 0:P], 1, 4), ALU.mult)
                    tt(inv[s], pw[s], bc(C("ident"), 1, 4), ALU.add).then_inc(matrices_ready, 1)
                elif kind == "power" and k != "1":
                    bank = filled(dve, "t", l, b, int(k))
                    if k == "2":
                        dve.wait_ge(matrices_ready, len(RW_BATCHES) * l + b + 1)
                    else:
                        taken(dve, "t", l, b, int(k) - 1)
                    tt(inv[s], inv[s], shaped(bank[:, :], 4, P), ALU.add).then_inc(read("t", l, b, int(k)), 1)
                elif kind == "cross":
                    k = int(k)
                    bank = filled(dve, "cross", l, b, k)
                    mask = C("inv")[:, (1 + k) * P:(2 + k) * P]
                    tt(cross[s], shaped(bank[:, :], 4, P), bc(mask, 1, 4), ALU.mult)\
                        .then_inc(read("cross", l, b, k), 1)
                elif kind == "merge":
                    k = int(k)
                    if k < 2:
                        bank = filled(dve, "t", l, b, 5 + k)
                        taken(dve, "t", l, b, 4 + k)
                        tt(inv[s], inv[s], shaped(bank[:, :], 4, P), ALU.add).then_inc(read("t", l, b, 5 + k), 1)
                    bank = filled(dve, "tt", l, b, k)
                    if k:
                        taken(dve, "tt", l, b, k - 1)
                    else:
                        taken(dve, "tT", l, b)
                    tt(invT[s], invT[s], shaped(bank[:, :], 4, P), ALU.add).then_inc(read("tt", l, b, k), 1)
                elif step == "solve":
                    bank = filled(dve, "x", l, b)
                    v.tensor_copy(x_sol[s], shaped(bank[:, 0:256], 4, 64)).then_inc(read("x", l, b), 1)
                elif step == "output":
                    bank = filled(dve, "y", l, b)
                    src, out = shaped(bank[:, 0:2 * P], 2, P), y_rw[:, :, COL[t]:COL[t] + P]
                    if b in (0, 2, 3):
                        last = v.tensor_copy(out, src)
                    else:
                        taken(dve, "y", l, {1: 0, 4: 3, 5: 2}[b])
                        last = tt(out, out, src, ALU.add)
                    last.then_inc(read("y", l, b), 1)
                elif step == "state":
                    bank = filled(dve, "st", l, b)
                    if t > 0:
                        link(tt(S_lat[:, 2 * d:2 * d + 2, :], S_til[:, 2 * d:2 * d + 2, :],
                                shaped(bank[:, 0:P], 2, 64), ALU.add))
                    for i in range(2):
                        k = 2 * d + i
                        x = S_lat[:, k, :] if t > 0 else bank[:, i * 64:(i + 1) * 64]
                        out = S_lat[:, k, :] if t > 0 else state_rw[l][:, k, :]
                        last = ts(out, x, decay_half[:, k, t:t + 1], None, ALU.mult)
                    last.then_inc(read("st", l, b), 1)
                    taken(dve, "st", l, b)

            def rwkv_norm(l):
                last = v.memset(y_rw[:, :, P:LAT], 0.0)
                last.then_inc(gn_in_ready, 1)
                dve.wait_ge(gn_in_ready, l + 1)
                for i in range(2):
                    bank = filled(dve, "gnm", l, i)
                    stt(y_rw[:, i, :], bank[:, 0:W], -1.0 / 64, y_rw[:, i, :], ALU.mult, ALU.add).then_inc(read("gnm", l, i), 1)
                taken(dve, "gnm", l, 1)
                tt(sq[:, 0:2, :], y_rw, y_rw, ALU.mult).then_inc(gn_sq_ready, 1)
                taken(dve, "gnv", l, 1)
                link(v.reciprocal(tmp[:, :], tmp[:, :]))
                link(tt(y_rw, y_rw, shaped(tmp[:, :], 2, W), ALU.mult))
                for i in range(2):
                    last = ts(y_rw[:, i, :], y_rw[:, i, :], Lc("lnw", i), Lc("lnb", i), ALU.mult, ALU.add)
                link(last)
                link(tt(y_rw, y_rw, bonus, ALU.add))
                for lo, hi in ((0, P), (LAT, W)):
                    last = tt(o[:, 4:6, lo:hi], y_rw[:, :, lo:hi], gate_rw[:, :, lo:hi], ALU.mult)
                last.then_inc(rwkv_done, 1)
                dve.wait_ge(rwkv_done, l + 1)

            def ssd(l):
                R = slice(0, DT_ROWS)
                for c in range(13, 20):
                    taken(dve, "u", l, c)
                cw = Lp("cw")
                conv = shaped(sq_flat[:, 0:4 * W], 4, W)
                for j in range(4):
                    last = ts(conv[:, j, :], u[:, UX + j, 1:W + 1], cw[:, 4 + j:5 + j], Lc("cb", j),
                              ALU.mult, ALU.add)
                link(last)
                for j in range(4):
                    last = stt(conv[:, j, :], u[:, UX + j, 0:W], cw[:, j:j + 1], conv[:, j, :], ALU.mult, ALU.add)
                link(last)
                for j in range(4):
                    last = stt(conv[:, j, :], u[:, UX + j, 2:W + 2], cw[:, 8 + j:9 + j], conv[:, j, :],
                               ALU.mult, ALU.add)
                link(last)
                v.tensor_copy(u[:, UX:UDT, 1:W + 1], conv).then_inc(conv_ready, 1)
                dve.wait_ge(dt_parts, l + 1)
                link(tt(dt_t[R, :], dt_t[R, :], dta[R, :], ALU.add))
                link(ts(dta[R, :], dt_t[R, :], neg_a[R, 0:1], -1.0, ALU.mult, ALU.mult))
                link(v.tensor_tensor_scan(cs[R, :], C("restart", R), dta[R, :], 0.0, ALU.mult, ALU.add))
                B = slice(32, 64)
                link(tt(dtmp[B, :], dta[B, :], cs[B, :], ALU.subtract))
                for t in range(TILES):
                    e = COL[t] + P - 1
                    last = v.tensor_copy(cols[B, 16 + t:17 + t], cs[B, e:e + 1])
                link(last)
                for t in range(TILES):
                    c0 = COL[t]
                    last = ts(cs[B, c0:c0 + P], dtmp[B, c0:c0 + P], cols[B, 16 + t:17 + t], None, ALU.add)
                last.then_inc(cs_ready, 1)
                taken(dve, "cs", l, 7)
                taken(dve, "dtt", l)
                for t in range(TILES):
                    for d in range(2):
                        e = COL[t] + (P - 1 if d == 0 else 0)
                        last = v.tensor_copy(total_b[:, 4 * d:4 * d + 4, t:t + 1], le[:, 4 * d:4 * d + 4, e:e + 1])
                link(last)
                for t in range(TILES):
                    for d in range(2):
                        last = tt(decay_in[:, t, 4 * d:4 * d + 4], total_b[:, 4 * d:4 * d + 4, t],
                                  dtc[:, t, 1, 32 * d:32 * d + 4], ALU.subtract)
                last.then_inc(din_arg_ready, 1)
                dve.wait_ge(lat_decay_ready, l + 1)
                for r in range(8):
                    d, row = r // 4, 32 * (r // 4) + r % 4
                    for t in range(TILES):
                        last = stt(le[:, r, COL[t]:COL[t] + P], le[:, r, COL[t]:COL[t] + P],
                                   dtc[:, t, 1, row:row + 1], C(f"ssd{d}"), ALU.subtract, ALU.add)
                last.then_inc(le_arg_ready, 1)
                taken(dve, "xt", l, 2)
                for t in range(TILES):
                    xv = x_tm[:, t, 0:2 * P].rearrange("p (h c) -> p h c", h=4)
                    for d in range(2):
                        last = tt(xdt[:, t, d, :, :], xv, bc(dtc[:, t, 0, 32 * d:32 * d + 4], 2, 64), ALU.mult)
                link(last)
                dve.wait_ge(din_ready, l + 1)
                for s, (t, d) in enumerate(SSD_STATES):
                    last = tt(xdd[:, s, :, :], xdt[:, t, d, :, :], bc(decay_in[:, t, 4 * d:4 * d + 4], 2, 64),
                              ALU.mult)
                last.then_inc(xdd_ready, 1)
                dve.wait_ge(silu_ready, l + 1)
                for g in range(2):
                    q = slice(64 * g, 64 * g + 64)
                    for d in range(2):
                        r = 4 * d + 2 * g
                        last = tt(ce[q, r:r + 2, :], ce[q, r:r + 2, :], bc(u[q, UC, 1 + LAT:1 + W], 1, 2), ALU.mult)
                dve.wait_ge(le_ready, l + 1)
                for t in range(TILES):
                    for g in range(2):
                        bank = filled(dve, "gt", l, t, g)
                        for r in (2 * g, 4 + 2 * g):
                            x = le[:, r:r + 2, COL[t]:COL[t] + P]
                            last = tt(x, x, bc(bank[:, 0:P], 1, 2), ALU.mult)
                        last.then_inc(read("gt", l, t, g), 1)
                init = shaped(Lp("sssd"), 4, 64)
                for s, (t, d) in enumerate(SSD_STATES):
                    bank = filled(dve, "hst", l, s)
                    src = shaped(bank[:, 0:P], 2, 64)
                    if t == 0:
                        last = v.tensor_copy(state_ssd[l][:, 2 * d:2 * d + 2, :], src)
                    else:
                        for g in range(2):
                            q = slice(64 * g, 64 * g + 64)
                            for hh in range(2):
                                r = 4 * d + 2 * g + hh
                                last = stt(h_mid[q, 2 * d + hh, :], init[q, 2 * d + hh, :],
                                           chunk_decay[q, r, t:t + 1], src[q, hh, :], ALU.mult, ALU.add)
                    last.then_inc(read("hst", l, s), 1)
                fill(l, "ys")
                for t in range(TILES):
                    for i in range(2):
                        bank = filled(dve, "ys", l, t, i)
                        last = stt(y_ssd[:, i, COL[t]:COL[t] + P], u[:, UX + i, 1 + COL[t]:1 + COL[t] + P],
                                   Lc("dskip", i), bank[:, 0:P], ALU.mult, ALU.add)
                        last.then_inc(read("ys", l, t, i), 1)
                link(v.memset(y_ssd[:, :, P:LAT], 0.0))
                dve.wait_ge(z_ready, l + 1)
                link(tt(y_ssd, y_ssd, u[:, UZ:UZ + 2, 1:W + 1], ALU.mult))
                tt(sq[:, 0:2, :], y_ssd, y_ssd, ALU.mult).then_inc(gated_sq_ready, 1)
                taken(dve, "yms", l)
                link(v.reciprocal(tmp[:, 0:W], tmp[:, 0:W]))
                for i in range(2):
                    for lo, hi in ((0, P), (LAT, W)):
                        last = stt(o[:, 6 + i, lo:hi], y_ssd[:, i, lo:hi], Lc("nw", i), tmp[:, lo:hi],
                                   ALU.mult, ALU.mult)
                last.then_inc(mix_ready, 1)

            def add_gated(bank, n, first):
                for g, lo, hi in SEGMENTS:
                    last = stt(xT[:, n, lo:hi], bank[:, lo:hi], mod[:, first + n, g:g + 1], xT[:, n, lo:hi],
                               ALU.mult, ALU.add)
                return last

            def routing(l):
                taken(dve, "lg", l)
                s = rt[:, 1, :]
                sel = rt[:, 2, :]

                def g3(k):
                    return shaped(rt[:, k, :], TILES, 16)

                def g4v(k):
                    return shaped(rt[:, k, :], TILES, 4, 4)

                link(tt(g3(2), g3(1), bc(C("rbias"), 1, TILES), ALU.add))
                q = g4v(2)

                def small4(k):
                    return rt[:, k, 0:12].rearrange("p (t g) -> p t g", t=TILES)
                tt(small4(3), q[:, :, :, 0], q[:, :, :, 1], ALU.max)
                tt(small4(4), q[:, :, :, 2], q[:, :, :, 3], ALU.max)
                tt(small4(5), q[:, :, :, 0], q[:, :, :, 1], ALU.min)
                link(tt(small4(6), q[:, :, :, 2], q[:, :, :, 3], ALU.min))
                tt(small4(7), small4(3), small4(4), ALU.max)
                tt(small4(8), small4(3), small4(4), ALU.min)
                link(tt(small4(9), small4(5), small4(6), ALU.max))
                link(tt(small4(8), small4(8), small4(9), ALU.max))
                link(tt(small4(7), small4(7), small4(8), ALU.add))

                def first_max(x, rank, n, w1, w2, w3):
                    m = rt[:, w1, 0:TILES]
                    link(v.tensor_reduce(m, x, X, ALU.max))
                    link(tt(w2, x, bc(m, 2, n), ALU.is_equal))
                    link(tt(w2, w2, bc(C(rank), 1, TILES), ALU.mult))
                    link(v.tensor_reduce(m, w2, X, ALU.max))
                    link(tt(w3, w2, bc(m, 2, n), ALU.is_equal))

                first_max(small4(7), "rank4", 4, 10, small4(8), small4(9))
                inside = g4v(11)
                link(v.tensor_copy(inside, bc(small4(9), 3, 4)))
                link(ts(rt[:, 12, :], rt[:, 11, :], -NEG, NEG, ALU.mult, ALU.add))
                link(tt(rt[:, 2, :], rt[:, 2, :], rt[:, 11, :], ALU.mult))
                link(tt(rt[:, 2, :], rt[:, 2, :], rt[:, 12, :], ALU.add))
                first_max(g3(2), "rank16", 16, 10, g3(13), g3(14))
                link(stt(rt[:, 2, :], rt[:, 14, :], 2 * NEG, rt[:, 2, :], ALU.mult, ALU.add))
                first_max(g3(2), "rank16", 16, 10, g3(13), g3(15))
                tt(rt[:, 16, :], rt[:, 14, :], rt[:, 15, :], ALU.add).then_inc(assigned_ready, 1)
                fill(l, "router")
                bank = filled(dve, "pos", l)
                count, nb, ends = rt[:, 17, 0:16], rt[:, 18, 0:16], rt[:, 18, 16:32]
                v.tensor_copy(rt[:, 19, :], bank[:, 0:48])
                v.tensor_copy(count, bank[:, 48:64]).then_inc(read("pos", l), 1)
                taken(dve, "pos", l)
                link(ts(nb, count, 0.0, None, ALU.is_gt))
                for k in range(1, TILES * P // SLOT):
                    link(stt(nb, count, float(k * SLOT), nb, ALU.is_gt, ALU.add))
                link(v.tensor_tensor_scan(ends, C("ones")[:, 0:16], nb, 0.0, ALU.mult, ALU.add))
                base = rt[:, 17, 16:32]
                link(tt(base, ends, nb, ALU.subtract))
                link(ts(base, base, float(SLOT), None, ALU.mult))
                link(tt(g3(19), g3(19), bc(base, 1, TILES), ALU.add))
                tt(rt[:, 20, :], rt[:, 14, :], rt[:, 19, :], ALU.mult)
                link(tt(rt[:, 21, :], rt[:, 15, :], rt[:, 19, :], ALU.mult))
                v.tensor_reduce(rt[:, 22, 0:3], g3(20), X, ALU.add)
                link(v.tensor_reduce(rt[:, 22, 3:6], g3(21), X, ALU.add))
                v.tensor_copy(rows[:, :], rt[:, 22, 0:6]).then_inc(rows_ready, 1)
                link(tt(cmp, bc(ends, 1, BLOCKS), bc(C("block"), 2, EXPERTS), ALU.is_le))
                link(v.tensor_reduce(rt[:, 23, 0:BLOCKS], cmp, X, ALU.add))
                link(ts(rt[:, 23, 0:BLOCKS], rt[:, 23, 0:BLOCKS], float(EXPERTS - 1), None, ALU.min))
                v.tensor_copy(block_expert[:, BLOCKS:BLOCKS + 1], rt[:, 18, 31:32])
                v.tensor_copy(block_expert[:, 0:BLOCKS], rt[:, 23, 0:BLOCKS]).then_inc(blocks_ready, 1)
                tt(rt[:, 20, :], rt[:, 14, :], rt[:, 1, :], ALU.mult)
                link(tt(rt[:, 21, :], rt[:, 15, :], rt[:, 1, :], ALU.mult))
                v.tensor_reduce(w12[:, 0, :], g3(20), X, ALU.add)
                link(v.tensor_reduce(w12[:, 1, :], g3(21), X, ALU.add))
                link(tt(rt[:, 10, 0:3], w12[:, 0, :], w12[:, 1, :], ALU.add))
                link(v.reciprocal(rt[:, 10, 4:7], rt[:, 10, 0:3]))
                link(tt(w12, w12, bc(rt[:, 10, 4:7], 1, 2), ALU.mult))

            def moe(l):
                def nothing(out, bank):
                    return v.tensor_copy(out, bank[0:out.shape[0], 0:1])

                def expert_block(b, run):
                    taken(dve, "gate", l, b)
                    bank = filled(dve, "up", l, b)
                    (tt(hid[b % 2].rearrange("p f n -> p (f n)"), sg, bank[:, 0:2 * SLOT], ALU.mult)
                     if run else nothing(hid[b % 2][:, 0, 0:1], bank)).then_inc(read("up", l, b), 1)
                    bank = filled(dve, "down", l, b, 1)
                    if b >= 2:
                        dve.wait_ge(y_written[b % 2], 16 * (l * BLOCKS_OF[b % 2] + b // 2))
                    (v.tensor_copy(ye[b % 2][0:SLOT, 512:D], bank[0:SLOT, :])
                     if run else nothing(ye[b % 2][0:SLOT, 512:513], bank))\
                        .then_inc(read("down", l, b, 1), 1)

                used = blocks_used(dve, l)
                for b in range(BLOCKS):
                    on_both_ways(dve, used, b, [released], expert_block)
                for t in range(TILES):
                    dve.wait_ge(y_gathered[t], 32 * (l + 1))
                    link(ts(y1[:, t, :], y1[:, t, :], w12[:, 0, t:t + 1], None, ALU.mult))
                    stt(y1[:, t, :], y2[:, t, :], w12[:, 1, t:t + 1], y1[:, t, :], ALU.mult, ALU.add)\
                        .then_inc(y_summed, 1)
                for t in range(TILES):
                    g = min(t, 1)
                    for k in range(2):
                        bank = filled(dve, "yt", l, t, k)
                        for i in range(4):
                            n = 4 * k + i
                            out = xT[:, n, COL[t]:COL[t] + P]
                            last = stt(out, bank[:, i * P:(i + 1) * P], mod[:, 40 + n, g:g + 1], out,
                                       ALU.mult, ALU.add)
                        last.then_inc(read("yt", l, t, k), 1)
                taken(dve, "yt", l, TILES - 1, 1)

            v.memset(u[:, :, 0:1], 0.0)
            v.memset(u[:, :, W + 1:W + 2], 0.0)
            v.memset(csum, 0.0)
            v.memset(ye[0], 0.0).then_inc(zeros_set, 1)
            link(v.memset(o[:, :, P:LAT], 0.0))
            v.memset(cols[:, :], 0.0).then_inc(gaps_cleared, 1)
            dve.wait_ge(gaps_cleared, 1)
            dve.wait_ge(consts_loaded, 48)
            for l in range(DEPTH):
                fill(l, "start")
                dve.wait_ge(small_loaded, 16 * (l + 1))
                norm(l, 1)
                if l:
                    v.memset(u[:, :, 0:1], 0.0)
                    v.memset(u[:, :, W + 1:W + 2], 0.0)
                for c in range(0, U_TILES, 2):
                    bank = filled(dve, "u", l, c)
                    v.tensor_copy(u[:, c, 1:W + 1], bank[:, 0:W]).then_inc(read("u", l, c), 1)
                attention(l)
                rwkv_inputs(l)
                fill(l, "batches")
                for step, b in RW_ORDER:
                    rwkv_step(l, step, b)
                rwkv_norm(l)
                fill(l, "ssd")
                ssd(l)
                for n in range(KT):
                    bank = filled(dve, "out", l, n)
                    add_gated(bank, n, 16).then_inc(read("out", l, n), 1)
                taken(dve, "out", l, KT - 1)
                norm(l, 2)
                routing(l)
                moe(l)


def constants():
    import numpy as np
    i = np.arange(P)
    row, col = i[:, None], i[None, :]
    same = lambda n: (row // n == col // n).astype(np.float32)
    rot = np.zeros((P, P), np.float32)
    for m in range(P):
        if m % 32 < 16:
            rot[m + 16, m] = -1.0
        else:
            rot[m - 16, m] = 1.0
    strict = [(row < col), (row > col)]
    incl = [(row <= col), (row >= col)]
    c = {
        "head": same(64), "ident": np.eye(P), "rot": rot,
        "inv": np.concatenate([same(16)] + [same(2 * n) - same(n) for n in (16, 32, 64)], 1),
    }
    for d in range(2):
        c[f"rw{d}"] = np.concatenate([strict[d], incl[d]] * 2, 1)
        c[f"nd{d}"] = strict[1 - d] * same(16)
        c[f"ssd{d}"] = np.where(incl[d], 0.0, NEG)
    tok = np.arange(2 * P)
    pos = np.stack([tok // 64, tok % 64]).astype(np.float32)
    freq = np.float32(10000.0) ** (-np.arange(16, dtype=np.float32) / np.float32(16))
    ang = np.stack([pos[(f % 64) // 32] * freq[f % 16] for f in range(P)]).astype(np.float32)
    c["cos"], c["sin"] = np.cos(ang), np.sin(ang)
    restart = np.ones((P, W), np.float32)
    restart[:, COL] = 0.0
    c["restart"] = restart
    c["rank16"] = np.broadcast_to(np.arange(16, 0, -1), (P, 16))
    c["eps"], c["eps_kk"], c["eps_gn"] = EPS, 1e-12, GN_EPS
    c["ones"] = np.ones((P, P))
    c["block"] = np.broadcast_to(np.arange(BLOCKS), (P, BLOCKS))
    c["rank4"] = np.broadcast_to(np.arange(4, 0, -1), (P, 4))
    return c


def tokens(prompt, sample):
    import numpy as np
    out = np.zeros((P, KT, W), np.float32)
    out[:, :, 0:P] = prompt.T.reshape(KT, P, P).transpose(1, 0, 2)
    out[:, :, LAT:] = sample.T.reshape(KT, P, 2 * P).transpose(1, 0, 2)
    return out.reshape(P, KT * W)


def by_feature(v):
    return v.reshape(-1, P).T


def kernel(**inputs):
    import numpy as np
    import concourse.bacc as bacc
    from concourse.bass_utils import run_bass_kernel_spmd

    x = {k: np.asarray(v) for k, v in inputs.items()}

    def tiles_of(w):
        k, n = w.shape
        return w.reshape(k // P, P, n // P, P).transpose(2, 1, 0, 3).reshape(n // P, P, k)

    q_cols = np.concatenate([np.r_[64 * m:64 * m + 64, 64 * (m + 4):64 * (m + 4) + 64] for m in range(4)])
    in_cols = np.concatenate([q_cols, np.arange(512, 2432)])
    out_rows = np.concatenate([q_cols, np.arange(512, 1024)])
    weights = np.zeros((DEPTH * LAYER_ITEMS, P, ITEM), np.float32)
    n = 0
    for l in range(DEPTH):
        def put(t):
            nonlocal n
            t = t.reshape(-1, ITEM // t.shape[2], P, t.shape[2]).transpose(0, 2, 1, 3).reshape(-1, P, ITEM)
            weights[n:n + len(t)] = t
            n += len(t)
        w = x["w_mod"][l].reshape(2, 4, P, MOD_CHUNKS, 512).transpose(3, 0, 2, 1, 4)
        weights[n:n + MOD_ITEMS] = w.reshape(MOD_ITEMS, P, ITEM)
        n += MOD_ITEMS
        dt = np.zeros((KT, P, DT_ROWS), np.float32)
        for d in range(2):
            dt[:, :, 32 * d:32 * d + 4] = x["w_in"][l][:, 2432:2436].reshape(KT, P, 4)
        t = np.zeros((20, P, D), np.float32)
        t[:19] = tiles_of(x["w_in"][l][:, in_cols])
        t[19, :, :KT * DT_ROWS] = dt.transpose(1, 0, 2).reshape(P, -1)
        put(t)
        put(tiles_of(x["w_out"][l][out_rows]))
        for e in range(EXPERTS):
            put(tiles_of(x["exp_gate"][l, e]))
            put(tiles_of(x["exp_up"][l, e]))
            weights[n] = x["exp_down"][l, e].reshape(2, P, D).transpose(1, 0, 2).reshape(P, ITEM)
            n += 1
    assert n == len(weights)

    small = np.zeros((DEPTH, P, LAYER_N), np.float32)
    for l in range(DEPTH):
        def s(name, v, rows=slice(0, P)):
            lo, hi = LAYER_COLS[name]
            small[l][rows, lo:hi] = v
        s("qw", np.tile(x["q_norm_w"][l], 2)[:, None])
        s("kw", np.tile(x["k_norm_w"][l], 2)[:, None])
        s("sink", np.broadcast_to(x["attn_sink"][l], (P, 8)))
        s("mu0", by_feature(x["rw_mu"][l, 0]))
        s("mu1", by_feature(x["rw_mu"][l, 1]))
        s("w0", by_feature(x["rw_w0"][l].reshape(-1)))
        s("a0", by_feature(x["rw_a0"][l].reshape(-1)))
        s("kk", by_feature(x["rw_k_k"][l]))
        s("ka", by_feature(x["rw_k_a"][l]))
        s("rk", by_feature(x["rw_r_k"][l].reshape(-1)))
        s("lnw", by_feature(x["rw_ln_w"][l]))
        s("lnb", by_feature(x["rw_ln_b"][l]))
        s("cw", by_feature(x["ssd_conv_w"][l].reshape(-1)))
        s("cb", by_feature(x["ssd_conv_b"][l]))
        for d in range(2):
            r = slice(32 * d, 32 * d + 4)
            s("dtb", x["ssd_dt_bias"][l, d][:, None], r)
            s("alog", x["ssd_a_log"][l, d][:, None], r)
        s("dskip", by_feature(np.repeat(x["ssd_d"][l], 64)))
        s("nw", by_feature(x["ssd_norm_w"][l]))
        s("lora", x["rw_w_up"][l].transpose(1, 0, 2).reshape(32, 512), slice(0, 32))
        s("lora", x["rw_a_up"][l].transpose(1, 0, 2).reshape(32, 512), slice(32, 64))
        lo = LAYER_COLS["lora"][0]
        small[l][64:, lo:lo + 256] = x["rw_g_up"][l]
        s("kc", x["cache_k"][0, l].transpose(1, 2, 0).reshape(P, P))
        s("vc", x["cache_v"][0, l].reshape(P, P))
        s("srw", x["state_rwkv"][0, l].reshape(2, 2, 2, 64, 64).transpose(2, 4, 0, 1, 3).reshape(P, 256))
        s("sssd", x["state_ssd"][0, l].reshape(2, 2, 2, 64, 64).transpose(1, 4, 0, 2, 3).reshape(P, 256))

    consts = np.zeros((P, CONST_N), np.float32)
    table = constants()
    table["router"] = x["router_w"].reshape(KT, P, 16).transpose(1, 0, 2).reshape(P, P)
    table["rbias"] = np.broadcast_to(x["router_bias"], (P, 16))
    for l in range(DEPTH):
        table[f"bmod{l}"] = by_feature(x["b_mod"][l])
        table[f"n1_{l}"] = by_feature(x["norm1_w"][l])
        table[f"n2_{l}"] = by_feature(x["norm2_w"][l])
    for name, (lo, hi) in CONST_COLS.items():
        consts[:, lo:hi] = table[name]
    cond = np.stack([by_feature(x["c_ctx"]), by_feature(x["c"][0])], 2).reshape(P, 16)

    nc = bacc.Bacc("TRN2", target_bir_lowering=False, num_devices=1)
    arrays = {"weights": weights, "small": small, "consts": consts, "cond": np.ascontiguousarray(cond),
              "x": tokens(x["x_prompt"][0], x["x_sample"][0])}
    shapes = {"y": (P, KT * W), "new_k": (DEPTH, P, P), "new_v": (DEPTH, P, P),
              "new_rw": (DEPTH, P, 256), "new_ssd": (DEPTH, P, 256)}
    f32 = mybir.dt.float32
    a = {k: nc.dram_tensor(k, v.shape, f32, kind="ExternalInput").ap() for k, v in arrays.items()}
    a.update({k: nc.dram_tensor(k, v, f32, kind="ExternalOutput").ap() for k, v in shapes.items()})
    program(nc, a)
    r = run_bass_kernel_spmd(nc, [arrays], core_ids=[0]).results[0]

    y = r["y"].reshape(P, KT, W).transpose(2, 1, 0).reshape(W, D)
    cache = lambda v: np.ascontiguousarray(v.transpose(0, 2, 1).reshape(1, DEPTH, P, 2, 64))
    rw = r["new_rw"].reshape(DEPTH, 2, 64, 2, 2, 64).transpose(0, 3, 4, 1, 5, 2).reshape(1, DEPTH, 2, 4, 64, 64)
    sd = r["new_ssd"].reshape(DEPTH, 2, 64, 2, 2, 64).transpose(0, 3, 1, 4, 5, 2).reshape(1, DEPTH, 2, 4, 64, 64)
    return (np.ascontiguousarray(y[None, 0:P]), np.ascontiguousarray(y[None, LAT:]), cache(r["new_k"]),
            cache(r["new_v"]), np.ascontiguousarray(rw), np.ascontiguousarray(sd))
```

```python
import concourse.bass as bass
from concourse import mybir
from contextlib import ExitStack

DEPTH = 2
P = 128
D = 1024
KT = D // P
TILES = 3
COL = [0, P + 1, 2 * P + 1]
W = 3 * P + 1
LAT = COL[1]
SEGMENTS = [(0, 0, P), (1, LAT, W)]
EPS = 1e-6
GN_EPS = 64e-5
DECAY = 0.606531
NEG = -1e30

UQ, UK, UV, UR, URK, URV, ULORA, UZ, UX, UB, UC, UDT = 0, 4, 5, 6, 8, 10, 12, 13, 15, 17, 18, 19
U_TILES = 20
DT_ROWS = 64
EXPERTS = 16
GROUPS = 4
EXPERT_ITEMS = 3
TOP_K = 2
SLOT = 100
BLOCKS = (TILES * P * TOP_K - EXPERTS) // SLOT + EXPERTS
ITEM = 2048
GATHERED = 2
MOD_ITEMS, IN_ITEMS, OUT_ITEMS = 24, 10, 4
DENSE_ITEMS = MOD_ITEMS + IN_ITEMS + OUT_ITEMS
LAYER_ITEMS = DENSE_ITEMS + EXPERTS * EXPERT_ITEMS
SLOTS = 5

MOD_CHUNKS = 12
MOD_PLACES = ["start", "norm1", "sc0", "pv0", "pv1", "pv2", "batches", "ssd", "ys", "norm2", "rows"]
MOD_AT = {(0, "start"): 2, (0, "norm1"): 2, (0, "sc0"): 1, (0, "pv0"): 1, (0, "pv1"): 1, (0, "pv2"): 1,
          (0, "batches"): 3, (0, "ssd"): 1, (0, "ys"): 1, (0, "norm2"): 1, (0, "rows"): 1,
          (1, "norm1"): 1, (1, "sc0"): 1, (1, "pv0"): 1, (1, "pv1"): 1, (1, "batches"): 3, (1, "ssd"): 1,
          (1, "ys"): 1}

AFTER_U = {6: "qk_squares", 8: "v_columns", 13: "rotation"}


def modulation_schedule():
    queue = [(l, c) for l in range(DEPTH) for c in range(MOD_CHUNKS)]
    out = {}
    for l in range(DEPTH):
        for place in MOD_PLACES:
            n = MOD_AT.get((l, place), 0)
            out[l, place], queue = queue[:n], queue[n:]
    assert not queue
    return out


MOD_SCHEDULE = modulation_schedule()


def modulation_steps(l, place):
    chunks = MOD_SCHEDULE[l, place]
    for i, chunk in enumerate(chunks):
        yield ("mod", *chunk)
        if i:
            yield ("modT", *chunks[i - 1])
    if chunks:
        yield ("modT", *chunks[-1])

RW_BATCHES = [(0, 0), (0, 1), (1, 0), (2, 1), (2, 0), (1, 1)]
STATE_BATCHES = 4
RW_STEPS = ["matrices", "power1", "power2", "power3", "power4", "transpose", "cross0", "merge0", "cross1",
            "merge1", "cross2", "merge2", "rhs", "solve", "output", "factors", "state"]
RW_ORDER = [(step, b) for pair in ((0, 1), (2, 3), (4, 5)) for step in RW_STEPS for b in pair
            if b < STATE_BATCHES or step not in ("factors", "state")]
SSD_STATES = [(0, 0), (0, 1), (1, 0), (2, 1)]


ATT_STEPS = [("scores", 0), ("scores", 1), ("values", 0), ("scores", 2), ("values", 1), ("values", 2)]


def columns(names):
    at, out = 0, {}
    for name, n in names:
        out[name] = (at, at + n)
        at += n
    return out, at


LAYER_COLS, LAYER_N = columns([
    ("qw", 1), ("kw", 1), ("sink", 8), ("mu0", 7), ("mu1", 7),
    ("w0", 4), ("a0", 4), ("kk", 2), ("ka", 2), ("rk", 2), ("lnw", 2), ("lnb", 2), ("cw", 12), ("cb", 4),
    ("dtb", 1), ("alog", 1), ("dskip", 2), ("nw", 2), ("lora", 512), ("kc", 128), ("vc", 128),
    ("srw", 256), ("sssd", 256)])
CONST_COLS, CONST_N = columns([
    ("head", 128), ("ident", 128), ("rot", 128),
    ("inv", 512), ("rw0", 512), ("rw1", 512), ("nd0", 128), ("nd1", 128), ("ssd0", 128),
    ("ssd1", 128), ("cos", 256), ("sin", 256), ("restart", W), ("rank16", 16), ("rank4", 4),
    ("router", 128), ("rbias", 16), ("ones", 128), ("block", BLOCKS), ("slot", GATHERED * SLOT), ("bmod0", 48), ("bmod1", 48),
    ("n1_0", 8), ("n1_1", 8), ("n2_0", 8), ("n2_1", 8), ("eps", 1), ("eps_kk", 1), ("eps_gn", 1)])


def psum_plan():
    plan = []

    def g(consumer, *key):
        plan.append((key, consumer))

    def fill(l, place):
        for step in modulation_steps(l, place):
            g("a" if step[0] == "mod" else "v", *step)

    for l in range(DEPTH):
        fill(l, "start")
        g("a", "ms", l, 1)
        fill(l, "norm1")
        for c in range(U_TILES):
            g("va"[c % 2], "u", l, c)
            if AFTER_U.get(c) == "qk_squares":
                for i in range(5):
                    g("a", "qkms", l, i)
            elif AFTER_U.get(c) == "v_columns":
                g("a", "vt", l)
            elif AFTER_U.get(c) == "rotation":
                for i in range(5):
                    g("v", "rope", l, i)
        for step, t in ATT_STEPS:
            if step == "scores":
                for h in range(8):
                    g("v", "sc", l, t, h)
                if t == 0:
                    fill(l, "sc0")
            else:
                for h in range(8):
                    g("a", "pT", l, t, h)
                g("a", "pv", l, t)
                fill(l, f"pv{t}")
        for d in range(2):
            for i in range(2):
                g("a", "wl", l, d, i)
        for d in range(2):
            for i in range(2):
                g("a", "al", l, d, i)
        for i in range(2):
            g("a", "gg", l, i)
        for i in range(2):
            g("a", "kkn", l, i)
        for i in range(2):
            g("v", "bon", l, i)
        for i in range(2):
            g("a", "rvt", l, i)
        fill(l, "batches")
        for step, b in RW_ORDER:
            kind, k = step[:5], step[-1]
            if kind == "matri":
                for j in range(4):
                    g("v", "g4", l, b, j)
                for half in range(2):
                    g("v", "nd", l, b, half)
            elif kind == "power":
                if k != "1":
                    g("v", "t", l, b, int(k))
                if k != "4":
                    g("a", "p", l, b, int(k))
                    g("a", "pt", l, b, int(k))
            elif kind == "trans":
                g("a", "tT", l, b)
            elif kind == "cross":
                g("v", "cross", l, b, int(k))
            elif kind == "merge":
                if k != "2":
                    g("v", "t", l, b, 5 + int(k))
                g("v", "tt", l, b, int(k))
            elif kind == "rhs":
                g("a", "rhs", l, b)
            elif kind == "solve":
                g("v", "x", l, b)
            elif kind == "outpu":
                g("v", "y", l, b)
            elif kind == "facto":
                g("a", "kbt", l, b)
            elif kind == "state":
                g("v", "st", l, b)
        for i in range(2):
            g("v", "gnm", l, i)
        for i in range(2):
            g("a", "gnv", l, i)
        fill(l, "ssd")
        g("a", "dtt", l)
        for r in range(8):
            g("a", "cs", l, r)
        for t in range(TILES):
            g("a", "xt", l, t)
            for grp in range(2):
                g("v", "gt", l, t, grp)
        for s in range(4):
            g("v", "hst", l, s)
        fill(l, "ys")
        for t in range(TILES):
            for grp in range(2):
                g("v", "ys", l, t, grp)
        g("a", "yms", l)
        for n in range(KT):
            g("v", "out", l, n)
        g("a", "ms", l, 2)
        fill(l, "norm2")
        g("a", "lg", l)
        for t in range(TILES):
            for k in range(2):
                g("a", "hm", l, t, k)
        g("v", "pos", l)
        fill(l, "rows")
        for k in range(2):
            g("a", "xb", l, 0, k)
        for b in range(BLOCKS):
            g("a", "gate", l, b)
            g("v", "up", l, b)
            if b + 1 < BLOCKS:
                for k in range(2):
                    g("a", "xb", l, b + 1, k)
            g("a", "down", l, b, 0)
            g("v", "down", l, b, 1)
        for t in range(TILES):
            for k in range(2):
                g("v", "yt", l, t, k)
    return plan


def weight_stream(plan):
    out = []
    for key, _ in plan:
        kind, l, rest = key[0], key[1], key[2:]
        if kind == "mod":
            out += [(("fixed", l, 2 * rest[0] + i), key) for i in range(2)]
        elif kind == "u" and rest[0] % 2 == 0:
            out.append((("fixed", l, MOD_ITEMS + rest[0] // 2), ("u", l, rest[0] + 1)))
        elif kind == "out" and rest[0] % 2 == 0:
            out.append((("fixed", l, MOD_ITEMS + IN_ITEMS + rest[0] // 2), ("out", l, rest[0] + 1)))
        elif kind == "gate":
            out.append((("expert", l, rest[0], 0), key))
        elif kind == "up":
            out.append((("expert", l, rest[0], 1), key))
        elif kind == "down" and rest[1] == 0:
            out.append((("expert", l, rest[0], 2), ("down", l, rest[0], 1)))
    return out


BLOCKS_OF = [(BLOCKS + 1) // 2, BLOCKS // 2]


def loads_before(l, b):
    assert GATHERED % 2 == 0
    return l * (BLOCKS_OF[b % 2] - GATHERED // 2) + (b - GATHERED) // 2


def program(nc, a):
    fp32 = mybir.dt.float32
    ALU = mybir.AluOpType
    ACT = mybir.ActivationFunctionType
    X = mybir.AxisListType.X

    ctx = ExitStack()
    with ctx:
        def sb(name, n):
            return ctx.enter_context(nc.sbuf_tensor("sb_" + name, [P, n], fp32))

        def sem(name):
            return ctx.enter_context(nc.semaphore(name))

        def shaped(ap, *dims):
            names = [f"d{i}" for i in range(len(dims))]
            sizes = {k: v for k, v in zip(names[1:], dims[1:])}
            return ap.rearrange(f"p ({' '.join(names)}) -> p {' '.join(names)}", **sizes)

        ring = sb("ring", SLOTS * ITEM)
        xT = shaped(sb("xT", KT * W)[:, :], KT, W)
        hT_flat = sb("hT", KT * W)[:, :]
        hT = shaped(hT_flat, KT, W)
        u_flat = sb("u", U_TILES * (W + 2))[:, :]
        u = shaped(u_flat, U_TILES, W + 2)
        sq_flat = sb("sq", KT * W)[:, :]
        sq = shaped(sq_flat, KT, W)
        o = shaped(sb("o", KT * W)[:, :], KT, W)
        small = sb("small", LAYER_N)
        consts = sb("consts", CONST_N)
        cond = sb("cond", 16)
        scond = sb("scond", 16)
        mod = shaped(sb("mod", 96)[:, :], 48, 2)
        scale1 = shaped(sb("scale1", 16)[:, :], 8, 2)
        scale2 = shaped(sb("scale2", 16)[:, :], 8, 2)
        tmp = sb("tmp", 2 * W)
        mod_rows = [sb(f"mod_rows{i}", 512) for i in range(2)]
        cols = sb("cols", 32)
        AREN = 13776
        arena = sb("arena", AREN)
        state_rw = [shaped(sb(f"state_rw{l}", 256)[:, :], 4, 64) for l in range(DEPTH)]
        state_ssd = [shaped(sb(f"state_ssd{l}", 256)[:, :], 4, 64) for l in range(DEPTH)]
        new_k = [sb(f"new_k{l}", P) for l in range(DEPTH)]
        new_v = [sb(f"new_v{l}", P) for l in range(DEPTH)]

        rows = ctx.enter_context(nc.sbuf_tensor("sb_rows", [P, 2 * TILES], mybir.dt.uint32))
        block_expert = ctx.enter_context(nc.sbuf_tensor("sb_block_expert", [P, BLOCKS + 1], mybir.dt.int32))
        x_slots = nc.dram_tensor("x_slots", (BLOCKS * SLOT, D), fp32, kind="Internal").ap()
        y_slots = nc.dram_tensor("y_slots", (BLOCKS * SLOT, D), fp32, kind="Internal").ap()

        banks = [ctx.enter_context(nc.psum_tensor(f"bank{i}", [P, 512], fp32)) for i in range(8)]

        def carve(base, *dims):
            n = 1
            for x in dims:
                n *= x
            assert base[1] + n <= base[2], (base, dims)
            ap = base[0][:, base[1]:base[1] + n]
            base[1] += n
            return shaped(ap, *dims) if len(dims) > 1 else ap

        at = [arena, 0, AREN]
        qn = carve(at, 5, W)
        scores = [carve(at, 8, 3 * P) for _ in range(2)]
        probsT = carve(at, 8, 3 * P)
        v_tm = carve(at, TILES, P)
        att_cols = carve(at, 3 * 64)
        rw = [arena, 0, AREN]
        mixed_end = AREN - 5 * W
        assert at[1] <= mixed_end
        mixed_r = o[:, 6:8, :]
        mixed_k, mixed_v, mixed_lora = (shaped(arena[:, mixed_end + c * W:mixed_end + (c + n) * W], n, W)
                                        for c, n in ((0, 2), (2, 2), (4, 1)))
        mixed_tiles = [x[:, i, :] for x in (mixed_r, mixed_k, mixed_v) for i in range(2)] + [mixed_lora[:, 0, :]]
        rw[2] = mixed_end
        kdir = carve(rw, 2, W)
        gate_rw = carve(rw, 2, W)
        bonus = carve(rw, 2, W)
        y_rw = carve(rw, 2, W)
        rv_tm = carve(rw, 2, TILES, P)
        S_til = carve(rw, 4, 64)
        S_diag = carve(rw, 4, 2, 64)
        S_lat = carve(rw, 4, 64)
        decay_half = carve(rw, 4, TILES)
        half_total = carve(rw, 4, TILES)
        reuse = rw[1]
        sgw = carve(rw, 4, W)
        asig = carve(rw, 4, W)
        csum = carve(rw, 4, W)
        rw2 = [arena, reuse, AREN]
        tail = [u_flat, 0, 13 * (W + 2)]
        g4 = [carve(rw2, 4, 4, P) for _ in range(2)]
        r_rhs = [carve(rw2, 4, 64) for _ in range(2)]
        x_sol = [carve(rw2, 4, 64) for _ in range(2)]
        pw = [carve(tail, 4, P) for _ in range(2)]
        pwT = [carve(tail, 4, P) for _ in range(2)]
        inv = [carve(tail, 4, P) for _ in range(2)]
        invT = [carve(tail, 4, P) for _ in range(2)]
        cross = [carve(tail, 4, P), carve(rw2, 4, P)]
        kb_tm = cross
        ar = shaped(hT_flat, 2, 2, 2, W)
        kb = shaped(sq_flat, 2, 2, 2, W)
        norm_start, norm_end = 2 * W, 8 * W
        ss = [arena, 0, norm_start]
        dtc = carve(ss, TILES, 2, DT_ROWS)
        total_b = carve(ss, 8, TILES)
        decay_in = carve(ss, TILES, 8)
        chunk_decay = carve(ss, 8, TILES)
        h_mid = carve(ss, 4, 64)
        ss = [arena, norm_start, norm_end]
        xdt = carve(ss, TILES, 2, 4, 64)
        y_ssd = carve(ss, 2, W)
        ss = [arena, norm_end, rw2[1]]
        le = carve(ss, 8, W)
        ce = carve(ss, 8, 2 * P)
        x_tm = carve(ss, TILES, 3 * P)
        xdd = carve(ss, 4, 4, 64)
        dt_t = carve(rw2, W)
        dta = carve(rw2, W)
        cs = carve(rw2, W)
        neg_a = carve(rw2, 4)
        assert rw2[1] <= mixed_end
        dtmp = mixed_lora[:, 0, :]
        conv = shaped(sq_flat[:, 0:4 * W], 4, W)
        mo = [arena, 0, AREN]
        rt = carve(mo, 24, 48)
        cmp = carve(mo, BLOCKS, EXPERTS)
        w12 = carve(mo, 2, TILES)
        sg = carve(mo, 2 * SLOT)
        hid = [carve(mo, 2, SLOT) for _ in range(2)]
        xb = [carve(mo, D) for _ in range(2)]
        xbT = [carve(mo, KT, SLOT) for _ in range(2)]
        ye = [carve(mo, D) for _ in range(2)]
        h_tm = carve(mo, TILES, D)
        mo2 = [u_flat, 0, U_TILES * (W + 2)]
        y1 = carve(mo2, TILES, D)
        y2 = carve(mo2, TILES, D)
        picks_2 = carve(mo2, TILES, GATHERED * SLOT)
        picks = carve(mo2, TILES, GATHERED * SLOT)

        def C(name, rows=slice(0, P)):
            lo, hi = CONST_COLS[name]
            return consts[rows, lo:hi]

        def Lp(name, rows=slice(0, P)):
            lo, hi = LAYER_COLS[name]
            return small[rows, lo:hi]

        def Lc(name, i, rows=slice(0, P)):
            lo = LAYER_COLS[name][0]
            return small[rows, lo + i:lo + i + 1]

        def bc(ap, dim, n):
            ap = ap.unsqueeze(dim)
            shape = list(ap.shape)
            shape[dim] = n
            return ap.broadcast_to(shape)

        plan = psum_plan()
        stream = weight_stream(plan)
        index = {key: n for n, (key, _) in enumerate(plan)}
        read_no = {}
        count = {"a": 0, "v": 0}
        for key, consumer in plan:
            count[consumer] += 1
            read_no[key] = count[consumer]
        psum_filled = sem("psum_filled")
        psum_read = {"a": sem("psum_read_by_scalar"), "v": sem("psum_read_by_vector")}
        opened = [0]
        released = {"a": 0, "v": 0}

        def open_bank(pe, *key):
            n = index[key]
            assert n == opened[0], (key, plan[opened[0]])
            opened[0] += 1
            if n >= 8:
                old, consumer = plan[n - 8]
                pe.wait_ge(psum_read[consumer], read_no[old])
            return banks[n % 8]

        def filled(eng, *key):
            eng.wait_ge(psum_filled, index[key] + 1)
            return banks[index[key] % 8]

        def read(*key):
            consumer = plan[index[key]][1]
            released[consumer] += 1
            assert read_no[key] == released[consumer], key
            return psum_read[consumer]

        def taken(eng, *key):
            eng.wait_ge(psum_read[plan[index[key]][1]], read_no[key])

        def blocks_used(eng, l):
            eng.wait_ge(blocks_ready, l + 1)
            return eng.value_load(block_expert[0:1, BLOCKS:BLOCKS + 1], min_val=0, max_val=BLOCKS)

        def block_groups(l, b):
            return index["gate", l, b], index["down", l, b, 1] + 1

        def reads_before(consumer, n):
            return sum(c == consumer for _, c in plan[:n])

        def skip_reads(eng, consumer, l, b):
            first, end = block_groups(l, b)
            before = reads_before(consumer, first)
            eng.wait_ge(psum_read[consumer], before)
            eng.nop().then_inc(psum_read[consumer], reads_before(consumer, end) - before)

        item_ready = [sem(f"weights_ready{i}") for i in range(SLOTS)]
        consts_loaded = sem("consts_loaded")
        cond_loaded = sem("cond_loaded")
        x_loaded = sem("x_loaded")
        small_loaded = sem("small_loaded")
        out_written = sem("out_written")
        gaps_cleared = sem("gaps_cleared")
        cond_ready = sem("cond_ready")
        xsq_ready = sem("xsq_ready")
        h_scaled = sem("h_scaled")
        h_ready = sem("h_ready")
        qk_sq_ready = sem("qk_sq_ready")
        qn_ready = sem("qn_ready")
        rope_ready = sem("rope_ready")
        shifted_ready = sem("shifted_ready")
        exps_ready = sem("exps_ready")
        probs_ready = sem("probs_ready")
        kv_copied = sem("kv_copied")
        mixed_ready = sem("mixed_ready")
        lora_ready = sem("lora_ready")
        kk_sq_ready = sem("kk_sq_ready")
        bonus_in_ready = sem("bonus_in_ready")
        decay_arg_ready = sem("decay_arg_ready")
        decay_exp_ready = sem("decay_exp_ready")
        factors_ready = sem("factors_ready")
        state_ready = sem("state_ready")
        matrices_ready = sem("matrices_ready")
        gn_in_ready = sem("gn_in_ready")
        gn_sq_ready = sem("gn_sq_ready")
        rwkv_done = sem("rwkv_done")
        conv_ready = sem("conv_ready")
        silu_ready = sem("silu_ready")
        dt_parts = sem("dt_parts")
        cs_ready = sem("cs_ready")
        lat_decay_ready = sem("lat_decay_ready")
        le_arg_ready = sem("le_arg_ready")
        din_arg_ready = sem("din_arg_ready")
        le_ready = sem("le_ready")
        din_ready = sem("din_ready")
        xdd_ready = sem("xdd_ready")
        gated_sq_ready = sem("gated_sq_ready")
        z_ready = sem("z_ready")
        mix_ready = sem("mix_ready")
        zeros_set = sem("zeros_set")
        slots_cleared = sem("slots_cleared")
        assigned_ready = sem("assigned_ready")
        rows_ready = sem("rows_ready")
        blocks_ready = sem("blocks_ready")
        picks_ready = sem("picks_ready")
        scattered = sem("scattered")
        xb_loaded = [sem(f"xb_loaded{i}") for i in range(2)]
        y_written = [sem(f"y_written{i}") for i in range(2)]
        more_y_written = [[sem(f"y_written_{l}_{b}") for b in range(EXPERTS, BLOCKS)] for l in range(DEPTH)]

        def wait_stored(eng, l, b):
            if b < EXPERTS:
                eng.wait_ge(y_written[b % 2], 16 * (l * (EXPERTS // 2) + b // 2 + 1))
            else:
                eng.wait_ge(more_y_written[l][b - EXPERTS], 16)

        y_gathered = [sem(f"y_gathered{t}") for t in range(TILES)]
        y_summed = sem("y_summed")
        chain_v = sem("vector_chain")
        chain_a = sem("scalar_chain")

        block = ctx.enter_context(nc.Block())

        @block.sync
        def _(sp):
            sp.dma_start(cond[:, :], a["cond"][:, :]).then_inc(cond_loaded, 16)

            def load_block(l, b, first_item, used):
                def load():
                    expert = sp.value_load(block_expert[0:1, b:b + 1], min_val=0, max_val=EXPERTS - 1)
                    for j in range(EXPERT_ITEMS):
                        n = first_item + j
                        first = expert * EXPERT_ITEMS + (l * LAYER_ITEMS + DENSE_ITEMS + j)
                        filled(sp, *stream[n - SLOTS][1])
                        sp.dma_start(ring[:, (n % SLOTS) * ITEM:(n % SLOTS + 1) * ITEM],
                                     a["weights"][bass.ds(first, 1)].rearrange("a p n -> (a p) n"))\
                            .then_inc(item_ready[n % SLOTS], 16)
                        if j == 1 and b >= GATHERED:
                            if b == GATHERED:
                                sp.wait_ge(scattered, 6 * 16 * (l + 1))
                            if b >= GATHERED + 2:
                                filled(sp, "xb", l, b - 2, 1)
                            sp.dma_start(xb[b % 2][0:SLOT, :], x_slots[b * SLOT:(b + 1) * SLOT, :])\
                                .then_inc(xb_loaded[b % 2], 16)

                if b < EXPERTS:
                    load()
                    return
                with sp.If(used > b):
                    load()
                with sp.Else():
                    for n in range(first_item, first_item + EXPERT_ITEMS):
                        sp.wait_ge(item_ready[n % SLOTS], 16 * (n // SLOTS))
                        sp.nop().then_inc(item_ready[n % SLOTS], 16)
                    sp.wait_ge(xb_loaded[b % 2], 16 * loads_before(l, b))
                    sp.nop().then_inc(xb_loaded[b % 2], 16)

            for n, (where, _) in enumerate(stream):
                kind, l = where[:2]
                if n == 2:
                    sp.dma_start(consts[:, :], a["consts"][:, :]).then_inc(consts_loaded, 16)
                if n == 4:
                    sp.dma_start(xT, shaped(a["x"][:, :], KT, W)).then_inc(x_loaded, 16)
                    sp.dma_start(small[:, :], a["small"][0]).then_inc(small_loaded, 16)
                if kind == "expert":
                    b, j = where[2:]
                    if j:
                        continue
                    if b == 0:
                        used = blocks_used(sp, l)
                    if b == BLOCKS // 2 and l < DEPTH - 1:
                        sp.wait_ge(mix_ready, l + 1)
                        sp.dma_start(small[:, :], a["small"][l + 1]).then_inc(small_loaded, 16)
                    load_block(l, b, n, used)
                else:
                    if n and stream[n - 1][0][0] == "expert":
                        sp.wait_ge(y_gathered[1], 32 * l)
                    if n >= SLOTS:
                        filled(sp, *stream[n - SLOTS][1])
                    sp.dma_start(ring[:, (n % SLOTS) * ITEM:(n % SLOTS + 1) * ITEM],
                                 a["weights"][l * LAYER_ITEMS + where[2]]).then_inc(item_ready[n % SLOTS], 16)

        @block.gpsimd
        def _(pool):
            pool.wait_ge(zeros_set, 1)
            filled(pool, "u", 0, 3)
            pool.dma_start(x_slots.rearrange("(b p) c -> p b c", p=SLOT),
                           bc(ye[0][0:SLOT, :], 1, BLOCKS)).then_inc(slots_cleared, 16)
            pool.dma_start(y_slots[EXPERTS * SLOT:, :].rearrange("(b p) c -> p b c", p=SLOT),
                           bc(ye[0][0:SLOT, :], 1, BLOCKS - EXPERTS)).then_inc(slots_cleared, 16)
            for l in range(DEPTH):
                pool.wait_ge(kv_copied, 2 * (l + 1))
                pool.dma_start(a["new_k"][l], new_k[l][:, :]).then_inc(out_written, 16)
                pool.dma_start(a["new_v"][l], new_v[l][:, :]).then_inc(out_written, 16)
                taken(pool, "st", l, 1)
                pool.dma_start(shaped(a["new_rw"][l], 4, 64), state_rw[l]).then_inc(out_written, 16)
                taken(pool, "hst", l, 1)
                pool.dma_start(shaped(a["new_ssd"][l], 4, 64), state_ssd[l]).then_inc(out_written, 16)
                pool.wait_ge(slots_cleared, 32)
                pool.wait_ge(rows_ready, l + 1)
                taken(pool, "hm", l, TILES - 1, 1)
                for k in range(2):
                    for t in range(TILES):
                        c = k * TILES + t
                        pool.indirect_dma_start(x_slots, bass.IndirectOffsetOnAxis(rows[:, c:c + 1], 0),
                                                h_tm[:, t, :], None).then_inc(scattered, 16)
                used = blocks_used(pool, l)

                def store_block(b):
                    taken(pool, "down", l, b, 0)
                    taken(pool, "down", l, b, 1)
                    done = y_written[b % 2] if b < EXPERTS else more_y_written[l][b - EXPERTS]
                    pool.dma_start(y_slots[b * SLOT:(b + 1) * SLOT, :], ye[b % 2][0:SLOT, :]).then_inc(done, 16)

                for b in range(EXPERTS):
                    store_block(b)
                for b in range(EXPERTS, BLOCKS):
                    with pool.If(used > b):
                        store_block(b)
                for b in (EXPERTS - 2, EXPERTS - 1):
                    wait_stored(pool, l, b)
                for b in range(EXPERTS, BLOCKS):
                    with pool.If(used > b):
                        wait_stored(pool, l, b)
                for t in range(TILES):
                    for k, y in enumerate((y1, y2)):
                        c = k * TILES + t
                        pool.indirect_dma_start(y[:, t, :], None, y_slots,
                                                bass.IndirectOffsetOnAxis(rows[:, c:c + 1], 0))\
                            .then_inc(y_gathered[t], 16)
            taken(pool, "yt", DEPTH - 1, TILES - 1, 1)
            pool.dma_start(shaped(a["y"][:, :], KT, W), xT).then_inc(out_written, 16)
            pool.wait_ge(out_written, 16 * (4 * DEPTH + 1))

        @block.tensor
        def _(pe):
            items = [0]

            def next_item():
                n = items[0]
                pe.wait_ge(item_ready[n % SLOTS], 16 * (n // SLOTS + 1))
                items[0] += 1
                return ring[:, (n % SLOTS) * ITEM:(n % SLOTS + 1) * ITEM]

            def mm(out, lhsT, rhs, start=True, stop=True):
                return nc.tensor.matmul(out, lhsT, rhs, start=start, stop=stop, skip_group_check=True)

            def tr(out, in_, n=P):
                return nc.tensor.transpose(out, in_, C("ident")[0:n, 0:n])

            def mean_square(l, which):
                bank = open_bank(pe, "ms", l, which)
                for k in range(KT):
                    pe.wait_ge(xsq_ready, KT * (2 * l + which - 1) + k + 1)
                    last = mm(bank[:, 0:W], C("ones"), sq[:, k, :], k == 0, k == KT - 1)
                last.then_inc(psum_filled, 1)
                fill(l, f"norm{which}")

            def project(item, off, src, kts, out, m=P, ready=None):
                for k in range(kts):
                    if ready is not None:
                        pe.wait_ge(h_ready, ready + k + 1)
                    last = mm(out, item[:, off + k * m:off + (k + 1) * m], src[:, k, :], k == 0, k == kts - 1)
                return last

            def fill(l, place):
                cv = shaped(scond[:, :], KT, 2)
                for kind, ml, c in modulation_steps(l, place):
                    bank = open_bank(pe, kind, ml, c)
                    if kind == "mod":
                        if (ml, c) == (0, 0):
                            pe.wait_ge(cond_ready, 1)
                        for i in range(2):
                            item = shaped(next_item(), 4, 512)
                            for k in range(4):
                                last = mm(bank[0:2, :], cv[:, 4 * i + k, :], item[:, k, :], i + k == 0, i + k == 4)
                    else:
                        if (ml, c) == (0, 0):
                            pe.wait_ge(consts_loaded, 16)
                        taken(pe, "mod", ml, c)
                        for i in range(4):
                            last = tr(bank[:, 2 * i:2 * i + 2], mod_rows[c % 2][0:2, i * P:(i + 1) * P], 2)
                    last.then_inc(psum_filled, 1)

            def in_projection(l):
                for c in range(U_TILES):
                    if c % 2 == 0:
                        item = next_item()
                    bank = open_bank(pe, "u", l, c)
                    m = DT_ROWS if c == UDT else P
                    project(item, (c % 2) * KT * P, hT, KT, bank[0:m, 0:W], m,
                            KT * 2 * l if c == 0 else None).then_inc(psum_filled, 1)
                    after_u(l, AFTER_U.get(c))

            def after_u(l, step):
                for i in range(5 if step == "qk_squares" else 0):
                    bank = open_bank(pe, "qkms", l, i)
                    pe.wait_ge(qk_sq_ready, l + 1)
                    mm(bank[:, 0:W], C("head"), sq[:, i, :]).then_inc(psum_filled, 1)
                if step == "v_columns":
                    bank = open_bank(pe, "vt", l)
                    taken(pe, "u", l, UV)
                    for t in range(TILES):
                        last = tr(bank[:, t * P:(t + 1) * P], u[:, UV, 1 + COL[t]:1 + COL[t] + P])
                    last.then_inc(psum_filled, 1)
                for i in range(5 if step == "rotation" else 0):
                    bank = open_bank(pe, "rope", l, i)
                    pe.wait_ge(qn_ready, 5 * l + i + 1)
                    mm(bank[:, 0:2 * P], C("rot"), qn[:, i, LAT:W]).then_inc(psum_filled, 1)

            def attention(l):
                def att_scores(t):
                    c0 = COL[t]
                    for h in range(8):
                        m, p = h % 4, 64 * (h // 4)
                        bank = open_bank(pe, "sc", l, t, h)
                        if t == 0 and h == 0:
                            pe.wait_ge(rope_ready, l + 1)
                        q = qn[p:p + 64, m, c0:c0 + P]
                        if t == 0:
                            last = mm(bank[:, 0:P], q, qn[p:p + 64, 4, 0:P])
                        else:
                            mm(bank[:, 0:2 * P], q, qn[p:p + 64, 4, LAT:W])
                            last = mm(bank[:, 2 * P:3 * P], q, Lp("kc", slice(p, p + 64)))
                        last.then_inc(psum_filled, 1)

                def att_values(t):
                    blocks = 1 if t == 0 else 3
                    for h in range(8):
                        bank = open_bank(pe, "pT", l, t, h)
                        if h % 4 == 0:
                            pe.wait_ge(probs_ready, 2 * (TILES * l + t) + h // 4 + 1)
                        for b in range(blocks):
                            last = tr(bank[:, b * P:(b + 1) * P], scores[t % 2][:, h, b * P:(b + 1) * P])
                        last.then_inc(psum_filled, 1)
                    bank = open_bank(pe, "pv", l, t)
                    taken(pe, "pT", l, t, 7)
                    for h in range(8):
                        m, p = h % 4, 64 * (h // 4)
                        for b in range(blocks):
                            if t == 0:
                                v = v_tm[:, 0, p:p + 64]
                            elif b < 2:
                                v = v_tm[:, 1 + b, p:p + 64]
                            else:
                                v = Lp("vc")[:, p:p + 64]
                            last = mm(bank[p:p + 64, m * P:(m + 1) * P], v, probsT[:, h, b * P:(b + 1) * P],
                                      b == 0, b == blocks - 1)
                    last.then_inc(psum_filled, 1)

                for step, t in ATT_STEPS:
                    if step == "scores":
                        att_scores(t)
                        if t == 0:
                            fill(l, "sc0")
                    else:
                        att_values(t)
                        fill(l, f"pv{t}")

            def rwkv_inputs(l):
                for name, r0, r1 in (("wl", 0, 32), ("al", 32, 64)):
                    for d in range(2):
                        for i in range(2):
                            bank = open_bank(pe, name, l, d, i)
                            pe.wait_ge(lora_ready, l + 1)
                            c = d * 256 + i * P
                            mm(bank[:, 0:W], Lp("lora", slice(r0, r1))[:, c:c + P], mixed_lora[r0:r1, 0, :])\
                                .then_inc(psum_filled, 1)
                for i in range(2):
                    bank = open_bank(pe, "gg", l, i)
                    mm(bank[:, 0:W], Lp("lora", slice(64, P))[:, i * P:(i + 1) * P], mixed_lora[64:P, 0, :])\
                        .then_inc(psum_filled, 1)
                for i in range(2):
                    bank = open_bank(pe, "kkn", l, i)
                    pe.wait_ge(kk_sq_ready, l + 1)
                    mm(bank[:, 0:W], C("head"), sq[:, i, :]).then_inc(psum_filled, 1)
                for i in range(2):
                    bank = open_bank(pe, "bon", l, i)
                    pe.wait_ge(bonus_in_ready, l + 1)
                    mm(bank[:, 0:W], C("head"), sq[:, 2 + i, :]).then_inc(psum_filled, 1)
                for i in range(2):
                    bank = open_bank(pe, "rvt", l, i)
                    for t in range(TILES):
                        last = tr(bank[:, t * P:(t + 1) * P], mixed_v[:, i, COL[t]:COL[t] + P])
                    last.then_inc(psum_filled, 1)

            def four(bank, lhsT, rhs):
                for j in range(4):
                    last = mm(bank[:, j * P:(j + 1) * P], lhsT[:, j, :], rhs[:, j, :])
                last.then_inc(psum_filled, 1)

            def rwkv_step(l, step, b):
                t, d = RW_BATCHES[b]
                c0, c1 = COL[t], COL[t] + P
                s = b % 2
                kind, k = step[:5], step[-1]
                if step == "matrices":
                    if b == 0:
                        pe.wait_ge(factors_ready, l + 1)
                    for j in range(4):
                        i, p = j // 2, 64 * (j % 2)
                        bank = open_bank(pe, "g4", l, b, j)
                        both = ar[p:p + 64, d, i, :, c0:c1]
                        mm(bank[:, 0:2 * P], kb[p:p + 64, 0, d, i, c0:c1], both)
                        mm(bank[:, 2 * P:4 * P], kb[p:p + 64, 1, d, i, c0:c1], both).then_inc(psum_filled, 1)
                    for half in range(2):
                        bank = open_bank(pe, "nd", l, b, half)
                        p = 64 * half
                        for i in range(2):
                            last = mm(bank[:, i * P:(i + 1) * P], ar[p:p + 64, d, i, 0, c0:c1],
                                      kb[p:p + 64, 1, d, i, c0:c1])
                        last.then_inc(psum_filled, 1)
                elif kind == "power":
                    k = int(k)
                    if k == 1:
                        pe.wait_ge(matrices_ready, len(RW_BATCHES) * l + b + 1)
                    else:
                        bank = open_bank(pe, "t", l, b, k)
                        taken(pe, "pt", l, b, k - 1)
                        if k > 2:
                            taken(pe, "t", l, b, k - 1)
                        four(bank, pwT[s], inv[s])
                    if k < 4:
                        four(open_bank(pe, "p", l, b, k), pwT[s], pw[s])
                        four(open_bank(pe, "pt", l, b, k), pw[s], pwT[s])
                elif step == "transpose":
                    bank = open_bank(pe, "tT", l, b)
                    taken(pe, "t", l, b, 4)
                    for j in range(4):
                        last = tr(bank[:, j * P:(j + 1) * P], inv[s][:, j, :])
                    last.then_inc(psum_filled, 1)
                elif kind == "cross":
                    bank = open_bank(pe, "cross", l, b, int(k))
                    if k != "0":
                        taken(pe, "t", l, b, 4 + int(k))
                    four(bank, g4[s][:, :, 2, :], inv[s])
                elif kind == "merge":
                    k = int(k)
                    if k < 2:
                        bank = open_bank(pe, "t", l, b, 5 + k)
                        taken(pe, "cross", l, b, k)
                        if k:
                            taken(pe, "tt", l, b, k - 1)
                        else:
                            taken(pe, "tT", l, b)
                        four(bank, invT[s], cross[s])
                    bank = open_bank(pe, "tt", l, b, k)
                    taken(pe, "cross", l, b, k)
                    if k:
                        taken(pe, "tt", l, b, k - 1)
                    four(bank, cross[s], invT[s])
                elif step == "rhs":
                    bank = open_bank(pe, "rhs", l, b)
                    if t > 0:
                        pe.wait_ge(state_ready, 4 * l + b - 1)
                    for i in range(2):
                        if t > 0:
                            mm(bank[:, i * P:(i + 1) * P], ar[:, d, i, 0, c0:c1], S_diag[:, 2 * d + i, :, :],
                               True, False)
                        for j in (2 * i, 2 * i + 1):
                            p = 64 * (j % 2)
                            last = mm(bank[:, j * 64:(j + 1) * 64], g4[s][:, j, 0, :],
                                      rv_tm[:, i, t, p:p + 64], t == 0, True)
                    last.then_inc(psum_filled, 1)
                elif step == "solve":
                    bank = open_bank(pe, "x", l, b)
                    taken(pe, "rhs", l, b)
                    taken(pe, "tt", l, b, 2)
                    for j in range(4):
                        last = mm(bank[:, j * 64:(j + 1) * 64], invT[s][:, j, :], r_rhs[s][:, j, :])
                    last.then_inc(psum_filled, 1)
                elif step == "output":
                    bank = open_bank(pe, "y", l, b)
                    taken(pe, "x", l, b)
                    for i in range(2):
                        if t > 0:
                            mm(bank[:, i * P:(i + 1) * P], S_diag[:, 2 * d + i, :, :], ar[:, d, i, 1, c0:c1],
                               True, False)
                        for j in (2 * i, 2 * i + 1):
                            p = 64 * (j % 2)
                            out = bank[p:p + 64, i * P:(i + 1) * P]
                            mm(out, rv_tm[:, i, t, p:p + 64], g4[s][:, j, 1, :], t == 0, False)
                            last = mm(out, x_sol[s][:, j, :], g4[s][:, j, 3, :], False, True)
                    last.then_inc(psum_filled, 1)
                elif step == "factors":
                    bank = open_bank(pe, "kbt", l, b)
                    for i in range(2):
                        tr(bank[:, (2 * i) * P:(2 * i + 1) * P], kb[:, 0, d, i, c0:c1])
                        last = tr(bank[:, (2 * i + 1) * P:(2 * i + 2) * P], kb[:, 1, d, i, c0:c1])
                    last.then_inc(psum_filled, 1)
                elif step == "state":
                    bank = open_bank(pe, "st", l, b)
                    taken(pe, "kbt", l, b)
                    for j in range(4):
                        i, p = j // 2, 64 * (j % 2)
                        out = bank[p:p + 64, i * 64:(i + 1) * 64]
                        mm(out, kb_tm[s][:, 2 * i, p:p + 64], rv_tm[:, i, t, p:p + 64], True, False)
                        last = mm(out, kb_tm[s][:, 2 * i + 1, p:p + 64], x_sol[s][:, j, :], False, True)
                    last.then_inc(psum_filled, 1)

            def rwkv_norm(l):
                for i in range(2):
                    bank = open_bank(pe, "gnm", l, i)
                    pe.wait_ge(gn_in_ready, l + 1)
                    mm(bank[:, 0:W], C("head"), y_rw[:, i, :]).then_inc(psum_filled, 1)
                for i in range(2):
                    bank = open_bank(pe, "gnv", l, i)
                    pe.wait_ge(gn_sq_ready, l + 1)
                    mm(bank[:, 0:W], C("head"), sq[:, i, :]).then_inc(psum_filled, 1)

            def ssd(l):
                fill(l, "ssd")
                bank = open_bank(pe, "dtt", l)
                pe.wait_ge(cs_ready, l + 1)
                for t in range(TILES):
                    for k, src in ((0, dt_t), (1, cs)):
                        c = (2 * t + k) * DT_ROWS
                        last = tr(bank[:, c:c + DT_ROWS], src[0:DT_ROWS, COL[t]:COL[t] + P], DT_ROWS)
                last.then_inc(psum_filled, 1)
                for r in range(8):
                    bank = open_bank(pe, "cs", l, r)
                    row = 32 * (r // 4) + r % 4
                    pick = C("ident")[0:DT_ROWS, row:row + 1].broadcast_to([DT_ROWS, P])
                    mm(bank[:, 0:W], pick, cs[0:DT_ROWS, :]).then_inc(psum_filled, 1)
                for t in range(TILES):
                    bank = open_bank(pe, "xt", l, t)
                    pe.wait_ge(silu_ready, l + 1)
                    for i in range(3):
                        last = tr(bank[:, i * P:(i + 1) * P], u[:, UX + i, 1 + COL[t]:1 + COL[t] + P])
                    last.then_inc(psum_filled, 1)
                    for g in range(2):
                        bank = open_bank(pe, "gt", l, t, g)
                        p = 64 * g
                        mm(bank[:, 0:P], u[p:p + 64, UB, 1 + COL[t]:1 + COL[t] + P],
                           u[p:p + 64, UC, 1 + COL[t]:1 + COL[t] + P]).then_inc(psum_filled, 1)
                for s, (t, d) in enumerate(SSD_STATES):
                    bank = open_bank(pe, "hst", l, s)
                    pe.wait_ge(xdd_ready, l + 1)
                    for g in range(2):
                        p = 64 * g
                        last = mm(bank[p:p + 64, 0:P], x_tm[:, t, 2 * P + p:2 * P + p + 64],
                                  xdd[:, s, 2 * g:2 * g + 2, :])
                    last.then_inc(psum_filled, 1)
                fill(l, "ys")
                for t in range(TILES):
                    c0, c1 = COL[t], COL[t] + P
                    if t == 0:
                        taken(pe, "gt", l, 2, 1)
                    if t == 1:
                        taken(pe, "hst", l, 3)
                    for g in range(2):
                        bank = open_bank(pe, "ys", l, t, g)
                        for hh in range(2):
                            h, p = 2 * g + hh, 64 * hh
                            out = bank[p:p + 64, 0:P]
                            for d in range(2):
                                r = 4 * d + h
                                last = mm(out, xdt[:, t, d, h, :], le[:, r, c0:c1], d == 0, d == 1 and t == 0)
                            if t > 0:
                                for d in range(2):
                                    r, q = 4 * d + h, 64 * g
                                    first = t == 1 + d
                                    src = shaped(Lp("sssd"), 4, 64) if first else h_mid
                                    hs = src[q:q + 64, 2 * d + hh, :]
                                    last = mm(out, hs, ce[q:q + 64, r, (t - 1) * P:t * P], False, d == 1)
                        last.then_inc(psum_filled, 1)
                bank = open_bank(pe, "yms", l)
                pe.wait_ge(gated_sq_ready, l + 1)
                for i in range(2):
                    last = mm(bank[:, 0:W], C("ones"), sq[:, i, :], i == 0, i == 1)
                last.then_inc(psum_filled, 1)

            def out_projection(l):
                taken(pe, "pv", l, 2)
                pe.wait_ge(mix_ready, l + 1)
                for n in range(KT):
                    if n % 2 == 0:
                        item = next_item()
                    bank = open_bank(pe, "out", l, n)
                    project(item, (n % 2) * KT * P, o, KT, bank[:, 0:W]).then_inc(psum_filled, 1)

            def moe(l):
                bank = open_bank(pe, "lg", l)
                rw_ = shaped(C("router"), KT, 16)
                for t in range(TILES):
                    for k in range(KT):
                        if t == 0:
                            pe.wait_ge(h_ready, KT * (2 * l + 1) + k + 1)
                        last = mm(bank[:, 16 * t:16 * t + 16], hT[:, k, COL[t]:COL[t] + P], rw_[:, k, :],
                                  k == 0, k == KT - 1)
                last.then_inc(psum_filled, 1)
                for t in range(TILES):
                    for k in range(2):
                        bank = open_bank(pe, "hm", l, t, k)
                        for i in range(4):
                            last = tr(bank[:, i * P:(i + 1) * P], hT[:, 4 * k + i, COL[t]:COL[t] + P])
                        last.then_inc(psum_filled, 1)
                bank = open_bank(pe, "pos", l)
                pe.wait_ge(assigned_ready, l + 1)
                for t in range(TILES):
                    for i in range(t):
                        mm(bank[:, 16 * t:16 * t + 16], C("ones"), rt[:, 16, 16 * i:16 * i + 16], i == 0, False)
                    mm(bank[:, 16 * t:16 * t + 16], C("rw0")[:, 0:P], rt[:, 16, 16 * t:16 * t + 16], t == 0, True)
                for i in range(TILES):
                    last = mm(bank[:, 48:64], C("ones"), rt[:, 16, 16 * i:16 * i + 16], i == 0, i == 2)
                last.then_inc(psum_filled, 1)
                fill(l, "rows")

                def transposed(b):
                    for k in range(2):
                        bank = open_bank(pe, "xb", l, b, k)
                        if k == 0 and b < GATHERED:
                            pe.wait_ge(picks_ready, l + 1)
                            taken(pe, "hm", l, TILES - 1, 1)
                        elif k == 0:
                            pe.wait_ge(xb_loaded[b % 2], 16 * (loads_before(l, b) + 1))
                        for i in range(4):
                            c = (4 * k + i) * P
                            out = bank[:, i * SLOT:(i + 1) * SLOT]
                            if b < GATHERED:
                                for t in range(TILES):
                                    last = mm(out, h_tm[:, t, c:c + P], picks[:, t, b * SLOT:(b + 1) * SLOT],
                                              t == 0, t == TILES - 1)
                            else:
                                last = tr(out, xb[b % 2][0:SLOT, c:c + P], SLOT)
                        last.then_inc(psum_filled, 1)

                def expert_block(b):
                    for name in ("gate", "up"):
                        item = next_item()
                        bank = open_bank(pe, name, l, b)
                        if name == "gate":
                            taken(pe, "xb", l, b, 1)
                        for f in range(2):
                            last = project(item, f * KT * P, xbT[b % 2], KT, bank[:, f * SLOT:(f + 1) * SLOT])
                        last.then_inc(psum_filled, 1)
                    if b + 1 < BLOCKS:
                        transposed(b + 1)
                    item = next_item()
                    for k in range(2):
                        bank = open_bank(pe, "down", l, b, k)
                        if k == 0:
                            taken(pe, "up", l, b)
                        for f in range(2):
                            last = mm(bank[0:SLOT, :], hid[b % 2][:, f, :],
                                      item[:, f * D + k * 512:f * D + (k + 1) * 512], f == 0, f == 1)
                        last.then_inc(psum_filled, 1)

                transposed(0)
                used = blocks_used(pe, l)
                for b in range(EXPERTS):
                    expert_block(b)
                for b in range(EXPERTS, BLOCKS):
                    with pe.If(used > b):
                        expert_block(b)
                    with pe.Else():
                        first, end = block_groups(l, b)
                        pe.wait_ge(psum_filled, first)
                        for consumer in "av":
                            pe.wait_ge(psum_read[consumer], reads_before(consumer, first))
                        pe.nop().then_inc(psum_filled, end - first)
                for t in range(TILES):
                    for k in range(2):
                        bank = open_bank(pe, "yt", l, t, k)
                        if k == 0:
                            pe.wait_ge(y_summed, TILES * l + t + 1)
                        for i in range(4):
                            c = (4 * k + i) * P
                            last = tr(bank[:, i * P:(i + 1) * P], y1[:, t, c:c + P])
                        last.then_inc(psum_filled, 1)

            for l in range(DEPTH):
                fill(l, "start")
                mean_square(l, 1)
                in_projection(l)
                attention(l)
                rwkv_inputs(l)
                fill(l, "batches")
                for step, b in RW_ORDER:
                    rwkv_step(l, step, b)
                rwkv_norm(l)
                ssd(l)
                out_projection(l)
                mean_square(l, 2)
                moe(l)
            assert opened[0] == len(plan)

        @block.scalar
        def _(act):
            chain = [0]

            def link(ins):
                chain[0] += 1
                ins.then_inc(chain_a, 1)
                act.wait_ge(chain_a, chain[0])

            def f(out, in_, func, **kw):
                return nc.scalar.activation(out, in_, func, **kw)

            def root(out, n, eps, *key):
                bank = filled(act, *key)
                f(out, bank[:, 0:W], ACT.Sqrt, bias=C(eps), scale=1.0 / n).then_inc(read(*key), 1)

            def fill(l, place):
                for ml, c in MOD_SCHEDULE[l, place]:
                    bank = filled(act, "mod", ml, c)
                    f(mod_rows[c % 2][0:2, :], bank[0:2, :], ACT.Copy).then_inc(read("mod", ml, c), 1)

            def squares(l, which):
                if which == 2:
                    for n in range(KT):
                        taken(act, "out", l, n)
                        f(sq[:, n, :], xT[:, n, :], ACT.Square).then_inc(xsq_ready, 1)
                elif l:
                    for t, (lo, hi) in enumerate(((0, LAT), (LAT, COL[2]), (COL[2], W))):
                        taken(act, "yt", l - 1, t, 1)
                        last = f(sq[:, :, lo:hi], xT[:, :, lo:hi], ACT.Square)
                    last.then_inc(xsq_ready, KT)
                else:
                    act.wait_ge(consts_loaded, 16)
                    act.wait_ge(x_loaded, 16)
                    f(sq, xT, ACT.Square).then_inc(xsq_ready, KT)
                root(tmp[:, 0:W], D, "eps", "ms", l, which)
                fill(l, f"norm{which}")
                first = 0 if which == 1 else 24
                for k in range(KT):
                    act.wait_ge(h_scaled, KT * (2 * l + which - 1) + k + 1)
                    for g, lo, hi in SEGMENTS:
                        last = f(hT[:, k, lo:hi], hT[:, k, lo:hi], ACT.Identity,
                                 bias=mod[:, first + k, g:g + 1])
                    last.then_inc(h_ready, 1)

            def after_u(l, step):
                if step == "qk_squares":
                    for i in range(5):
                        root(qn[:, i, :], 64, "eps", "qkms", l, i)
                elif step == "v_columns":
                    bank = filled(act, "vt", l)
                    f(v_tm, shaped(bank[:, 0:3 * P], 3, P), ACT.Copy).then_inc(read("vt", l), 1)

            def attention(l):

                def exps(t):
                    n, c = (3 * P if t else P), 64 * t
                    for h in range(8):
                        if h % 4 == 0:
                            act.wait_ge(shifted_ready, 2 * (TILES * l + t) + h // 4 + 1)
                            f(att_cols[:, c + 32 + h:c + 36 + h], att_cols[:, c + 24 + h:c + 28 + h], ACT.Exp)
                        last = f(scores[t % 2][:, h, 0:n], scores[t % 2][:, h, 0:n], ACT.Exp,
                                 bias=att_cols[:, c + 8 + h:c + 9 + h],
                                 accum_out=att_cols[:, c + 16 + h:c + 17 + h])
                        if h % 4 == 3:
                            last.then_inc(exps_ready, 1)

                def copies(t):
                    n = 3 * P if t else P
                    if t:
                        filled(act, "pv", l, t - 1)
                    for h in range(8):
                        bank = filled(act, "pT", l, t, h)
                        f(probsT[:, h, 0:n], bank[:, 0:n], ACT.Copy).then_inc(read("pT", l, t, h), 1)
                    bank = filled(act, "pv", l, t)
                    f(o[:, 0:4, COL[t]:COL[t] + P], shaped(bank[:, :], 4, P), ACT.Copy)\
                        .then_inc(read("pv", l, t), 1)

                for step, t in ATT_STEPS:
                    if step == "scores":
                        exps(t)
                        if t == 0:
                            fill(l, "sc0")
                    else:
                        copies(t)
                        fill(l, f"pv{t}")

            def rwkv_inputs(l):
                for name, out, bias in (("wl", sgw, "w0"), ("al", asig, "a0")):
                    for d in range(2):
                        for i in range(2):
                            bank = filled(act, name, l, d, i)
                            k = 2 * d + i
                            f(out[:, k, :], bank[:, 0:W], ACT.Sigmoid, bias=Lc(bias, k))\
                                .then_inc(read(name, l, d, i), 1)
                for i in range(2):
                    bank = filled(act, "gg", l, i)
                    f(gate_rw[:, i, :], bank[:, 0:W], ACT.Copy).then_inc(read("gg", l, i), 1)
                for i in range(2):
                    root(tmp[:, i * W:(i + 1) * W], 1, "eps_kk", "kkn", l, i)
                for i in range(2):
                    bank = filled(act, "rvt", l, i)
                    f(rv_tm[:, i, :, :], shaped(bank[:, 0:3 * P], 3, P), ACT.Copy).then_inc(read("rvt", l, i), 1)
                act.wait_ge(decay_arg_ready, l + 1)
                for d in range(2):
                    Dd, Fd = csum[:, 2 * d:2 * d + 2, :], sgw[:, 2 * d:2 * d + 2, :]
                    incl, excl, s = (Dd, Fd, -DECAY) if d == 0 else (Fd, Dd, DECAY)
                    f(ar[:, d, :, 0, :], excl, ACT.Exp, scale=s)
                    f(ar[:, d, :, 1, :], incl, ACT.Exp, scale=s)
                    f(kb[:, 0, d, :, :], incl, ACT.Exp, scale=-s)
                f(decay_half, half_total, ACT.Exp, scale=DECAY).then_inc(decay_exp_ready, 1)

            def ssd_steps(l):
                z = dt_t[0:DT_ROWS, :]
                raw = u[0:DT_ROWS, UDT, 1:W + 1]
                b1 = Lc("dtb", 0, slice(0, DT_ROWS))
                taken(act, "u", l, UDT)
                link(f(dta[0:DT_ROWS, :], raw, ACT.Abs, bias=b1))
                f(z, raw, ACT.Relu, bias=b1)
                f(neg_a[0:DT_ROWS, 0:1], Lc("alog", 0, slice(0, DT_ROWS)), ACT.Exp)
                link(f(dta[0:DT_ROWS, :], dta[0:DT_ROWS, :], ACT.Exp, scale=-1.0))
                f(dta[0:DT_ROWS, :], dta[0:DT_ROWS, :], ACT.Ln, bias=1.0).then_inc(dt_parts, 1)

            def rwkv_step(l, step, b):
                s = b % 2
                kind, k = step[:5], step[-1]

                def copy(out, *key):
                    bank = filled(act, *key)
                    n = out.shape[1] * out.shape[2]
                    f(out, shaped(bank[:, 0:n], out.shape[1], out.shape[2]), ACT.Copy).then_inc(read(*key), 1)
                if kind == "power" and k != "4":
                    filled(act, "pt", l, b, int(k))
                    copy(pw[s], "p", l, b, int(k))
                    copy(pwT[s], "pt", l, b, int(k))
                elif step == "transpose":
                    copy(invT[s], "tT", l, b)
                elif step == "rhs":
                    copy(r_rhs[s], "rhs", l, b)
                elif step == "factors":
                    copy(kb_tm[s], "kbt", l, b)

            def ssd(l):
                taken(act, "y", l, len(RW_BATCHES) - 1)
                bank = filled(act, "dtt", l)
                f(dtc, bank[:, 0:6 * DT_ROWS].rearrange("p (t k r) -> p t k r", t=TILES, k=2), ACT.Copy)\
                    .then_inc(read("dtt", l), 1)
                for r in range(8):
                    bank = filled(act, "cs", l, r)
                    f(le[:, r, :], bank[:, 0:W], ACT.Copy).then_inc(read("cs", l, r), 1)
                taken(act, "cs", l, 7)
                f(ce, le[:, :, LAT:W], ACT.Exp).then_inc(lat_decay_ready, 1)
                for t in range(TILES):
                    bank = filled(act, "xt", l, t)
                    f(x_tm[:, t, :], bank[:, 0:3 * P], ACT.Copy).then_inc(read("xt", l, t), 1)
                act.wait_ge(din_arg_ready, l + 1)
                f(decay_in, decay_in, ACT.Exp)
                f(chunk_decay, total_b, ACT.Exp).then_inc(din_ready, 1)
                act.wait_ge(le_arg_ready, l + 1)
                f(le, le, ACT.Exp).then_inc(le_ready, 1)
                fill(l, "ys")

            def moe(l):
                bank = filled(act, "lg", l)
                f(rt[:, 1, :], bank[:, 0:48], ACT.Sigmoid).then_inc(read("lg", l), 1)
                for t in range(TILES):
                    for k in range(2):
                        bank = filled(act, "hm", l, t, k)
                        f(h_tm[:, t, 512 * k:512 * k + 512], bank[:, :], ACT.Copy).then_inc(read("hm", l, t, k), 1)
                fill(l, "rows")

                def copy_block(b):
                    for k in range(2):
                        bank = filled(act, "xb", l, b, k)
                        f(xbT[b % 2][:, 4 * k:4 * k + 4, :], shaped(bank[:, 0:4 * SLOT], 4, SLOT), ACT.Copy)\
                            .then_inc(read("xb", l, b, k), 1)

                def expert_block(b):
                    bank = filled(act, "gate", l, b)
                    if b:
                        taken(act, "up", l, b - 1)
                    f(sg, bank[:, 0:2 * SLOT], ACT.Silu).then_inc(read("gate", l, b), 1)
                    if b + 1 < BLOCKS:
                        copy_block(b + 1)
                    bank = filled(act, "down", l, b, 0)
                    if b >= 2:
                        wait_stored(act, l, b - 2)
                    f(ye[b % 2][0:SLOT, 0:512], bank[0:SLOT, :], ACT.Copy).then_inc(read("down", l, b, 0), 1)

                copy_block(0)
                used = blocks_used(act, l)
                for b in range(EXPERTS):
                    expert_block(b)
                for b in range(EXPERTS, BLOCKS):
                    with act.If(used > b):
                        expert_block(b)
                    with act.Else():
                        skip_reads(act, "a", l, b)

            act.wait_ge(cond_loaded, 16)
            f(scond[:, :], cond[:, :], ACT.Silu).then_inc(cond_ready, 1)
            for l in range(DEPTH):
                fill(l, "start")
                squares(l, 1)
                if l == 0:
                    act.wait_ge(gaps_cleared, 1)
                for c in range(U_TILES):
                    if c % 2:
                        bank = filled(act, "u", l, c)
                        m = DT_ROWS if c == UDT else P
                        f(u[0:m, c, 1:W + 1], bank[0:m, 0:W], ACT.Copy).then_inc(read("u", l, c), 1)
                    if c == UK + 1:
                        for i in range(5):
                            taken(act, "u", l, i)
                        f(sq[:, 0:5, :], u[:, 0:5, 1:W + 1], ACT.Square).then_inc(qk_sq_ready, 1)
                    after_u(l, AFTER_U.get(c))
                act.wait_ge(conv_ready, l + 1)
                f(u[:, UX:UDT, 1:W + 1], conv, ACT.Silu).then_inc(silu_ready, 1)
                f(u[:, UZ:UZ + 2, 1:W + 1], u[:, UZ:UZ + 2, 1:W + 1], ACT.Silu).then_inc(z_ready, 1)
                act.wait_ge(mixed_ready, l + 1)
                f(mixed_lora[0:32, 0, :], mixed_lora[0:32, 0, :], ACT.Tanh)
                f(mixed_lora[64:P, 0, :], mixed_lora[64:P, 0, :], ACT.Sigmoid).then_inc(lora_ready, 1)
                attention(l)
                rwkv_inputs(l)
                ssd_steps(l)
                fill(l, "batches")
                for step, b in RW_ORDER:
                    rwkv_step(l, step, b)
                for i in range(2):
                    root(tmp[:, i * W:(i + 1) * W], 64, "eps_gn", "gnv", l, i)
                fill(l, "ssd")
                ssd(l)
                root(tmp[:, 0:W], 256, "eps", "yms", l)
                squares(l, 2)
                moe(l)

        @block.vector
        def _(dve):
            v = nc.vector
            chain = [0]

            def link(ins):
                chain[0] += 1
                ins.then_inc(chain_v, 1)
                dve.wait_ge(chain_v, chain[0])

            def tt(out, x, y, op):
                return v.tensor_tensor(out, x, y, op)

            def stt(out, x, s, y, op0, op1):
                return v.scalar_tensor_tensor(out, x, s, y, op0, op1)

            def ts(out, x, s1, s2, op0, op1=None):
                return v.tensor_scalar(out, x, s1, s2, op0, op1) if op1 is not None else \
                    v.tensor_scalar(out, x, s1, None, op0)

            def norm(l, which):
                scale = scale1 if which == 1 else scale2
                taken(dve, "ms", l, which)
                if which == 1:
                    v.memset(hT[:, :, P:LAT], 0.0)
                link(v.reciprocal(tmp[:, 0:W], tmp[:, 0:W]))
                fill(l, f"norm{which}")
                for k in range(KT):
                    for g, lo, hi in SEGMENTS:
                        last = stt(hT[:, k, lo:hi], xT[:, k, lo:hi], scale[:, k, g:g + 1], tmp[:, lo:hi],
                                   ALU.mult, ALU.mult)
                    last.then_inc(h_scaled, 1)

            def fill(l, place):
                for ml, c in MOD_SCHEDULE[l, place]:
                    bank = filled(dve, "modT", ml, c)
                    out = mod[:, 4 * c:4 * c + 4, :]
                    bm = bc(C(f"bmod{ml}")[:, 4 * c:4 * c + 4], 2, 2)
                    tt(out, shaped(bank[:, 0:8], 4, 2), bm, ALU.add).then_inc(read("modT", ml, c), 1)
                    for scale, name, last_chunk in ((scale1, "n1", 3), (scale2, "n2", 9)):
                        if c == last_chunk:
                            taken(dve, "modT", ml, c)
                            sc = mod[:, 4 * c - 4:4 * c + 4, :]
                            link(stt(scale, sc, 1.0, bc(C(f"{name}_{ml}"), 2, 2), ALU.add, ALU.mult))

            def qk_norm(l):
                for i in range(5):
                    taken(dve, "qkms", l, i)
                    link(v.reciprocal(qn[:, i, :], qn[:, i, :]))
                    stt(qn[:, i, :], u[:, i, 1:W + 1], Lc("kw" if i == 4 else "qw", 0), qn[:, i, :],
                        ALU.mult, ALU.mult).then_inc(qn_ready, 1)
                dve.wait_ge(qn_ready, 5 * (l + 1))
                v.tensor_copy(new_k[l][:, :], qn[:, 4, 0:P]).then_inc(kv_copied, 1)
                taken(dve, "u", l, UV)
                v.tensor_copy(new_v[l][:, :], u[:, UV, 1:P + 1]).then_inc(kv_copied, 1)

            def rotation(l):
                for i in range(5):
                    bank = filled(dve, "rope", l, i)
                    link(tt(tmp[:, 0:2 * P], bank[:, 0:2 * P], C("sin"), ALU.mult))
                    tt(qn[:, i, LAT:W], qn[:, i, LAT:W], C("cos"), ALU.mult).then_inc(read("rope", l, i), 1)
                    taken(dve, "rope", l, i)
                    last = tt(qn[:, i, LAT:W], qn[:, i, LAT:W], tmp[:, 0:2 * P], ALU.add)
                    if i < 4:
                        link(last)
                last.then_inc(rope_ready, 1)

            def attention(l):
                if l == 0:
                    dve.wait_ge(slots_cleared, 32)

                def maxima(t):
                    n, c = (3 * P if t else P), 64 * t
                    sc = scores[t % 2]
                    if t == 2:
                        filled(dve, "pT", l, 0, 7)
                    for h in range(8):
                        bank = filled(dve, "sc", l, t, h)
                        scale = 64 ** -0.5
                        if t:
                            cut, whole = (1, slice(0, 3, 2)) if t == 1 else (0, slice(1, 3))
                            src, out = shaped(bank[:, 0:3 * P], 3, P), shaped(sc[:, h, 0:3 * P], 3, P)
                            stt(out[:, cut, :], src[:, cut, :], scale, C(f"ssd{2 - t}"), ALU.mult, ALU.add)
                            last = ts(out[:, whole, :], src[:, whole, :], scale, None, ALU.mult)
                        else:
                            last = ts(sc[:, h, 0:P], bank[:, 0:P], scale, None, ALU.mult)
                        last.then_inc(read("sc", l, t, h), 1)
                        if h % 4 < 3:
                            continue
                        taken(dve, "sc", l, t, h)
                        h0 = h - 3
                        top, sink = att_cols[:, c + h0:c + h0 + 4], Lp("sink")[:, h0:h0 + 4]
                        link(v.tensor_reduce(top, sc[:, h0:h0 + 4, 0:n], X, ALU.max))
                        link(tt(top, top, sink, ALU.max))
                        ts(att_cols[:, c + 8 + h0:c + 12 + h0], top, -1.0, None, ALU.mult)
                        tt(att_cols[:, c + 24 + h0:c + 28 + h0], sink, top, ALU.subtract)\
                            .then_inc(shifted_ready, 1)

                def probabilities(t):
                    n, c = (3 * P if t else P), 64 * t
                    sc = scores[t % 2]
                    for i in range(2):
                        h = c + 4 * i
                        dve.wait_ge(exps_ready, 2 * (TILES * l + t) + i + 1)
                        link(tt(att_cols[:, h + 40:h + 44], att_cols[:, h + 16:h + 20],
                                att_cols[:, h + 32:h + 36], ALU.add))
                        link(v.reciprocal(att_cols[:, h + 48:h + 52], att_cols[:, h + 40:h + 44]))
                        part = sc[:, 4 * i:4 * i + 4, 0:n]
                        tt(part, part, bc(att_cols[:, h + 48:h + 52], 2, n), ALU.mult).then_inc(probs_ready, 1)

                for step, t in ATT_STEPS:
                    if step == "scores":
                        maxima(t)
                        if t == 0:
                            fill(l, "sc0")
                    else:
                        probabilities(t)
                        fill(l, f"pv{t}")

            def token_shift(l):
                for c in range(UR, UR + 7):
                    taken(dve, "u", l, c)
                keep = cols[:, 0:7]
                link(tt(keep, Lp("mu0"), Lp("mu1"), ALU.add))
                link(ts(keep, keep, -1.0, 1.0, ALU.mult, ALU.add))
                for j, out in enumerate(mixed_tiles):
                    last = ts(out, u[:, UR + j, 1:W + 1], cols[:, j:j + 1], None, ALU.mult)
                link(last)
                for j, out in enumerate(mixed_tiles):
                    last = stt(out, u[:, UR + j, 0:W], Lc("mu0", j), out, ALU.mult, ALU.add)
                link(last)
                for j, out in enumerate(mixed_tiles):
                    last = stt(out, u[:, UR + j, 2:W + 2], Lc("mu1", j), out, ALU.mult, ALU.add)
                last.then_inc(mixed_ready, 1)

            def rwkv_inputs(l):
                taken(dve, "pv", l, 2)
                dve.wait_ge(mixed_ready, l + 1)
                for i in range(2):
                    ts(kdir[:, i, :], mixed_k[:, i, :], Lc("kk", i), None, ALU.mult)
                    last = stt(sq[:, 2 + i, :], mixed_r[:, i, :], Lc("rk", i), mixed_k[:, i, :],
                               ALU.mult, ALU.mult)
                last.then_inc(bonus_in_ready, 1)
                dve.wait_ge(bonus_in_ready, l + 1)
                tt(sq[:, 0:2, :], kdir, kdir, ALU.mult).then_inc(kk_sq_ready, 1)
                taken(dve, "kkn", l, 1)
                link(v.reciprocal(tmp[:, :], tmp[:, :]))
                link(tt(kdir, kdir, shaped(tmp[:, :], 2, W), ALU.mult))
                for i in range(2):
                    bank = filled(dve, "bon", l, i)
                    tt(bonus[:, i, :], bank[:, 0:W], mixed_v[:, i, :], ALU.mult).then_inc(read("bon", l, i), 1)
                for k in range(4):
                    taken(dve, "wl", l, k // 2, k % 2)
                    last = v.tensor_tensor_scan(csum[:, k, :], C("restart"), sgw[:, k, :], 0.0, ALU.mult, ALU.add)
                link(last)
                for t in range(TILES):
                    e = COL[t] + P - 1
                    last = ts(half_total[:, :, t:t + 1], csum[:, :, e:e + 1], -0.5, None, ALU.mult)
                link(last)
                for t in range(TILES):
                    c0 = COL[t]
                    last = tt(csum[:, :, c0:c0 + P], csum[:, :, c0:c0 + P],
                              half_total[:, :, t:t + 1].broadcast_to([P, 4, P]), ALU.add)
                link(last)
                tt(sgw, csum, sgw, ALU.subtract).then_inc(decay_arg_ready, 1)
                taken(dve, "al", l, 1, 1)
                for d in range(2):
                    last = stt(kb[:, 1, d, :, :], kdir, -1.0, asig[:, 2 * d:2 * d + 2, :], ALU.mult, ALU.mult)
                link(last)
                link(ts(cols[:, 8:10], Lp("ka"), -1.0, 1.0, ALU.mult, ALU.add))
                for k in range(4):
                    last = ts(asig[:, k, :], asig[:, k, :], Lc("ka", k % 2), cols[:, 8 + k % 2:9 + k % 2],
                              ALU.mult, ALU.add)
                link(last)
                for d in range(2):
                    last = tt(asig[:, 2 * d:2 * d + 2, :], asig[:, 2 * d:2 * d + 2, :], mixed_k, ALU.mult)
                link(last)
                dve.wait_ge(decay_exp_ready, l + 1)
                for d in range(2):
                    tt(ar[:, d, :, 0, :], ar[:, d, :, 0, :], kdir, ALU.mult)
                    tt(ar[:, d, :, 1, :], ar[:, d, :, 1, :], mixed_r, ALU.mult)
                    last = tt(kb[:, 1, d, :, :], kb[:, 1, d, :, :], kb[:, 0, d, :, :], ALU.mult)
                link(last)
                for d in range(2):
                    last = tt(kb[:, 0, d, :, :], kb[:, 0, d, :, :], asig[:, 2 * d:2 * d + 2, :], ALU.mult)
                last.then_inc(factors_ready, 1)
                dve.wait_ge(factors_ready, l + 1)

            def scale_state(t, d, src):
                for i in range(2):
                    k = 2 * d + i
                    ts(S_til[:, k, :], src[:, k, :], decay_half[:, k, t:t + 1], None, ALU.mult)
                    for half in range(2):
                        q = slice(64 * half, 64 * half + 64)
                        last = ts(S_diag[q, k, half, :], src[q, k, :], decay_half[q, k, t:t + 1], None, ALU.mult)
                return last

            def rwkv_step(l, step, b):
                t, d = RW_BATCHES[b]
                s = b % 2
                kind, k = step[:5], step[-1]
                if step == "matrices":
                    if t > 0:
                        src = shaped(Lp("srw"), 4, 64) if b < STATE_BATCHES else S_lat
                        scale_state(t, d, src).then_inc(state_ready, 1)
                    if b == 0:
                        v.memset(S_diag, 0.0)
                    for j in range(4):
                        bank = filled(dve, "g4", l, b, j)
                        tt(g4[s][:, j, :, :], shaped(bank[:, :], 4, P), shaped(C(f"rw{d}"), 4, P), ALU.mult)\
                            .then_inc(read("g4", l, b, j), 1)
                    for half in range(2):
                        bank = filled(dve, "nd", l, b, half)
                        tt(pw[s][:, half::2, :], shaped(bank[:, 0:2 * P], 2, P), bc(C(f"nd{d}"), 1, 2), ALU.mult)\
                            .then_inc(read("nd", l, b, half), 1)
                    taken(dve, "nd", l, b, 1)
                    tt(pwT[s], g4[s][:, :, 2, :], bc(C("inv")[:, 0:P], 1, 4), ALU.mult)
                    tt(inv[s], pw[s], bc(C("ident"), 1, 4), ALU.add).then_inc(matrices_ready, 1)
                elif kind == "power" and k != "1":
                    bank = filled(dve, "t", l, b, int(k))
                    if k == "2":
                        dve.wait_ge(matrices_ready, len(RW_BATCHES) * l + b + 1)
                    else:
                        taken(dve, "t", l, b, int(k) - 1)
                    tt(inv[s], inv[s], shaped(bank[:, :], 4, P), ALU.add).then_inc(read("t", l, b, int(k)), 1)
                elif kind == "cross":
                    k = int(k)
                    bank = filled(dve, "cross", l, b, k)
                    mask = C("inv")[:, (1 + k) * P:(2 + k) * P]
                    tt(cross[s], shaped(bank[:, :], 4, P), bc(mask, 1, 4), ALU.mult)\
                        .then_inc(read("cross", l, b, k), 1)
                elif kind == "merge":
                    k = int(k)
                    if k < 2:
                        bank = filled(dve, "t", l, b, 5 + k)
                        taken(dve, "t", l, b, 4 + k)
                        tt(inv[s], inv[s], shaped(bank[:, :], 4, P), ALU.add).then_inc(read("t", l, b, 5 + k), 1)
                    bank = filled(dve, "tt", l, b, k)
                    if k:
                        taken(dve, "tt", l, b, k - 1)
                    else:
                        taken(dve, "tT", l, b)
                    tt(invT[s], invT[s], shaped(bank[:, :], 4, P), ALU.add).then_inc(read("tt", l, b, k), 1)
                elif step == "solve":
                    bank = filled(dve, "x", l, b)
                    v.tensor_copy(x_sol[s], shaped(bank[:, 0:256], 4, 64)).then_inc(read("x", l, b), 1)
                elif step == "output":
                    bank = filled(dve, "y", l, b)
                    src, out = shaped(bank[:, 0:2 * P], 2, P), y_rw[:, :, COL[t]:COL[t] + P]
                    if b in (0, 2, 3):
                        last = v.tensor_copy(out, src)
                    else:
                        taken(dve, "y", l, {1: 0, 4: 3, 5: 2}[b])
                        last = tt(out, out, src, ALU.add)
                    last.then_inc(read("y", l, b), 1)
                elif step == "state":
                    bank = filled(dve, "st", l, b)
                    if t > 0:
                        link(tt(S_lat[:, 2 * d:2 * d + 2, :], S_til[:, 2 * d:2 * d + 2, :],
                                shaped(bank[:, 0:P], 2, 64), ALU.add))
                    for i in range(2):
                        k = 2 * d + i
                        x = S_lat[:, k, :] if t > 0 else bank[:, i * 64:(i + 1) * 64]
                        out = S_lat[:, k, :] if t > 0 else state_rw[l][:, k, :]
                        last = ts(out, x, decay_half[:, k, t:t + 1], None, ALU.mult)
                    last.then_inc(read("st", l, b), 1)
                    taken(dve, "st", l, b)

            def rwkv_norm(l):
                last = v.memset(y_rw[:, :, P:LAT], 0.0)
                last.then_inc(gn_in_ready, 1)
                dve.wait_ge(gn_in_ready, l + 1)
                for i in range(2):
                    bank = filled(dve, "gnm", l, i)
                    stt(y_rw[:, i, :], bank[:, 0:W], -1.0 / 64, y_rw[:, i, :], ALU.mult, ALU.add).then_inc(read("gnm", l, i), 1)
                taken(dve, "gnm", l, 1)
                tt(sq[:, 0:2, :], y_rw, y_rw, ALU.mult).then_inc(gn_sq_ready, 1)
                taken(dve, "gnv", l, 1)
                link(v.reciprocal(tmp[:, :], tmp[:, :]))
                link(tt(y_rw, y_rw, shaped(tmp[:, :], 2, W), ALU.mult))
                for i in range(2):
                    last = ts(y_rw[:, i, :], y_rw[:, i, :], Lc("lnw", i), Lc("lnb", i), ALU.mult, ALU.add)
                link(last)
                link(tt(y_rw, y_rw, bonus, ALU.add))
                for lo, hi in ((0, P), (LAT, W)):
                    last = tt(o[:, 4:6, lo:hi], y_rw[:, :, lo:hi], gate_rw[:, :, lo:hi], ALU.mult)
                last.then_inc(rwkv_done, 1)
                dve.wait_ge(rwkv_done, l + 1)

            def ssd_convolution(l):
                for c in range(UX, UDT):
                    taken(dve, "u", l, c)
                cw = Lp("cw")
                for j in range(4):
                    last = ts(conv[:, j, :], u[:, UX + j, 1:W + 1], cw[:, 4 + j:5 + j], Lc("cb", j),
                              ALU.mult, ALU.add)
                link(last)
                for j in range(4):
                    last = stt(conv[:, j, :], u[:, UX + j, 0:W], cw[:, j:j + 1], conv[:, j, :], ALU.mult, ALU.add)
                link(last)
                for j in range(4):
                    last = stt(conv[:, j, :], u[:, UX + j, 2:W + 2], cw[:, 8 + j:9 + j], conv[:, j, :],
                               ALU.mult, ALU.add)
                last.then_inc(conv_ready, 1)

            def ssd_steps(l):
                R = slice(0, DT_ROWS)
                dve.wait_ge(dt_parts, l + 1)
                link(tt(dt_t[R, :], dt_t[R, :], dta[R, :], ALU.add))
                link(ts(dta[R, :], dt_t[R, :], neg_a[R, 0:1], -1.0, ALU.mult, ALU.mult))
                link(v.tensor_tensor_scan(cs[R, :], C("restart", R), dta[R, :], 0.0, ALU.mult, ALU.add))
                B = slice(32, 64)
                link(tt(dtmp[B, :], dta[B, :], cs[B, :], ALU.subtract))
                for t in range(TILES):
                    e = COL[t] + P - 1
                    last = v.tensor_copy(cols[B, 16 + t:17 + t], cs[B, e:e + 1])
                link(last)
                for t in range(TILES):
                    c0 = COL[t]
                    last = ts(cs[B, c0:c0 + P], dtmp[B, c0:c0 + P], cols[B, 16 + t:17 + t], None, ALU.add)
                last.then_inc(cs_ready, 1)

            def ssd(l):
                dve.wait_ge(rwkv_done, l + 1)
                taken(dve, "cs", l, 7)
                taken(dve, "dtt", l)
                for t in range(TILES):
                    for d in range(2):
                        e = COL[t] + (P - 1 if d == 0 else 0)
                        last = v.tensor_copy(total_b[:, 4 * d:4 * d + 4, t:t + 1], le[:, 4 * d:4 * d + 4, e:e + 1])
                link(last)
                for t in range(TILES):
                    for d in range(2):
                        last = tt(decay_in[:, t, 4 * d:4 * d + 4], total_b[:, 4 * d:4 * d + 4, t],
                                  dtc[:, t, 1, 32 * d:32 * d + 4], ALU.subtract)
                last.then_inc(din_arg_ready, 1)
                dve.wait_ge(lat_decay_ready, l + 1)
                for r in range(8):
                    d, row = r // 4, 32 * (r // 4) + r % 4
                    for t in range(TILES):
                        last = stt(le[:, r, COL[t]:COL[t] + P], le[:, r, COL[t]:COL[t] + P],
                                   dtc[:, t, 1, row:row + 1], C(f"ssd{d}"), ALU.subtract, ALU.add)
                last.then_inc(le_arg_ready, 1)
                taken(dve, "xt", l, 2)
                for t in range(TILES):
                    xv = x_tm[:, t, 0:2 * P].rearrange("p (h c) -> p h c", h=4)
                    for d in range(2):
                        last = tt(xdt[:, t, d, :, :], xv, bc(dtc[:, t, 0, 32 * d:32 * d + 4], 2, 64), ALU.mult)
                link(last)
                dve.wait_ge(din_ready, l + 1)
                for s, (t, d) in enumerate(SSD_STATES):
                    last = tt(xdd[:, s, :, :], xdt[:, t, d, :, :], bc(decay_in[:, t, 4 * d:4 * d + 4], 2, 64),
                              ALU.mult)
                last.then_inc(xdd_ready, 1)
                dve.wait_ge(silu_ready, l + 1)
                for g in range(2):
                    q = slice(64 * g, 64 * g + 64)
                    for d in range(2):
                        r = 4 * d + 2 * g
                        last = tt(ce[q, r:r + 2, :], ce[q, r:r + 2, :], bc(u[q, UC, 1 + LAT:1 + W], 1, 2), ALU.mult)
                dve.wait_ge(le_ready, l + 1)
                for t in range(TILES):
                    for g in range(2):
                        bank = filled(dve, "gt", l, t, g)
                        for r in (2 * g, 4 + 2 * g):
                            x = le[:, r:r + 2, COL[t]:COL[t] + P]
                            last = tt(x, x, bc(bank[:, 0:P], 1, 2), ALU.mult)
                        last.then_inc(read("gt", l, t, g), 1)
                init = shaped(Lp("sssd"), 4, 64)
                for s, (t, d) in enumerate(SSD_STATES):
                    bank = filled(dve, "hst", l, s)
                    src = shaped(bank[:, 0:P], 2, 64)
                    if t == 0:
                        last = v.tensor_copy(state_ssd[l][:, 2 * d:2 * d + 2, :], src)
                    else:
                        for g in range(2):
                            q = slice(64 * g, 64 * g + 64)
                            for hh in range(2):
                                r = 4 * d + 2 * g + hh
                                last = stt(h_mid[q, 2 * d + hh, :], init[q, 2 * d + hh, :],
                                           chunk_decay[q, r, t:t + 1], src[q, hh, :], ALU.mult, ALU.add)
                    last.then_inc(read("hst", l, s), 1)
                fill(l, "ys")
                for t in range(TILES):
                    for i in range(2):
                        bank = filled(dve, "ys", l, t, i)
                        last = stt(y_ssd[:, i, COL[t]:COL[t] + P], u[:, UX + i, 1 + COL[t]:1 + COL[t] + P],
                                   Lc("dskip", i), bank[:, 0:P], ALU.mult, ALU.add)
                        last.then_inc(read("ys", l, t, i), 1)
                link(v.memset(y_ssd[:, :, P:LAT], 0.0))
                dve.wait_ge(z_ready, l + 1)
                link(tt(y_ssd, y_ssd, u[:, UZ:UZ + 2, 1:W + 1], ALU.mult))
                tt(sq[:, 0:2, :], y_ssd, y_ssd, ALU.mult).then_inc(gated_sq_ready, 1)
                taken(dve, "yms", l)
                link(v.reciprocal(tmp[:, 0:W], tmp[:, 0:W]))
                for i in range(2):
                    for lo, hi in ((0, P), (LAT, W)):
                        last = stt(o[:, 6 + i, lo:hi], y_ssd[:, i, lo:hi], Lc("nw", i), tmp[:, lo:hi],
                                   ALU.mult, ALU.mult)
                last.then_inc(mix_ready, 1)

            def add_gated(bank, n, first):
                for g, lo, hi in SEGMENTS:
                    last = stt(xT[:, n, lo:hi], bank[:, lo:hi], mod[:, first + n, g:g + 1], xT[:, n, lo:hi],
                               ALU.mult, ALU.add)
                return last

            def routing(l):
                taken(dve, "lg", l)
                s = rt[:, 1, :]
                sel = rt[:, 2, :]

                def g3(k):
                    return shaped(rt[:, k, :], TILES, 16)

                def g4v(k):
                    return shaped(rt[:, k, :], TILES, 4, 4)

                link(tt(g3(2), g3(1), bc(C("rbias"), 1, TILES), ALU.add))
                q = g4v(2)

                def small4(k):
                    return rt[:, k, 0:12].rearrange("p (t g) -> p t g", t=TILES)
                tt(small4(3), q[:, :, :, 0], q[:, :, :, 1], ALU.max)
                tt(small4(4), q[:, :, :, 2], q[:, :, :, 3], ALU.max)
                tt(small4(5), q[:, :, :, 0], q[:, :, :, 1], ALU.min)
                link(tt(small4(6), q[:, :, :, 2], q[:, :, :, 3], ALU.min))
                tt(small4(7), small4(3), small4(4), ALU.max)
                tt(small4(8), small4(3), small4(4), ALU.min)
                link(tt(small4(9), small4(5), small4(6), ALU.max))
                link(tt(small4(8), small4(8), small4(9), ALU.max))
                link(tt(small4(7), small4(7), small4(8), ALU.add))

                def first_max(x, rank, n, w1, w2, w3):
                    m = rt[:, w1, 0:TILES]
                    link(v.tensor_reduce(m, x, X, ALU.max))
                    link(tt(w2, x, bc(m, 2, n), ALU.is_equal))
                    link(tt(w2, w2, bc(C(rank), 1, TILES), ALU.mult))
                    link(v.tensor_reduce(m, w2, X, ALU.max))
                    link(tt(w3, w2, bc(m, 2, n), ALU.is_equal))

                first_max(small4(7), "rank4", 4, 10, small4(8), small4(9))
                inside = g4v(11)
                link(v.tensor_copy(inside, bc(small4(9), 3, 4)))
                link(ts(rt[:, 12, :], rt[:, 11, :], -NEG, NEG, ALU.mult, ALU.add))
                link(tt(rt[:, 2, :], rt[:, 2, :], rt[:, 11, :], ALU.mult))
                link(tt(rt[:, 2, :], rt[:, 2, :], rt[:, 12, :], ALU.add))
                first_max(g3(2), "rank16", 16, 10, g3(13), g3(14))
                link(stt(rt[:, 2, :], rt[:, 14, :], 2 * NEG, rt[:, 2, :], ALU.mult, ALU.add))
                first_max(g3(2), "rank16", 16, 10, g3(13), g3(15))
                tt(rt[:, 16, :], rt[:, 14, :], rt[:, 15, :], ALU.add).then_inc(assigned_ready, 1)
                bank = filled(dve, "pos", l)
                count, nb, ends = rt[:, 17, 0:16], rt[:, 18, 0:16], rt[:, 18, 16:32]
                v.tensor_copy(rt[:, 19, :], bank[:, 0:48])
                v.tensor_copy(count, bank[:, 48:64]).then_inc(read("pos", l), 1)
                taken(dve, "pos", l)
                link(ts(nb, count, 0.0, None, ALU.is_gt))
                for k in range(1, -(-TILES * P // SLOT)):
                    link(stt(nb, count, float(k * SLOT), nb, ALU.is_gt, ALU.add))
                link(v.tensor_tensor_scan(ends, C("ones")[:, 0:16], nb, 0.0, ALU.mult, ALU.add))
                base = rt[:, 17, 16:32]
                tt(base, ends, nb, ALU.subtract)
                link(tt(cmp, bc(ends, 1, BLOCKS), bc(C("block"), 2, EXPERTS), ALU.is_le))
                link(v.tensor_reduce(rt[:, 23, 0:BLOCKS], cmp, X, ALU.add))
                link(ts(rt[:, 23, 0:BLOCKS], rt[:, 23, 0:BLOCKS], float(EXPERTS - 1), None, ALU.min))
                v.tensor_copy(block_expert[:, BLOCKS:BLOCKS + 1], rt[:, 18, 31:32])
                v.tensor_copy(block_expert[:, 0:BLOCKS], rt[:, 23, 0:BLOCKS]).then_inc(blocks_ready, 1)
                link(ts(base, base, float(SLOT), None, ALU.mult))
                link(tt(g3(19), g3(19), bc(base, 1, TILES), ALU.add))
                tt(rt[:, 20, :], rt[:, 14, :], rt[:, 19, :], ALU.mult)
                link(tt(rt[:, 21, :], rt[:, 15, :], rt[:, 19, :], ALU.mult))
                v.tensor_reduce(rt[:, 22, 0:3], g3(20), X, ALU.add)
                link(v.tensor_reduce(rt[:, 22, 3:6], g3(21), X, ALU.add))
                v.tensor_copy(rows[:, :], rt[:, 22, 0:6]).then_inc(rows_ready, 1)
                for k, out in ((0, picks), (1, picks_2)):
                    last = tt(out, bc(C("slot"), 1, TILES), bc(rt[:, 22, 3 * k:3 * k + 3], 2, GATHERED * SLOT),
                              ALU.is_equal)
                link(last)
                tt(picks, picks, picks_2, ALU.add).then_inc(picks_ready, 1)
                tt(rt[:, 20, :], rt[:, 14, :], rt[:, 1, :], ALU.mult)
                link(tt(rt[:, 21, :], rt[:, 15, :], rt[:, 1, :], ALU.mult))
                v.tensor_reduce(w12[:, 0, :], g3(20), X, ALU.add)
                link(v.tensor_reduce(w12[:, 1, :], g3(21), X, ALU.add))
                link(tt(rt[:, 10, 0:3], w12[:, 0, :], w12[:, 1, :], ALU.add))
                link(v.reciprocal(rt[:, 10, 4:7], rt[:, 10, 0:3]))
                link(tt(w12, w12, bc(rt[:, 10, 4:7], 1, 2), ALU.mult))
                fill(l, "rows")

            def moe(l):
                def expert_block(b):
                    taken(dve, "gate", l, b)
                    bank = filled(dve, "up", l, b)
                    tt(hid[b % 2].rearrange("p f n -> p (f n)"), sg, bank[:, 0:2 * SLOT], ALU.mult)\
                        .then_inc(read("up", l, b), 1)
                    bank = filled(dve, "down", l, b, 1)
                    if b >= 2:
                        wait_stored(dve, l, b - 2)
                    v.tensor_copy(ye[b % 2][0:SLOT, 512:D], bank[0:SLOT, :]).then_inc(read("down", l, b, 1), 1)

                used = blocks_used(dve, l)
                for b in range(EXPERTS):
                    expert_block(b)
                for b in range(EXPERTS, BLOCKS):
                    with dve.If(used > b):
                        expert_block(b)
                    with dve.Else():
                        skip_reads(dve, "v", l, b)
                for t in range(TILES):
                    dve.wait_ge(y_gathered[t], 32 * (l + 1))
                    link(ts(y1[:, t, :], y1[:, t, :], w12[:, 0, t:t + 1], None, ALU.mult))
                    stt(y1[:, t, :], y2[:, t, :], w12[:, 1, t:t + 1], y1[:, t, :], ALU.mult, ALU.add)\
                        .then_inc(y_summed, 1)
                for t in range(TILES):
                    g = min(t, 1)
                    for k in range(2):
                        bank = filled(dve, "yt", l, t, k)
                        for i in range(4):
                            n = 4 * k + i
                            out = xT[:, n, COL[t]:COL[t] + P]
                            last = stt(out, bank[:, i * P:(i + 1) * P], mod[:, 40 + n, g:g + 1], out,
                                       ALU.mult, ALU.add)
                        last.then_inc(read("yt", l, t, k), 1)
                taken(dve, "yt", l, TILES - 1, 1)

            v.memset(u[:, :, 0:1], 0.0)
            v.memset(u[:, :, W + 1:W + 2], 0.0)
            v.memset(csum, 0.0)
            v.memset(ye[0], 0.0).then_inc(zeros_set, 1)
            link(v.memset(o[:, :, P:LAT], 0.0))
            v.memset(cols[:, :], 0.0).then_inc(gaps_cleared, 1)
            dve.wait_ge(gaps_cleared, 1)
            dve.wait_ge(consts_loaded, 16)
            dve.wait_ge(x_loaded, 16)
            for l in range(DEPTH):
                fill(l, "start")
                dve.wait_ge(small_loaded, 16 * (l + 1))
                norm(l, 1)
                if l:
                    v.memset(u[:, :, 0:1], 0.0)
                    v.memset(u[:, :, W + 1:W + 2], 0.0)
                for c in range(U_TILES):
                    if c % 2 == 0:
                        bank = filled(dve, "u", l, c)
                        v.tensor_copy(u[:, c, 1:W + 1], bank[:, 0:W]).then_inc(read("u", l, c), 1)
                    if c == UC:
                        ssd_convolution(l)
                    if AFTER_U.get(c) == "qk_squares":
                        qk_norm(l)
                    elif AFTER_U.get(c) == "rotation":
                        rotation(l)
                        token_shift(l)
                attention(l)
                rwkv_inputs(l)
                ssd_steps(l)
                fill(l, "batches")
                for step, b in RW_ORDER:
                    rwkv_step(l, step, b)
                rwkv_norm(l)
                fill(l, "ssd")
                ssd(l)
                for n in range(KT):
                    bank = filled(dve, "out", l, n)
                    add_gated(bank, n, 16).then_inc(read("out", l, n), 1)
                taken(dve, "out", l, KT - 1)
                norm(l, 2)
                routing(l)
                moe(l)


def constants():
    import numpy as np
    i = np.arange(P)
    row, col = i[:, None], i[None, :]
    same = lambda n: (row // n == col // n).astype(np.float32)
    rot = np.zeros((P, P), np.float32)
    for m in range(P):
        if m % 32 < 16:
            rot[m + 16, m] = -1.0
        else:
            rot[m - 16, m] = 1.0
    strict = [(row < col), (row > col)]
    incl = [(row <= col), (row >= col)]
    c = {
        "head": same(64), "ident": np.eye(P), "rot": rot,
        "inv": np.concatenate([same(16)] + [same(2 * n) - same(n) for n in (16, 32, 64)], 1),
    }
    for d in range(2):
        c[f"rw{d}"] = np.concatenate([strict[d], incl[d]] * 2, 1)
        c[f"nd{d}"] = strict[1 - d] * same(16)
        c[f"ssd{d}"] = np.where(incl[d], 0.0, NEG)
    tok = np.arange(2 * P)
    pos = np.stack([tok // 64, tok % 64]).astype(np.float32)
    freq = np.float32(10000.0) ** (-np.arange(16, dtype=np.float32) / np.float32(16))
    ang = np.stack([pos[(f % 64) // 32] * freq[f % 16] for f in range(P)]).astype(np.float32)
    c["cos"], c["sin"] = np.cos(ang), np.sin(ang)
    restart = np.ones((P, W), np.float32)
    restart[:, COL] = 0.0
    c["restart"] = restart
    c["rank16"] = np.broadcast_to(np.arange(16, 0, -1), (P, 16))
    c["eps"], c["eps_kk"], c["eps_gn"] = EPS, 1e-12, GN_EPS
    c["ones"] = np.ones((P, P))
    c["block"] = np.broadcast_to(np.arange(BLOCKS), (P, BLOCKS))
    c["slot"] = np.broadcast_to(np.arange(GATHERED * SLOT), (P, GATHERED * SLOT))
    c["rank4"] = np.broadcast_to(np.arange(4, 0, -1), (P, 4))
    return c


def tokens(prompt, sample):
    import numpy as np
    out = np.zeros((P, KT, W), np.float32)
    out[:, :, 0:P] = prompt.T.reshape(KT, P, P).transpose(1, 0, 2)
    out[:, :, LAT:] = sample.T.reshape(KT, P, 2 * P).transpose(1, 0, 2)
    return out.reshape(P, KT * W)


def by_feature(v):
    return v.reshape(-1, P).T


def kernel(**inputs):
    import numpy as np
    import concourse.bacc as bacc
    from concourse.bass_utils import run_bass_kernel_spmd

    x = {k: np.asarray(v) for k, v in inputs.items()}

    def tiles_of(w):
        k, n = w.shape
        return w.reshape(k // P, P, n // P, P).transpose(2, 1, 0, 3).reshape(n // P, P, k)

    q_cols = np.concatenate([np.r_[64 * m:64 * m + 64, 64 * (m + 4):64 * (m + 4) + 64] for m in range(4)])
    in_cols = np.concatenate([q_cols, np.arange(512, 2432)])
    out_rows = np.concatenate([q_cols, np.arange(512, 1024)])
    weights = np.zeros((DEPTH * LAYER_ITEMS, P, ITEM), np.float32)
    n = 0
    for l in range(DEPTH):
        def put(t):
            nonlocal n
            t = t.reshape(-1, ITEM // t.shape[2], P, t.shape[2]).transpose(0, 2, 1, 3).reshape(-1, P, ITEM)
            weights[n:n + len(t)] = t
            n += len(t)
        w = x["w_mod"][l].reshape(2, 4, P, MOD_CHUNKS, 512).transpose(3, 0, 2, 1, 4)
        weights[n:n + MOD_ITEMS] = w.reshape(MOD_ITEMS, P, ITEM)
        n += MOD_ITEMS
        dt = np.zeros((KT, P, DT_ROWS), np.float32)
        for d in range(2):
            dt[:, :, 32 * d:32 * d + 4] = x["w_in"][l][:, 2432:2436].reshape(KT, P, 4)
        t = np.zeros((20, P, D), np.float32)
        t[:19] = tiles_of(x["w_in"][l][:, in_cols])
        t[19, :, :KT * DT_ROWS] = dt.transpose(1, 0, 2).reshape(P, -1)
        put(t)
        put(tiles_of(x["w_out"][l][out_rows]))
        for e in range(EXPERTS):
            put(tiles_of(x["exp_gate"][l, e]))
            put(tiles_of(x["exp_up"][l, e]))
            weights[n] = x["exp_down"][l, e].reshape(2, P, D).transpose(1, 0, 2).reshape(P, ITEM)
            n += 1
    assert n == len(weights)

    small = np.zeros((DEPTH, P, LAYER_N), np.float32)
    for l in range(DEPTH):
        def s(name, v, rows=slice(0, P)):
            lo, hi = LAYER_COLS[name]
            small[l][rows, lo:hi] = v
        s("qw", np.tile(x["q_norm_w"][l], 2)[:, None])
        s("kw", np.tile(x["k_norm_w"][l], 2)[:, None])
        s("sink", np.broadcast_to(x["attn_sink"][l], (P, 8)))
        s("mu0", by_feature(x["rw_mu"][l, 0]))
        s("mu1", by_feature(x["rw_mu"][l, 1]))
        s("w0", by_feature(x["rw_w0"][l].reshape(-1)))
        s("a0", by_feature(x["rw_a0"][l].reshape(-1)))
        s("kk", by_feature(x["rw_k_k"][l]))
        s("ka", by_feature(x["rw_k_a"][l]))
        s("rk", by_feature(x["rw_r_k"][l].reshape(-1)))
        s("lnw", by_feature(x["rw_ln_w"][l]))
        s("lnb", by_feature(x["rw_ln_b"][l]))
        s("cw", by_feature(x["ssd_conv_w"][l].reshape(-1)))
        s("cb", by_feature(x["ssd_conv_b"][l]))
        for d in range(2):
            r = slice(32 * d, 32 * d + 4)
            s("dtb", x["ssd_dt_bias"][l, d][:, None], r)
            s("alog", x["ssd_a_log"][l, d][:, None], r)
        s("dskip", by_feature(np.repeat(x["ssd_d"][l], 64)))
        s("nw", by_feature(x["ssd_norm_w"][l]))
        s("lora", x["rw_w_up"][l].transpose(1, 0, 2).reshape(32, 512), slice(0, 32))
        s("lora", x["rw_a_up"][l].transpose(1, 0, 2).reshape(32, 512), slice(32, 64))
        lo = LAYER_COLS["lora"][0]
        small[l][64:, lo:lo + 256] = x["rw_g_up"][l]
        s("kc", x["cache_k"][0, l].transpose(1, 2, 0).reshape(P, P))
        s("vc", x["cache_v"][0, l].reshape(P, P))
        s("srw", x["state_rwkv"][0, l].reshape(2, 2, 2, 64, 64).transpose(2, 4, 0, 1, 3).reshape(P, 256))
        s("sssd", x["state_ssd"][0, l].reshape(2, 2, 2, 64, 64).transpose(1, 4, 0, 2, 3).reshape(P, 256))

    consts = np.zeros((P, CONST_N), np.float32)
    table = constants()
    table["router"] = x["router_w"].reshape(KT, P, 16).transpose(1, 0, 2).reshape(P, P)
    table["rbias"] = np.broadcast_to(x["router_bias"], (P, 16))
    for l in range(DEPTH):
        table[f"bmod{l}"] = by_feature(x["b_mod"][l])
        table[f"n1_{l}"] = by_feature(x["norm1_w"][l])
        table[f"n2_{l}"] = by_feature(x["norm2_w"][l])
    for name, (lo, hi) in CONST_COLS.items():
        consts[:, lo:hi] = table[name]
    cond = np.stack([by_feature(x["c_ctx"]), by_feature(x["c"][0])], 2).reshape(P, 16)

    nc = bacc.Bacc("TRN2", target_bir_lowering=False, num_devices=1)
    arrays = {"weights": weights, "small": small, "consts": consts, "cond": np.ascontiguousarray(cond),
              "x": tokens(x["x_prompt"][0], x["x_sample"][0])}
    shapes = {"y": (P, KT * W), "new_k": (DEPTH, P, P), "new_v": (DEPTH, P, P),
              "new_rw": (DEPTH, P, 256), "new_ssd": (DEPTH, P, 256)}
    f32 = mybir.dt.float32
    a = {k: nc.dram_tensor(k, v.shape, f32, kind="ExternalInput").ap() for k, v in arrays.items()}
    a.update({k: nc.dram_tensor(k, v, f32, kind="ExternalOutput").ap() for k, v in shapes.items()})
    program(nc, a)
    r = run_bass_kernel_spmd(nc, [arrays], core_ids=[0]).results[0]

    y = r["y"].reshape(P, KT, W).transpose(2, 1, 0).reshape(W, D)
    cache = lambda v: np.ascontiguousarray(v.transpose(0, 2, 1).reshape(1, DEPTH, P, 2, 64))
    rw = r["new_rw"].reshape(DEPTH, 2, 64, 2, 2, 64).transpose(0, 3, 4, 1, 5, 2).reshape(1, DEPTH, 2, 4, 64, 64)
    sd = r["new_ssd"].reshape(DEPTH, 2, 64, 2, 2, 64).transpose(0, 3, 1, 4, 5, 2).reshape(1, DEPTH, 2, 4, 64, 64)
    return (np.ascontiguousarray(y[None, 0:P]), np.ascontiguousarray(y[None, LAT:]), cache(r["new_k"]),
            cache(r["new_v"]), np.ascontiguousarray(rw), np.ascontiguousarray(sd))
```
